# Optimizing a Trainium2 kernel written in Bass

```python
import jax, jax.numpy as jnp
from jax import lax
import numpy as np

D_MODEL = 2048
BATCH = 1
SEQ = 256
DEPTH = 1

EPS = 1e-6
Q_BLOCK = 128
NEG = -1e30

MLA_HEADS = 8
MLA_Q_RANK = 512
MLA_KV_RANK = 256
MLA_NOPE = 128
MLA_ROPE = 64
MLA_V = 128
ROPE_THETA = 10000.0

NSA_HEADS = 16
NSA_KV_GROUPS = 2
NSA_HPG = NSA_HEADS // NSA_KV_GROUPS
NSA_DK = 64
NSA_DV = 64
CMP_LEN = 32
CMP_STRIDE = 16
CMP_HIDDEN = 256
SEL_LEN = 64
SEL_TOPK = 16
WINDOW = 512
FORCE_BONUS = 1e4
NSA_KV_WIDTH = NSA_KV_GROUPS * (NSA_DK + NSA_DV)

MIX_WIDTH = MLA_HEADS * MLA_V + NSA_HEADS * NSA_DV
MLP_HIDDEN = 4 * D_MODEL

IN_SIZES = (MLA_Q_RANK, MLA_KV_RANK, MLA_ROPE, NSA_HEADS * NSA_DK,
            NSA_KV_WIDTH, NSA_KV_WIDTH, NSA_KV_WIDTH, 3 * NSA_HEADS)
IN_WIDTH = sum(IN_SIZES)

kernel_name = "hybrid_mla_nsa_block"

def rmsnorm(x, w):
    xf = x.astype(jnp.float32)
    y = xf * lax.rsqrt(jnp.mean(xf * xf, axis=-1, keepdims=True) + EPS)
    return (y * w.astype(jnp.float32)).astype(x.dtype)

def _split_cols(t, sizes):
    offs = np.cumsum(sizes)[:-1].tolist()
    return jnp.split(t, offs, axis=-1)

def rope_cos_sin(positions, dim):
    inv = 1.0 / (ROPE_THETA ** (jnp.arange(0, dim, 2, dtype=jnp.float32) / dim))
    ang = positions.astype(jnp.float32)[..., None] * inv
    return jnp.cos(ang), jnp.sin(ang)

def apply_rope(x, cos, sin):
    xf = x.astype(jnp.float32)
    half = xf.shape[-1] // 2
    x1, x2 = xf[..., :half], xf[..., half:]
    return jnp.concatenate([x1 * cos - x2 * sin, x2 * cos + x1 * sin], axis=-1).astype(x.dtype)

def alibi_slopes(n):
    start = 2.0 ** (-8.0 / n)
    return start ** jnp.arange(1, n + 1, dtype=jnp.float32)

def masked_softmax(s, mask):
    p = jax.nn.softmax(jnp.where(mask, s, NEG), axis=-1)
    return jnp.where(mask, p, 0.0)

def mla_attention(c_q, c_kv, k_rope, positions, q_norm_w, w_uq, kv_norm_w, w_ukv):
    B, T, _ = c_q.shape
    q = (rmsnorm(c_q, q_norm_w) @ w_uq).reshape(B, T, MLA_HEADS, MLA_NOPE + MLA_ROPE)
    q_nope, q_pe = q[..., :MLA_NOPE], q[..., MLA_NOPE:]
    kv = (rmsnorm(c_kv, kv_norm_w) @ w_ukv).reshape(B, T, MLA_HEADS, MLA_NOPE + MLA_V)
    k_nope, v = kv[..., :MLA_NOPE], kv[..., MLA_NOPE:]
    cos, sin = rope_cos_sin(positions, MLA_ROPE)
    q_pe = apply_rope(q_pe, cos[:, :, None], sin[:, :, None])
    k_pe = apply_rope(k_rope, cos, sin)
    scale = (MLA_NOPE + MLA_ROPE) ** -0.5
    nb = T // Q_BLOCK
    qn_b = jnp.moveaxis(q_nope.reshape(B, nb, Q_BLOCK, MLA_HEADS, MLA_NOPE), 1, 0)
    qp_b = jnp.moveaxis(q_pe.reshape(B, nb, Q_BLOCK, MLA_HEADS, MLA_ROPE), 1, 0)
    kpos = jnp.arange(T)

    def block(args):
        i, qn, qp = args
        s = (jnp.einsum('bqhd,bkhd->bhqk', qn, k_nope)
             + jnp.einsum('bqhd,bkd->bhqk', qp, k_pe)).astype(jnp.float32) * scale
        qpos = i * Q_BLOCK + jnp.arange(Q_BLOCK)
        p = masked_softmax(s, kpos[None, :] <= qpos[:, None])
        return jnp.einsum('bhqk,bkhd->bqhd', p.astype(v.dtype), v)

    out = lax.map(block, (jnp.arange(nb), qn_b, qp_b))
    return jnp.moveaxis(out, 0, 1).reshape(B, T, MLA_HEADS * MLA_V)

def nsa_attention(q, kv_cmp, kv_slc, kv_win, gate_logits,
                  cmp_pos_k, cmp_pos_v, cmp_w1_k, cmp_w2_k, cmp_w1_v, cmp_w2_v):
    B, T, _ = q.shape
    G, HG = NSA_KV_GROUPS, NSA_HPG
    q = q.reshape(B, T, G, HG, NSA_DK)
    gates = jax.nn.sigmoid(gate_logits.astype(jnp.float32)).reshape(B, T, G, HG, 3).astype(q.dtype)

    def kv_split(kv):
        kv = kv.reshape(B, T, G, NSA_DK + NSA_DV)
        return kv[..., :NSA_DK], kv[..., NSA_DK:]

    k_c, v_c = kv_split(kv_cmp)
    k_s, v_s = kv_split(kv_slc)
    k_w, v_w = kv_split(kv_win)

    n_cmp = (T - CMP_LEN) // CMP_STRIDE + 1
    cmp_start = jnp.arange(n_cmp) * CMP_STRIDE
    cmp_end = cmp_start + CMP_LEN - 1
    tok_idx = cmp_start[:, None] + jnp.arange(CMP_LEN)[None, :]

    def compress(t, pos, w1, w2):
        blk = t[:, tok_idx] + pos[None, None, :, None, :]
        blk = blk.transpose(0, 1, 3, 2, 4).reshape(B, n_cmp, G, CMP_LEN * t.shape[-1])
        return jax.nn.gelu(blk @ w1) @ w2

    k_cmp = compress(k_c, cmp_pos_k, cmp_w1_k, cmp_w2_k)
    v_cmp = compress(v_c, cmp_pos_v, cmp_w1_v, cmp_w2_v)

    n_sel = T // SEL_LEN
    top_k = min(SEL_TOPK, n_sel)
    sel_start = jnp.arange(n_sel) * SEL_LEN
    overlap = ((cmp_start[:, None] <= sel_start[None, :] + SEL_LEN - 1)
               & (cmp_end[:, None] >= sel_start[None, :])).astype(jnp.float32)
    slopes = alibi_slopes(NSA_HEADS).reshape(G, HG)[None, :, :, None, None]
    k_s_g = k_s.transpose(0, 2, 1, 3)
    v_s_g = v_s.transpose(0, 2, 1, 3)
    k_w_pad = jnp.pad(k_w, ((0, 0), (WINDOW, 0), (0, 0), (0, 0)))
    v_w_pad = jnp.pad(v_w, ((0, 0), (WINDOW, 0), (0, 0), (0, 0)))
    scale = NSA_DK ** -0.5
    gather = jax.vmap(jax.vmap(lambda src, idx: src[idx]))
    blk_ids = jnp.arange(n_sel)

    nb = T // Q_BLOCK
    q_b = jnp.moveaxis(q.reshape(B, nb, Q_BLOCK, G, HG, NSA_DK), 1, 0)
    g_b = jnp.moveaxis(gates.reshape(B, nb, Q_BLOCK, G, HG, 3), 1, 0)

    def block(args):
        i, qb, gb = args
        qpos = i * Q_BLOCK + jnp.arange(Q_BLOCK)
        s = jnp.einsum('bqghd,bngd->bghqn', qb, k_cmp).astype(jnp.float32) * scale
        dist = qpos[:, None] - cmp_end[None, :]
        s = s - slopes * dist.astype(jnp.float32)
        p_c = masked_softmax(s, dist >= 0)
        o_c = jnp.einsum('bghqn,bngd->bqghd', p_c.astype(v_cmp.dtype), v_cmp)
        imp = jnp.einsum('bghqn,ns->bgqs', p_c, overlap)
        cur = qpos // SEL_LEN
        forced = ((blk_ids[None, :] == 0) | (blk_ids[None, :] == cur[:, None])
                  | (blk_ids[None, :] == cur[:, None] - 1)).astype(jnp.float32)
        score = jnp.where(blk_ids[None, :] <= cur[:, None], imp + FORCE_BONUS * forced, NEG)
        top_val, top_idx = lax.top_k(score, top_k)
        tok = (top_idx[..., None] * SEL_LEN + jnp.arange(SEL_LEN)).reshape(B, G, Q_BLOCK, top_k * SEL_LEN)
        blk_ok = jnp.repeat(top_val > NEG * 0.5, SEL_LEN, axis=-1)
        k_sel = gather(k_s_g, tok)
        v_sel = gather(v_s_g, tok)
        s = jnp.einsum('bqghd,bgqmd->bghqm', qb, k_sel).astype(jnp.float32) * scale
        dist = qpos[None, None, :, None] - tok
        s = s - slopes * dist[:, :, None].astype(jnp.float32)
        p_s = masked_softmax(s, ((dist >= 0) & blk_ok)[:, :, None])
        o_s = jnp.einsum('bghqm,bgqmd->bqghd', p_s.astype(v_sel.dtype), v_sel)
        kw = lax.dynamic_slice_in_dim(k_w_pad, i * Q_BLOCK, WINDOW + Q_BLOCK, axis=1)
        vw = lax.dynamic_slice_in_dim(v_w_pad, i * Q_BLOCK, WINDOW + Q_BLOCK, axis=1)
        kpos = i * Q_BLOCK - WINDOW + jnp.arange(WINDOW + Q_BLOCK)
        dist = qpos[:, None] - kpos[None, :]
        mask = (dist >= 0) & (dist < WINDOW) & (kpos[None, :] >= 0)
        s = jnp.einsum('bqghd,bkgd->bghqk', qb, kw).astype(jnp.float32) * scale
        s = s - slopes * dist.astype(jnp.float32)
        p_w = masked_softmax(s, mask)
        o_w = jnp.einsum('bghqk,bkgd->bqghd', p_w.astype(vw.dtype), vw)
        return gb[..., 0:1] * o_c + gb[..., 1:2] * o_s + gb[..., 2:3] * o_w

    out = lax.map(block, (jnp.arange(nb), q_b, g_b))
    return jnp.moveaxis(out, 0, 1).reshape(B, T, NSA_HEADS * NSA_DV)

def setup_inputs(seed: int = 0) -> dict:
    key = jax.random.key(seed)
    ks = jax.random.split(key, 24)
    f32 = jnp.float32

    def w(k, shape, fan_in):
        return jax.random.normal(k, shape, f32) * (fan_in ** -0.5)

    def gain(k, shape):
        return 1.0 + 0.02 * jax.random.normal(k, shape, f32)

    L = DEPTH
    return {
        "x": jax.random.normal(ks[0], (BATCH, SEQ, D_MODEL), f32),
        "positions": jnp.broadcast_to(jnp.arange(SEQ, dtype=jnp.int32), (BATCH, SEQ)),
        "attn_norm_w": gain(ks[1], (L, D_MODEL)),
        "w_in": w(ks[2], (L, D_MODEL, IN_WIDTH), D_MODEL),
        "mla_q_norm_w": gain(ks[3], (L, MLA_Q_RANK)),
        "mla_w_uq": w(ks[4], (L, MLA_Q_RANK, MLA_HEADS * (MLA_NOPE + MLA_ROPE)), MLA_Q_RANK),
        "mla_kv_norm_w": gain(ks[5], (L, MLA_KV_RANK)),
        "mla_w_ukv": w(ks[6], (L, MLA_KV_RANK, MLA_HEADS * (MLA_NOPE + MLA_V)), MLA_KV_RANK),
        "cmp_pos_k": 0.1 * jax.random.normal(ks[7], (L, CMP_LEN, NSA_DK), f32),
        "cmp_pos_v": 0.1 * jax.random.normal(ks[8], (L, CMP_LEN, NSA_DV), f32),
        "cmp_w1_k": w(ks[9], (L, CMP_LEN * NSA_DK, CMP_HIDDEN), CMP_LEN * NSA_DK),
        "cmp_w2_k": w(ks[10], (L, CMP_HIDDEN, NSA_DK), CMP_HIDDEN),
        "cmp_w1_v": w(ks[11], (L, CMP_LEN * NSA_DV, CMP_HIDDEN), CMP_LEN * NSA_DV),
        "cmp_w2_v": w(ks[12], (L, CMP_HIDDEN, NSA_DV), CMP_HIDDEN),
        "mla_out_norm_w": gain(ks[13], (L, MLA_HEADS * MLA_V)),
        "nsa_out_norm_w": gain(ks[14], (L, NSA_HEADS * NSA_DV)),
        "w_o": w(ks[15], (L, MIX_WIDTH, D_MODEL), MIX_WIDTH),
        "mlp_norm_w": gain(ks[16], (L, D_MODEL)),
        "w_up": w(ks[17], (L, D_MODEL, MLP_HIDDEN), D_MODEL),
        "w_down": w(ks[18], (L, MLP_HIDDEN, D_MODEL), MLP_HIDDEN),
        "final_norm_w": gain(ks[19], (D_MODEL,)),
    }

def reference(x, positions, attn_norm_w, w_in, mla_q_norm_w, mla_w_uq, mla_kv_norm_w, mla_w_ukv,
              cmp_pos_k, cmp_pos_v, cmp_w1_k, cmp_w2_k, cmp_w1_v, cmp_w2_v,
              mla_out_norm_w, nsa_out_norm_w, w_o, mlp_norm_w, w_up, w_down, final_norm_w):
    h = x
    for l in range(DEPTH):
        n = rmsnorm(h, attn_norm_w[l])
        proj = n @ w_in[l]
        c_q, c_kv, k_rope, q_nsa, kv_cmp, kv_slc, kv_win, gate_logits = _split_cols(proj, IN_SIZES)
        y_mla = mla_attention(c_q, c_kv, k_rope, positions, mla_q_norm_w[l], mla_w_uq[l],
                              mla_kv_norm_w[l], mla_w_ukv[l])
        y_nsa = nsa_attention(q_nsa, kv_cmp, kv_slc, kv_win, gate_logits,
                              cmp_pos_k[l], cmp_pos_v[l], cmp_w1_k[l], cmp_w2_k[l],
                              cmp_w1_v[l], cmp_w2_v[l])
        y = jnp.concatenate([rmsnorm(y_mla, mla_out_norm_w[l]),
                             rmsnorm(y_nsa, nsa_out_norm_w[l])], axis=-1)
        h = h + y @ w_o[l]
        n = rmsnorm(h, mlp_norm_w[l])
        h = h + jnp.square(jax.nn.relu(n @ w_up[l])) @ w_down[l]
    return rmsnorm(h, final_norm_w)


_drawn_inputs = setup_inputs


def setup_inputs(seed=0):
    import zlib

    import numpy as np

    out = dict(_drawn_inputs(seed))
    spreads = {}
    factors = {'mla_q_norm_w': 5.986,
     'mla_kv_norm_w': 3.747,
     'cmp_pos_k': 8.0,
     'mla_out_norm_w': 5.162,
     'nsa_out_norm_w': 5.519,
     'mlp_norm_w': 3.818,
     'final_norm_w': 2.929}
    for name, (base, spread) in spreads.items():
        noise = np.random.default_rng([zlib.crc32(name.encode()), seed]).standard_normal(out[name].shape)
        drawn = base * np.exp(spread * noise) if base else spread * noise
        out[name] = __import__('jax').numpy.asarray(drawn.astype(out[name].dtype))
    for name, factor in factors.items():
        out[name] = (out[name] * factor).astype(out[name].dtype)
    return out
```

```python
from contextlib import ExitStack

import numpy as np

import concourse.bass as bass
from concourse import mybir

F32 = mybir.dt.float32
F32R = mybir.dt.float32r
I32 = mybir.dt.int32
ALU = mybir.AluOpType
ACT = mybir.ActivationFunctionType
AX = mybir.AxisListType

P = 128
T, D = 256, 2048
TT = T // P
KT = D // P
EPS = 1e-6
QR, KVR, NOPE, ROPE, MH, MV = 512, 256, 128, 64, 8, 128
NH, NG, DK = 16, 2, 64
CMP_LEN, CMP_STRIDE, CMP_HID = 32, 16, 256
NC = (T - CMP_LEN) // CMP_STRIDE + 1
WINDOW, SEL_LEN, SEL_TOPK = 512, 64, 16
assert T // SEL_LEN <= SEL_TOPK and WINDOW >= T
HID = 4 * D
CW = 832
BW = 816
OFF_Q = CW
OFF_B = CW + NH * DK
MLA_SCALE = float(NOPE + ROPE) ** -0.5
NSA_SCALE = float(DK) ** -0.5
HALF = ROPE // 2
SLOPE = [float(np.float32(2.0 ** (-8.0 / NH)) ** (h + 1)) for h in range(NH)]
BIG = 1e30
SEEN = 3 * P
TWO_PI = 2.0 * np.pi
C1 = 6.28125
C2 = float(np.float32(int((TWO_PI - C1) * 2 ** 20) / 2 ** 20))
C3 = float(TWO_PI - C1 - C2)
PI_IN = float(np.nextafter(np.float32(np.pi), np.float32(0)))
MAGIC = float(1.5 * 2 ** 23)

PRM = dict(attn=0, mlp=16, c=32, y=38, posk=54, posv=70)
NPRM = 86

C_IN, B_IN, UQ_PE, UQ_NOPE, UKV_K, UKV_V, A_IN = 0, 8, 16, 17, 19, 20, 21
CMP, WO_M, WO_N, MLP0 = 29, 33, 41, 49
RAW, SPLIT = 4, 2
G = 8
GC = 16


def raw_slot(c):
    return (c + 3) % RAW


def split_slot(c):
    return (c + 1) % SPLIT


STEPS = [("mla", h, h, 0) for h in range(MH)]
for _u in range(MH, 16):
    _a = 2 * (_u - MH)
    STEPS += [("slc", _u, _a, 0), ("win", _u, _a, 1), ("slc", _u, _a + 1, 0), ("win", _u, _a + 1, 1), ("cmp", _u, _a, 2)]
NMLA = MH
LASTSTEP = {s[1]: i for i, s in enumerate(STEPS)}
SOFT = {i: n for n, i in enumerate([i for i, s in enumerate(STEPS) if s[0] != "cmp"])}


MLA_PLAN = []
for _i in range(8):
    MLA_PLAN += [("w", A_IN + _i), ("hi", A_IN + _i + 1), ("s", _i), ("lo", A_IN + _i + 1)]
MLA_PLAN += [("s", 8), ("s", 9), ("s", 10)]

NSA_PLAN = []
_c, _s = CMP, NMLA
for _n in range(4):
    NSA_PLAN += [("w", _c), ("hi", _c + 1)] + ([("s", _s)] if _n != 1 else []) + [("lo", _c + 1)]
    _c += 1
    _s += _n != 1
NSA_PLAN += [("k", "gelu"), ("s", _s), ("k", "turn"), ("s", _s + 1), ("k", "project"), ("k", "scores"), ("s", _s + 2), ("k", "soft")]
_s += 3
while _s < len(STEPS) + 3:
    if _c < WO_N:
        NSA_PLAN += [("w", _c), ("hi", _c + 1)]
    for _j in range(4):
        if _s < len(STEPS) + 3:
            NSA_PLAN += [("s", _s)]
            _s += 1
        if _j == 0 and _c < WO_N:
            NSA_PLAN += [("lo", _c + 1)]
    _c += _c < WO_N
while _c < WO_N:
    NSA_PLAN += [("w", _c), ("hi", _c + 1), ("lo", _c + 1)]
    _c += 1


TURNS = ((0, 1, 2), (3, 4, 5), (6, 7))


def build(nc, a, out):
    with ExitStack() as ctx:
        def seq(base, *specs):
            made = []
            for name, shape, dt in specs:
                made.append(nc.alloc_sbuf_tensor_at(name, shape, dt, offset=base))
                base += (4 * int(np.prod(shape[1:])) + 31) // 32 * 32
            return (*made, base)

        X_AT = (nc.sbuf_base + 31) // 32 * 32
        xT, Y_AT = seq(X_AT, ("xT", [P, 2, KT, T], F32R))
        yT, W_AT = seq(Y_AT, ("yT", [P, 16, 2, T], F32R))
        w_hi, w_lo, raw, F_AT = seq(W_AT, ("w_hi", [P, SPLIT, 2048], F32R), ("w_lo", [P, SPLIT, 2048], F32R),
                                    ("raw", [P, RAW, 2048], F32))
        YN_AT = Y_AT + 4 * 8 * 2 * T
        cT, _ = seq(YN_AT, ("cT", [P, 2, 6, T], F32R))
        blk, kcT, e = seq(YN_AT, ("blk", [P, 2, 2, 16, 2 * NC], F32R), ("kcT", [P, 4, T], F32))
        assert e <= W_AT
        sink, kd, e = seq(Y_AT, ("sink", [P, D], F32), ("kd", [P, 8, TT, 2, DK], F32))
        assert e <= YN_AT
        hidT, _ = seq(Y_AT, ("hidT", [P, 2, 8, T], F32R))
        q_sb, qT, bias_h, cbias, pc, h1a, h1b, h1c, h1T, kcmpT, vcmp, e = seq(
            X_AT, ("q_sb", [P, TT, NH * DK], F32), ("qT", [P, 8, T], F32), ("bias_h", [P, 2, SEEN], F32),
            ("cbias", [P, NH, TT, NC], F32), ("pc", [P, NH, TT, NC], F32), ("h1a", [2 * NC, 2, CMP_HID], F32),
            ("h1b", [2 * NC, 2, CMP_HID], F32), ("h1c", [2 * NC, 2, CMP_HID], F32), ("h1T", [P, 4, 2 * NC], F32),
            ("kcmpT", [P, 2 * NC], F32), ("vcmp", [NC, NG, DK], F32))
        assert e <= Y_AT
        ident, wcols, ones, r1, r1q, rc, rm, rn, ssq, root_w, A_AT = seq(
            F_AT, ("ident", [P, P], F32), ("wcols", [P, NPRM], F32), ("ones", [P, 1], F32), ("r1", [P, TT], F32),
            ("r1q", [P, TT], F32), ("rc", [P, 4], F32), ("rm", [P, TT], F32), ("rn", [P, TT], F32),
            ("ssq", [P, 16], F32), ("root_w", [P, 4], F32))
        (posf, posi, den, scl, nmax, cden, cmx, cgate, valid, invf, gates, dist, mask, cdist, cdi, kv_sb, kT, prob, probT,
         sq, sqacc, w2k, w2v, prm, M_AT) = seq(
            A_AT, ("posf", [P, TT], F32), ("posi", [P, TT], I32), ("den", [P, 40, 2], F32), ("scl", [P, 40, 2], F32),
            ("nmax", [P, 40, 2], F32), ("cden", [P, NH * TT], F32), ("cmx", [P, NH * TT], F32),
            ("cgate", [P, NH, TT], F32), ("valid", [P, TT], F32), ("invf", [P, HALF], F32),
            ("gates", [P, TT, 3 * NH], F32), ("dist", [P, SEEN], F32), ("mask", [P, SEEN], F32),
            ("cdist", [P, TT, NC], F32), ("cdi", [P, TT, NC], I32), ("kv_sb", [P, TT, BW], F32), ("kT", [P, 4, T], F32),
            ("prob", [P, 3, SEEN], F32), ("probT", [P, 2, 512], F32), ("sq", [P, 2, T], F32),
            ("sqacc", [P, 2, T], F32), ("w2k", [P, 2, 2, DK], F32), ("w2v", [P, 2, DK], F32), ("prm", [NPRM, P], F32))
        cs, angs, angk, L_AT = seq(M_AT, ("cs", [P, 2, TT * HALF], F32), ("angs", [P, 2, TT * HALF], F32),
                                   ("angk", [P, 2, TT * HALF], F32))
        c_sb, qpr, v_sb, qnT, knT, qpT, kpT, kpe, rtmp, e = seq(
            L_AT, ("c_sb", [P, TT, CW], F32), ("qpr", [P, TT, MH * ROPE], F32), ("v_sb", [P, TT, MH * MV], F32),
            ("qnT", [P, MH, T], F32), ("knT", [P, MH, T], F32), ("qpT", [P, 4, T], F32), ("kpT", [P, T], F32),
            ("kpe", [P, TT, 2 * ROPE], F32), ("rtmp", [P, 2, MH * HALF], F32))
        blkf, e = seq(e, ("blkf", [P, 2, 16, 2 * NC], F32))
        assert e <= nc.sbuf_usable_end, (e, nc.sbuf_usable_end)
        di, _ = seq(L_AT, ("di", [P, SEEN], I32))
        qpe, _ = seq(L_AT, ("qpe", [P, TT, MH * ROPE], F32))
        x_sb, _ = seq(L_AT + 4 * 1664, ("x_sb", [P, TT, D], F32))
        h_sb, H_END = seq(L_AT, ("h_sb", [P, TT, D], F32))
        sink2, e = seq(H_END, ("sink2", [P, D], F32))
        assert e <= nc.sbuf_usable_end
        acc, hid, e = seq(A_AT, ("acc", [P, TT, D], F32), ("hid", [P, TT, 1024], F32))
        assert e <= M_AT, (e, M_AT)
        fw, _ = seq(X_AT, ("fw", [P, D], F32))

        ps = ctx.enter_context(nc.psum_tensor("ps", [P, 8, 512], F32))
        flat = ps[:, :, :].rearrange("p b n -> p (b n)")

        def bank(b, n=512, p0=0, p1=P):
            return ps[p0:p1, b, 0:n]

        def pairs(ap):
            return ap.rearrange("p (k t) -> p k t", k=2)

        def sems(*names):
            return [ctx.enter_context(nc.semaphore(n)) for n in names]

        x_in = sems("x_in0", "x_in1")
        raw_in = sems(*[f"raw_in{n}" for n in range(RAW)])
        prm_in, cst_in, w2_in, h_in, fw_in, stored = sems("prm_in", "cst_in", "w2_in", "h_in", "fw_in", "stored")
        hi_done, lo_done, w_used = sems("hi_done", "lo_done", "w_used")
        first_done, = sems("first_done")
        act_free, dve_free = sems("act_free", "dve_free")
        pool_c, dve_c = sems("pool_c", "dve_c")
        consts, tables, prm_t, wcols_ok = sems("consts", "tables", "prm_t", "wcols_ok")
        xt_t, xt_hi, xt_lo, ct_t, ct_hi, ct_lo = sems("xt_t", "xt_hi", "xt_lo", "ct_t", "ct_hi", "ct_lo")
        ssq_ok, rs_ok, ang_ok, sin_ok = sems("ssq_ok", "rs_ok", "ang_ok", "sin_ok")
        c_norm, kpe_ok, qpe_out, qpr_ok, qn_out, kn_out, v_out = sems(
            "c_norm", "kpe_ok", "qpe_out", "qpr_ok", "qn_out", "kn_out", "v_out")
        kv_t, kv_out, qp_t, qp_out, blk_f, blk_hi, blk_ok = sems(
            "kv_t", "kv_out", "qp_t", "qp_out", "blk_f", "blk_hi", "blk_ok")
        kd_ok, gexp, gate_ok, q_t, q_out = sems("kd_ok", "gexp", "gate_ok", "q_t", "q_out")
        g_sq, g_in, g_th, g_ok, g_t, g_turned, k_t, k_ok = sems(
            "g_sq", "g_in", "g_th", "g_ok", "g_t", "g_turned", "k_t", "k_ok")
        cs_t, cs_sub, cs_exp, pc_ok, cb_ok = sems("cs_t", "cs_sub", "cs_exp", "pc_ok", "cb_ok")
        bias_ok, score_t, score_m, exp_ok, prob_ok, pt_t, pt_out, o_t = sems(
            "bias_ok", "score_t", "score_m", "exp_ok", "prob_ok", "pt_t", "pt_out", "o_t")
        y_sq, y_hi, y_lo, sq_sum, ysum_t, ysum_ok, yr_ok, guessed = sems(
            "y_sq", "y_hi", "y_lo", "sq_sum", "ysum_t", "ysum_ok", "yr_ok", "guessed")
        relu_ok, hid_ok, acc0, added, normed, fsq = sems("relu_ok", "hid_ok", "acc0", "added", "normed", "fsq")
        ht_t, ht_hi, ht_lo, hd_t, hd_hi, hd_lo = sems("ht_t", "ht_hi", "ht_lo", "hd_t", "hd_hi", "hd_lo")

        win = a["w_in"][0].rearrange("(k p) n -> p k n", p=P)
        uq = a["mla_w_uq"][0].rearrange("(k p) (h e) -> p k h e", p=P, e=NOPE + ROPE)
        ukv = a["mla_w_ukv"][0].rearrange("(k p) (h e) -> p k h e", p=P, e=NOPE + MV)
        wo = a["w_o"][0].rearrange("(k p) n -> p k n", p=P)
        up = a["w_up"][0].rearrange("(k p) (g n) -> p k g n", p=P, g=G)
        dn = a["w_down"][0].rearrange("(g k p) n -> p g k n", p=P, g=G)
        cw1 = [a[n][0].rearrange("(k p) n -> p k n", p=P) for n in ("cmp_w1_k", "cmp_w1_v")]

        def chunk(c):
            if c < B_IN:
                return [win[:, 2 * c:2 * c + 2, 0:CW]], (2, CW)
            if c < UQ_PE:
                k = 2 * (c - B_IN)
                return [win[:, k:k + 2, OFF_B:OFF_B + BW]], (2, BW)
            if c == UQ_PE:
                return [uq[:, k, :, NOPE:] for k in range(4)], (4, 512)
            if c < UKV_K:
                h = 4 * (c - UQ_NOPE)
                return [uq[:, k, h:h + 4, 0:NOPE] for k in range(4)], (4, 512)
            if c < A_IN:
                o = 0 if c == UKV_K else NOPE
                return [ukv[:, k, :, o:o + NOPE] for k in range(2)], (2, 1024)
            if c < CMP:
                k = 2 * (c - A_IN)
                return [win[:, k:k + 2, OFF_Q:OFF_B]], (2, 1024)
            if c < WO_M:
                j = c - CMP
                return [cw1[j // 2][:, 8 * (j % 2):8 * (j % 2) + 8, :]], (8, CMP_HID)
            if c < MLP0:
                part, n, j = (c - WO_M) // 8, (c - WO_M) // 4 % 2, (c - WO_M) % 4
                k = 8 * part + 2 * j
                return [wo[:, k:k + 2, 1024 * n:1024 * n + 1024]], (2, 1024)
            j = c - MLP0
            return [up[:, 2 * j:2 * j + 2, 0, :]], (2, 1024)

        LOOP0 = MLP0 + 8
        assert raw_slot(LOOP0) == 0 and split_slot(LOOP0) == 0

        def loads(c):
            return sum(len(chunk(k)[0]) for k in range(c % RAW, c + 1, RAW))

        LOADS0 = [loads(LOOP0 - RAW + s) for s in range(RAW)]

        x_rows = a["x"][0].rearrange("(t p) d -> t p d", p=P)
        o_rows = out[0].rearrange("(t p) d -> t p d", p=P)
        block = ctx.enter_context(nc.Block())

        @block.sync
        def _(sp):
            for t in range(TT):
                sp.dma_start(x_sb[:, t, :], x_rows[t]).then_inc(x_in[t], 16)
            for c in range(LOOP0):
                if c >= RAW:
                    sp.wait_ge(lo_done, c - RAW + 1)
                src, (b, w) = chunk(c)
                dst = raw[:, raw_slot(c), 0:b * w].rearrange("p (b w) -> p b w", b=b)
                if len(src) == 1:
                    sp.dma_start(dst, src[0]).then_inc(raw_in[raw_slot(c)], 16)
                else:
                    for k, piece in enumerate(src):
                        sp.dma_start(dst[:, k, :].rearrange("p (h e) -> p h e", h=piece.shape[1]), piece)\
                            .then_inc(raw_in[raw_slot(c)], 16)
                if c == CMP + 1:
                    sp.wait_ge(ysum_ok, 1)
                    for t in range(TT):
                        sp.dma_start(h_sb[:, t, :], x_rows[t]).then_inc(h_in, 16)
            with sp.Fori(1, G) as g:
                for j in range(GC):
                    sp.wait_ge(lo_done, LOOP0 - GC + j - RAW + 1 + GC * g)
                    dst = raw[:, j % RAW, :].rearrange("p (a n) -> p a n", a=2)
                    if j < 8:
                        src = up[:, 2 * j:2 * j + 2, bass.ds(g, 1), :].rearrange("p a g n -> p a (g n)")
                    else:
                        k, n = 2 * (j % 4), (j - 8) // 4
                        src = dn[:, bass.ds(g - 1, 1), k:k + 2, 1024 * n:1024 * n + 1024].rearrange("p g a n -> p (g a) n")
                    sp.dma_start(dst, src).then_inc(raw_in[j % RAW], 16)
            for j in range(8):
                k, n = 2 * (j % 4), j // 4
                sp.wait_ge(lo_done, LOOP0 + GC * (G - 1) + j - RAW + 1)
                sp.dma_start(raw[:, j % RAW, :].rearrange("p (a n) -> p a n", a=2),
                             dn[:, G - 1, k:k + 2, 1024 * n:1024 * n + 1024]).then_inc(raw_in[j % RAW], 16)
            sp.wait_ge(w_used, LOOP0 + GC * (G - 1))
            sp.dma_start(fw[:, :], a["final_norm_w"].rearrange("(o d) -> o d", o=1).broadcast_to((P, D))).then_inc(fw_in, 16)
            for t in range(TT):
                sp.wait_ge(normed, t + 1)
                sp.dma_start(o_rows[t], h_sb[:, t, :]).then_inc(stored, 16)
            sp.wait_ge(stored, 16 * TT)

        @block.gpsimd
        def _(pool):
            chain = [0]

            def link(ins):
                chain[0] += 1
                ins.then_inc(pool_c, 1)
                pool.wait_ge(pool_c, chain[0])

            link(pool.memset(ident[:, :], 0.0))
            link(pool.affine_select(out=ident[:, :], in_=ident[:, :], compare_op=ALU.not_equal, fill=1.0, base=0,
                                    pattern=[[-1, P]], channel_multiplier=1))
            pool.memset(ones[:, :], 1.0).then_inc(consts, 1)
            pool.iota(di[:, 0:P], [[-1, P]], base=0, channel_multiplier=1)
            link(pool.iota(di[:, P:SEEN], [[-1, T]], base=P, channel_multiplier=1))
            link(pool.iota(cdi[:, :, :], [[P, TT], [-CMP_STRIDE, NC]], base=1 - CMP_LEN, channel_multiplier=1))
            link(pool.tensor_copy(dist[:, :], di[:, :]))
            link(pool.tensor_scalar(mask[:, :], dist[:, :], 0.0, BIG, ALU.is_lt, ALU.mult))
            link(pool.tensor_tensor(dist[:, :], dist[:, :], mask[:, :], ALU.add))
            link(pool.tensor_copy(cdist[:, :, :], cdi[:, :, :]))
            link(pool.tensor_scalar(valid[:, :], cdist[:, :, 0], 0.0, None, ALU.is_ge))
            cm = cden[:, 0:TT * NC].rearrange("p (t n) -> p t n", t=TT)
            link(pool.tensor_scalar(cm, cdist[:, :, :], 0.0, BIG, ALU.is_lt, ALU.mult))
            pool.tensor_tensor(cdist[:, :, :], cdist[:, :, :], cm, ALU.add).then_inc(tables, 1)
            pool.wait_ge(tables, 1)

            def improve(y, square, w):
                for _ in range(3):
                    link(pool.tensor_tensor(w, y, y, ALU.mult))
                    link(pool.tensor_tensor(w, w, square, ALU.mult))
                    link(pool.tensor_scalar(w, w, -0.5, 1.5, ALU.mult, ALU.add))
                    link(pool.tensor_tensor(y, y, w, ALU.mult))

            pool.wait_ge(guessed, 1)
            improve(r1[:, :], ssq[:, 0:2], root_w[:, 0:2])
            pool.tensor_scalar(r1q[:, :], r1[:, :], -NSA_SCALE, None, ALU.mult).then_inc(rs_ok, 1)
            pool.wait_ge(guessed, 2)
            improve(rc[:, :], ssq[:, 2:6], root_w[:, :])
            pool.tensor_copy(root_w[:, :], rc[:, :]).then_inc(rs_ok, 1)

            def rotate(src, dst, heads, t):
                x = src.rearrange("p (h c e) -> p h c e", h=heads, c=2)
                y = dst.rearrange("p (h c e) -> p h c e", h=heads, c=2)
                sin, cos = [cs[:, i, t * HALF:(t + 1) * HALF].unsqueeze(1).broadcast_to((P, heads, HALF)) for i in range(2)]
                u, v = [rtmp[:, i, 0:heads * HALF].rearrange("p (h e) -> p h e", h=heads) for i in range(2)]
                pool.tensor_tensor(u, x[:, :, 0, :], cos, ALU.mult)
                link(pool.tensor_tensor(v, x[:, :, 1, :], sin, ALU.mult))
                link(pool.tensor_tensor(y[:, :, 0, :], u, v, ALU.subtract))
                pool.tensor_tensor(u, x[:, :, 1, :], cos, ALU.mult)
                link(pool.tensor_tensor(v, x[:, :, 0, :], sin, ALU.mult))
                return pool.tensor_tensor(y[:, :, 1, :], u, v, ALU.add)

            pool.wait_ge(sin_ok, 1)
            pool.wait_ge(act_free, 2)
            for t in range(TT):
                link(rotate(c_sb[:, t, QR + KVR:CW], kpe[:, t, 0:ROPE], 1, t))
                pool.tensor_copy(kpe[:, t, ROPE:2 * ROPE], kpe[:, t, 0:ROPE]).then_inc(kpe_ok, 1)
            pool.wait_ge(act_free, 4)
            for i, off in enumerate((256, 384, 512, 640, 0, 128, 64, 192)):
                src = kv_sb[:, :, off:off + DK].unsqueeze(2).broadcast_to((P, TT, 2, DK))
                pool.tensor_copy(kd[:, i, :, :, :], src).then_inc(kd_ok, 1)
            for t in range(TT):
                pool.wait_ge(qpe_out, t + 1)
                link(rotate(qpe[:, t, :], qpr[:, t, :], MH, t))
                pool.tensor_copy(scl[:, 0, :], ones[:, 0:1].broadcast_to((P, 2))).then_inc(qpr_ok, 1)

            def sum_squares(u):
                part = u // MH
                s = sqacc[:, part, :]
                pool.wait_ge(y_sq, u + 1)
                if u % MH == 0:
                    pool.tensor_copy(s, sq[:, u % 2, :]).then_inc(sq_sum, 1)
                else:
                    pool.wait_ge(sq_sum, u)
                    pool.tensor_tensor(s, s, sq[:, u % 2, :], ALU.add).then_inc(sq_sum, 1)

            def root_of_sums(part, dst):
                pool.wait_ge(guessed, 3 + part)
                improve(dst, ssq[:, 6 + 2 * part:8 + 2 * part], root_w[:, 0:2])
                pool.tensor_copy(root_w[:, 0:2], dst).then_inc(yr_ok, 1)

            for u in range(MH):
                sum_squares(u)
            root_of_sums(0, rm[:, :])
            pool.wait_ge(w_used, CMP)
            for h in range(NH):
                m = pool.tensor_scalar(cbias[:, h, :, :], cdist[:, :, :], SLOPE[h], None, ALU.mult)
            m.then_inc(cb_ok, 1)
            made = 0
            for i in range(NMLA, len(STEPS) + 3):
                if i < len(STEPS) and STEPS[i][0] == "slc":
                    while made < min(NH, STEPS[i][2] + 2):
                        if made >= 2:
                            pool.wait_ge(score_m, NMLA + 2 * made - 2)
                        pool.tensor_scalar(bias_h[:, made % 2, :], dist[:, :], SLOPE[made], None, ALU.mult).then_inc(bias_ok, 1)
                        made += 1
                for u in range(MH, 16):
                    if LASTSTEP[u] + 3 == i:
                        sum_squares(u)
            root_of_sums(1, rn[:, :])
            pool.wait_ge(y_lo, 16)
            pool.memset(acc[:, :, :], 0.0).then_inc(acc0, 1)

            def square(t, n):
                pool.wait_ge(relu_ok, n)
                pool.tensor_tensor(hid[:, t, :], hid[:, t, :], hid[:, t, :], ALU.mult).then_inc(hid_ok, 1)

            for t in range(TT):
                square(t, t + 1)
            with pool.Fori(1, G) as g:
                for t in range(TT):
                    square(t, 2 * g + t + 1)

        def sums_ready(eng, t, group, last):
            if t == 0:
                eng.wait_ge(first_done, group + 1)
            else:
                eng.wait_ge(w_used, last + 1)

        @block.scalar
        def _(act):
            for name, row, n in (("attn_norm_w", 0, 16), ("mlp_norm_w", 16, 16), ("mla_q_norm_w", 32, 4),
                                 ("mla_kv_norm_w", 36, 2), ("mla_out_norm_w", 38, 8), ("nsa_out_norm_w", 46, 8)):
                act.dma_start(prm[row:row + n, :], a[name][0].rearrange("(r p) -> r p", p=P)).then_inc(prm_in, 16)
            for name, row in (("cmp_pos_k", 54), ("cmp_pos_v", 70)):
                act.dma_start(prm[row:row + 16, :], a[name][0].rearrange("(r two) d -> r (two d)", two=2)).then_inc(prm_in, 16)
            act.dma_start(posi[:, :], a["positions"].rearrange("b (t p) -> p (b t)", p=P),
                          allow_slow_non_contiguous=True).then_inc(cst_in, 16)
            act.dma_start(invf[:, :], a["inv_freq"].rearrange("(o d) -> o d", o=1).broadcast_to((P, HALF))).then_inc(cst_in, 16)
            for twice in range(2):
                act.dma_start(w2k[:, :, twice, :], a["cmp_w2_k"][0].rearrange("(k p) n -> p k n", p=P)).then_inc(w2_in, 16)
            act.dma_start(w2v[:, :, :], a["cmp_w2_v"][0].rearrange("(k p) n -> p k n", p=P)).then_inc(w2_in, 16)

            def split_hi(c):
                act.wait_ge(raw_in[raw_slot(c)], 16 * loads(c))
                if c >= SPLIT:
                    act.wait_ge(w_used, c - SPLIT + 1)
                b, w = chunk(c)[1]
                act.activation(w_hi[:, split_slot(c), 0:b * w], raw[:, raw_slot(c), 0:b * w], ACT.Copy).then_inc(hi_done, 1)

            def split_hi_loop(j, g):
                act.wait_ge(raw_in[j % RAW], 16 * (LOADS0[j % RAW] + j // RAW + 1 - GC // RAW) + 16 * (GC // RAW) * g)
                act.wait_ge(w_used, LOOP0 + j - GC - SPLIT + 1 + GC * g)
                act.activation(w_hi[:, j % SPLIT, :], raw[:, j % RAW, :], ACT.Copy).then_inc(hi_done, 1)

            act.wait_ge(ang_ok, 1)
            act.activation(cs[:, :, :], angs[:, :, :], ACT.Sin).then_inc(sin_ok, 1)
            act.wait_ge(wcols_ok, 1)
            for k in range(KT):
                act.wait_ge(xt_t, k + 1)
                act.activation(xT[:, 0, k, :], bank(k % 8, T), ACT.Copy, scale=wcols[:, k:k + 1]).then_inc(xt_hi, 1)
                if k in (9, 13):
                    split_hi(k // 13)
            for t in range(TT):
                if t:
                    act.wait_ge(ssq_ok, t)
                act.activation(sink[:, :], x_sb[:, t, :], ACT.Square, accum_out=ssq[:, t:t + 1]).then_inc(ssq_ok, 1)
            for c in range(2, 10):
                split_hi(c)
            act.wait_ge(rs_ok, 1)
            for t in range(TT):
                sums_ready(act, t, 0, UQ_PE - 9)
                act.activation(c_sb[:, t, :], flat[:, 1024 * t:1024 * t + CW], ACT.Copy, scale=r1[:, t:t + 1]).then_inc(act_free, 1)
            n = 2
            for t in range(TT):
                act.wait_ge(act_free, t + 1)
                for i, (lo, hi) in enumerate(((0, QR), (QR, QR + KVR))):
                    act.wait_ge(ssq_ok, n)
                    n += 1
                    act.activation(sink[:, lo:hi], c_sb[:, t, lo:hi], ACT.Square,
                                   accum_out=ssq[:, 2 + 2 * i + t:3 + 2 * i + t]).then_inc(ssq_ok, 1)
            for c in range(10, 18):
                split_hi(c)
            for k in range(6):
                act.wait_ge(ct_t, k + 1)
                act.activation(cT[:, 0, k, :], bank(k % 4, T), ACT.Copy,
                               scale=wcols[:, PRM["c"] + k:PRM["c"] + k + 1]).then_inc(ct_hi, 1)
            for t in range(TT):
                sums_ready(act, t, 1, UQ_PE - 1)
                act.activation(kv_sb[:, t, :], flat[:, 2048 + 1024 * t:2048 + 1024 * t + BW], ACT.Copy,
                               scale=r1[:, t:t + 1]).then_inc(act_free, 1)
            act.wait_ge(act_free, 4)
            act.activation(gates[:, :, :], kv_sb[:, :, 768:BW], ACT.Exp, scale=-1.0).then_inc(gexp, 1)
            split_hi(18)
            act.wait_ge(kpe_ok, 2)
            act.wait_ge(w_used, UQ_PE + 1)
            for t in range(TT):
                act.activation(qpe[:, t, :], bank(6 + t), ACT.Copy, scale=-MLA_SCALE).then_inc(qpe_out, 1)
            split_hi(19)
            for i, b0 in ((0, 4), (1, 2)):
                act.wait_ge(w_used, UQ_NOPE + i + 1)
                for j in range(2):
                    act.activation(qnT[:, 4 * i + 2 * j:4 * i + 2 * j + 2, :], pairs(bank(b0 + j)), ACT.Copy,
                                   scale=-MLA_SCALE).then_inc(qn_out, 1)
                split_hi(20 + i)
            for t in range(2):
                act.wait_ge(qp_t, t + 1)
                act.activation(qpT[:, 2 * t:2 * t + 2, :], pairs(bank(4 + t)), ACT.Copy).then_inc(qp_out, 1)
            act.wait_ge(qp_t, 3)
            act.activation(kpT[:, :], bank(2, T), ACT.Copy).then_inc(qp_out, 1)
            act.wait_ge(blk_f, 1)
            act.activation(blk[:, 0, :, :, :].rearrange("p y k n -> p (y k n)"),
                           blkf[:, :, :, :].rearrange("p y k n -> p (y k n)"), ACT.Copy).then_inc(blk_hi, 1)

            def slot(i, lo, hi):
                if lo <= i < hi and i in SOFT:
                    n = SOFT[i]
                    act.wait_ge(score_m, n + 1)
                    p = prob[:, n % 3, :]
                    act.activation(p[:, 0:P], p[:, 0:P], ACT.Exp, scale=-1.0, bias=nmax[:, n, 0:1], accum_out=den[:, n, 0:1])
                    act.activation(p[:, P:SEEN], p[:, P:SEEN], ACT.Exp, scale=-1.0, bias=nmax[:, n, 1:2],
                                   accum_out=den[:, n, 1:2]).then_inc(exp_ok, 1)
                j = i - 2
                if lo <= j < hi:
                    act.wait_ge(pt_t, j + 1)
                    if j >= 2:
                        act.wait_ge(o_t, j - 1)
                    r, w = (NC, 512) if STEPS[j][0] == "cmp" else (P, SEEN)
                    act.activation(probT[0:r, j % 2, 0:w], bank(6, w, 0, r), ACT.Copy).then_inc(pt_out, 1)
                j = i - 3
                if lo <= j < hi and LASTSTEP[STEPS[j][1]] == j:
                    u = STEPS[j][1]
                    act.wait_ge(o_t, j + 1)
                    if u >= 2:
                        act.wait_ge(sq_sum, u - 1)
                    act.activation(sq[:, u % 2, :], bank(7, T), ACT.Square).then_inc(y_sq, 1)
                    act.activation(yT[:, u, 0, :], bank(7, T), ACT.Copy,
                                   scale=wcols[:, PRM["y"] + u:PRM["y"] + u + 1]).then_inc(y_hi, 1)

            for kind, i in MLA_PLAN:
                if kind == "hi":
                    split_hi(i)
                elif kind == "s":
                    slot(i, 0, NMLA)
            for t in range(TT):
                sums_ready(act, t, 2, CMP - 1)
                act.activation(q_sb[:, t, :], flat[:, 1024 * t:1024 * t + 1024], ACT.Copy, scale=r1q[:, t:t + 1]).then_inc(act_free, 1)
            for j in range(4):
                act.wait_ge(q_t, j + 1)
                act.activation(qT[:, 2 * j:2 * j + 2, :], pairs(bank(j)), ACT.Copy).then_inc(q_out, 1)
            for kind, i in NSA_PLAN:
                if kind == "hi":
                    split_hi(i)
                elif kind == "s":
                    slot(i, NMLA, len(STEPS))
                elif i == "gelu":
                    act.wait_ge(w_used, CMP + 4)
                    act.activation(h1a[:, :, :], ps[0:2 * NC, 0:2, 0:CMP_HID], ACT.Square).then_inc(g_sq, 1)
                    act.wait_ge(g_in, 1)
                    act.activation(h1c[:, :, :], h1b[:, :, :], ACT.Tanh, scale=float(np.sqrt(2 / np.pi))).then_inc(g_th, 1)
                elif i == "soft":
                    act.wait_ge(cs_sub, 1)
                    act.activation(pc[:, :, :, :].rearrange("p h t n -> p (h t n)"), pc[:, :, :, :].rearrange("p h t n -> p (h t n)"),
                                   ACT.Exp, scale=-1.0).then_inc(cs_exp, 1)

            def turned_hi(k):
                act.wait_ge(ht_t, k + 1)
                act.activation(xT[:, 0, k, :], bank(4 + k % 4, T), ACT.Copy,
                               scale=wcols[:, PRM["mlp"] + k:PRM["mlp"] + k + 1]).then_inc(ht_hi, 1)

            for c in range(WO_N, MLP0):
                split_hi(c + 1)
                if c >= WO_N + 5:
                    for k in TURNS[c - WO_N - 5]:
                        turned_hi(k)
            for k in range(8, KT):
                turned_hi(k)
            for t in range(TT):
                act.wait_ge(ssq_ok, 6 + t)
                act.activation(sink2[:, :], h_sb[:, t, :], ACT.Square, accum_out=ssq[:, 10 + t:11 + t]).then_inc(ssq_ok, 1)

            def relu(group, last):
                for t in range(TT):
                    sums_ready(act, t, group, last)
                    act.activation(hid[:, t, :], flat[:, 1024 * t:1024 * t + 1024], ACT.Relu).then_inc(relu_ok, 1)

            def hidden_hi(done):
                for q in range(4):
                    act.wait_ge(hd_t, done + q + 1)
                    act.activation(hidT[:, 0, 2 * q:2 * q + 2, :], pairs(bank(4 + q)), ACT.Copy).then_inc(hd_hi, 1)

            for c in range(MLP0 + 1, LOOP0):
                split_hi(c)
            split_hi_loop(0, 1)
            relu(7, LOOP0 - 1)
            hidden_hi(0)
            with act.Fori(1, G) as g:
                for j in range(1, GC + 1):
                    split_hi_loop(j, g) if j < GC else split_hi_loop(0, g + 1)
                    if j == 9:
                        relu(8 - 3 + 3 * g, LOOP0 - GC + 7 + GC * g)
                hidden_hi(4 * g)
            for j in range(1, 8):
                split_hi_loop(j, G)
            for t in range(TT):
                act.wait_ge(added, t + 1)
                if t:
                    act.wait_ge(fsq, t)
                act.activation(sink2[:, :], h_sb[:, t, :], ACT.Square, accum_out=ssq[:, 12 + t:13 + t]).then_inc(fsq, 1)

        @block.vector
        def _(dve):
            chain = [0]

            def link(ins):
                chain[0] += 1
                ins.then_inc(dve_c, 1)
                dve.wait_ge(dve_c, chain[0])

            def low(dst, src, high, scale=None):
                if scale is None:
                    return dve.tensor_tensor(dst, src, high.bitcast(F32), ALU.subtract)
                return dve.scalar_tensor_tensor(out=dst, in0=src, scalar=scale, in1=high.bitcast(F32), op0=ALU.mult, op1=ALU.subtract)

            def split_lo(c):
                dve.wait_ge(hi_done, c + 1)
                b, w = chunk(c)[1]
                low(w_lo[:, split_slot(c), 0:b * w], raw[:, raw_slot(c), 0:b * w], w_hi[:, split_slot(c), 0:b * w]).then_inc(lo_done, 1)

            def split_lo_loop(j, g):
                dve.wait_ge(hi_done, LOOP0 - GC + j + 1 + GC * g)
                low(w_lo[:, j % SPLIT, :], raw[:, j % RAW, :], w_hi[:, j % SPLIT, :]).then_inc(lo_done, 1)

            def guess(y, square):
                yi = y.bitcast(I32)
                link(dve.tensor_scalar(yi, square.bitcast(I32), 1, None, ALU.logical_shift_right))
                return dve.tensor_scalar(yi, yi, -1.0, float(0x5F3759DF), ALU.mult, ALU.add)

            dve.wait_ge(cst_in, 32)
            link(dve.tensor_copy(posf[:, :], posi[:, :]))
            for v in range(2):
                for t in range(TT):
                    m = dve.tensor_scalar(angs[:, v, t * HALF:(t + 1) * HALF], invf[:, :], posf[:, t:t + 1], None, ALU.mult)
            link(m)
            for v, quarter in ((0, 0.0), (1, 0.25)):
                m = dve.tensor_scalar(angk[:, v, :], angs[:, v, :], 1.0 / TWO_PI, quarter, ALU.mult, ALU.add)
            link(m)
            link(dve.tensor_scalar(angk[:, :, :], angk[:, :, :], MAGIC, None, ALU.add))
            link(dve.tensor_scalar(angk[:, :, :], angk[:, :, :], -MAGIC, None, ALU.add))
            for c in (C1, C2, C3):
                link(dve.scalar_tensor_tensor(out=angs[:, :, :], in0=angk[:, :, :], scalar=-c, in1=angs[:, :, :],
                                              op0=ALU.mult, op1=ALU.add))
            link(dve.tensor_scalar(angs[:, 1, :], angs[:, 1, :], float(np.pi / 2), None, ALU.add))
            dve.tensor_scalar(angs[:, :, :], angs[:, :, :], PI_IN, -PI_IN, ALU.min, ALU.max).then_inc(ang_ok, 1)

            dve.wait_ge(prm_t, 1)
            dve.tensor_copy(wcols[:, :], bank(7, NPRM)).then_inc(wcols_ok, 1)
            dve.wait_ge(wcols_ok, 1)
            for k in range(KT):
                dve.wait_ge(xt_hi, k + 1)
                low(xT[:, 1, k, :], bank(k % 8, T), xT[:, 0, k, :], wcols[:, k:k + 1]).then_inc(xt_lo, 1)
                if k in (9, 13):
                    split_lo(k // 13)
            dve.wait_ge(ssq_ok, 2)
            link(dve.tensor_scalar(ssq[:, 0:2], ssq[:, 0:2], 1.0 / D, EPS, ALU.mult, ALU.add))
            guess(r1[:, :], ssq[:, 0:2]).then_inc(guessed, 1)
            for c in range(2, 10):
                split_lo(c)
            dve.wait_ge(ssq_ok, 6)
            link(dve.tensor_scalar(ssq[:, 2:4], ssq[:, 2:4], 1.0 / QR, EPS, ALU.mult, ALU.add))
            link(dve.tensor_scalar(ssq[:, 4:6], ssq[:, 4:6], 1.0 / KVR, EPS, ALU.mult, ALU.add))
            guess(rc[:, :], ssq[:, 2:6]).then_inc(guessed, 1)
            for c in range(10, 13):
                split_lo(c)
            dve.wait_ge(rs_ok, 2)
            for t in range(TT):
                dve.tensor_scalar(c_sb[:, t, 0:QR], c_sb[:, t, 0:QR], rc[:, t:t + 1], None, ALU.mult)
                m = dve.tensor_scalar(c_sb[:, t, QR:QR + KVR], c_sb[:, t, QR:QR + KVR], rc[:, 2 + t:3 + t], None, ALU.mult)
            m.then_inc(c_norm, 1)
            for c in range(13, 18):
                split_lo(c)
            for k in range(6):
                dve.wait_ge(ct_hi, k + 1)
                low(cT[:, 1, k, :], bank(k % 4, T), cT[:, 0, k, :], wcols[:, PRM["c"] + k:PRM["c"] + k + 1]).then_inc(ct_lo, 1)
            dve.wait_ge(gexp, 1)
            link(dve.tensor_scalar(gates[:, :, :], gates[:, :, :], 1.0, None, ALU.add))
            link(dve.reciprocal(gates[:, :, :], gates[:, :, :]))
            by_head = gates[:, :, :].rearrange("p t (h b) -> p b h t", b=3)
            dve.wait_ge(tables, 1)
            dve.tensor_tensor(cgate[:, :, :], by_head[:, 0, :, :], valid[:, :].unsqueeze(1).broadcast_to((P, NH, TT)),
                              ALU.mult).then_inc(gate_ok, 1)
            for c in range(18, 21):
                split_lo(c)
            dve.wait_ge(w_used, UKV_K + 1)
            for j, b in enumerate((0, 1, 6, 7)):
                dve.tensor_copy(knT[:, 2 * j:2 * j + 2, :], pairs(bank(b))).then_inc(kn_out, 1)
            split_lo(21)
            dve.wait_ge(w_used, UKV_V + 1)
            for t, col in ((0, 2048), (1, 1024)):
                dve.tensor_copy(v_sb[:, t, :], flat[:, col:col + 1024]).then_inc(v_out, 1)
            for j in range(2):
                dve.wait_ge(kv_t, j + 1)
                dve.tensor_copy(kT[:, 2 * j:2 * j + 2, :], pairs(bank(j))).then_inc(kv_out, 1)
            for j in range(2):
                dve.wait_ge(kv_t, 3 + j)
                src = pairs(bank(6 + j))
                dve.tensor_copy(kcT[0:64, 2 * j:2 * j + 2, :], src[0:64, :, :])
                dve.tensor_copy(kcT[64:P, 2 * j:2 * j + 2, 0:T - 1], src[64:P, :, 1:T]).then_inc(kv_out, 1)
            dve.wait_ge(kv_out, 4)
            for y in range(2):
                for g in range(NG):
                    for half in range(2):
                        src = kcT[:, 2 * y + g, 16 * half:16 * half + 16 * NC].rearrange("p (n k two) -> p k n two", n=NC, two=2)[:, :, :, 0]
                        o = PRM["posk"] + 16 * y + 8 * half
                        m = dve.tensor_tensor(blkf[:, y, 8 * half:8 * half + 8, NC * g:NC * g + NC], src,
                                              wcols[:, o:o + 8].unsqueeze(2).broadcast_to((P, 8, NC)), ALU.add)
            m.then_inc(blk_f, 1)
            dve.wait_ge(blk_hi, 1)
            low(blk[:, 1, :, :, :].rearrange("p y k n -> p (y k n)"), blkf[:, :, :, :].rearrange("p y k n -> p (y k n)"),
                blk[:, 0, :, :, :].rearrange("p y k n -> p (y k n)")).then_inc(blk_ok, 1)

            STEP_OF = {n: i for i, n in SOFT.items()}

            def slot(i, lo, hi):
                if lo <= i < hi and i in SOFT:
                    n = SOFT[i]
                    kind, u, h, branch = STEPS[i]
                    dve.wait_ge(score_t, n + 1)
                    if n >= 3:
                        dve.wait_ge(pt_t, STEP_OF[n - 3] + 1)
                    if kind == "mla":
                        bias = mask[:, :]
                    else:
                        dve.wait_ge(bias_ok, h + 1)
                        bias = bias_h[:, h % 2, :]
                    for q, (x, y) in enumerate(((0, P), (P, SEEN))):
                        m = dve.tensor_tensor_reduce(prob[:, n % 3, x:y], ps[:, 4 + n % 2, x:y], bias[:, x:y], 1.0, 3e38,
                                                     ALU.add, ALU.min, nmax[:, n, q:q + 1])
                    m.then_inc(score_m, 1)
                if lo <= i - 1 < hi and i - 1 in SOFT:
                    n = SOFT[i - 1]
                    kind, u, h, branch = STEPS[i - 1]
                    dve.wait_ge(exp_ok, n + 1)
                    link(dve.reciprocal(scl[:, n, :], den[:, n, :]))
                    if kind != "mla":
                        b = 1 if kind == "slc" else 2
                        link(dve.tensor_tensor(scl[:, n, :], scl[:, n, :], by_head[:, b, h, :], ALU.mult))
                    p = prob[:, n % 3, :]
                    dve.tensor_scalar(p[:, 0:P], p[:, 0:P], scl[:, n, 0:1], None, ALU.mult)
                    dve.tensor_scalar(p[:, P:SEEN], p[:, P:SEEN], scl[:, n, 1:2], None, ALU.mult).then_inc(prob_ok, 1)
                j = i - 3
                if lo <= j < hi and LASTSTEP[STEPS[j][1]] == j:
                    u = STEPS[j][1]
                    dve.wait_ge(y_hi, u + 1)
                    low(yT[:, u, 1, :], bank(7, T), yT[:, u, 0, :], wcols[:, PRM["y"] + u:PRM["y"] + u + 1]).then_inc(y_lo, 1)

            def mean_square(part, dst):
                dve.wait_ge(ysum_t, part + 1)
                square = ssq[:, 6 + 2 * part:8 + 2 * part]
                dve.tensor_scalar(square, ps[:, 7, 256:258], 1.0 / (MH * MV), EPS, ALU.mult, ALU.add).then_inc(ysum_ok, 1)
                dve.wait_ge(ysum_ok, part + 1)
                guess(dst, square).then_inc(guessed, 1)

            for kind, i in MLA_PLAN:
                if kind == "lo":
                    split_lo(i)
                elif kind == "s":
                    slot(i, 0, NMLA)
            mean_square(0, rm[:, :])

            def add_attention(part, n, group, last):
                dve.wait_ge(yr_ok, part + 1)
                dve.wait_ge(h_in, 32)
                r = (rm, rn)[part]
                for t in range(TT):
                    sums_ready(dve, t, group, last)
                    if part:
                        dve.wait_ge(dve_free, 2 * n + t + 1)
                    o = h_sb[:, t, 1024 * n:1024 * n + 1024]
                    dve.scalar_tensor_tensor(out=o, in0=flat[:, 1024 * t:1024 * t + 1024], scalar=r[:, t:t + 1], in1=o,
                                             op0=ALU.mult, op1=ALU.add).then_inc(dve_free, 1)

            for kind, i in NSA_PLAN:
                if kind == "w" and i == WO_M + 4:
                    add_attention(0, 0, 3, WO_M + 3)
                elif kind == "lo":
                    split_lo(i)
                elif kind == "s":
                    slot(i, NMLA, len(STEPS))
                elif i == "gelu":
                    u = ps[0:2 * NC, 0:2, 0:CMP_HID]
                    dve.wait_ge(g_sq, 1)
                    link(dve.tensor_scalar(h1b[:, :, :], h1a[:, :, :], 0.044715, 1.0, ALU.mult, ALU.add))
                    dve.tensor_tensor(h1b[:, :, :], u, h1b[:, :, :], ALU.mult).then_inc(g_in, 1)
                    dve.wait_ge(g_th, 1)
                    dve.scalar_tensor_tensor(out=h1a[:, :, :], in0=h1c[:, :, :], scalar=1.0, in1=u, op0=ALU.add,
                                             op1=ALU.mult).then_inc(g_ok, 1)
                elif i == "turn":
                    dve.wait_ge(g_t, 1)
                    dve.tensor_scalar(h1T[:, :, :].rearrange("p k n -> p (k n)"), bank(2, 4 * 2 * NC), 0.5, None, ALU.mult).then_inc(g_turned, 1)
                elif i == "project":
                    dve.wait_ge(k_t, 1)
                    dve.tensor_copy(kcmpT[:, :], bank(3, 2 * NC))
                    dve.tensor_copy(vcmp[:, :, :], ps[0:NC, 3, 64:64 + NG * DK].rearrange("p (g d) -> p g d", g=NG)).then_inc(k_ok, 1)
                elif i == "soft":
                    rows = pc[:, :, :, :].rearrange("p h t n -> p (h t) n")
                    by_parity = [b[:, :, :, :].rearrange("p (i e) t n -> p e i (t n)", e=2) for b in (pc, cbias)]
                    sums = ps[:, 2:4, 0:NH * NC].rearrange("p e (i m) -> p e i m", i=NH // 2)
                    dve.wait_ge(cs_t, 1)
                    dve.wait_ge(cb_ok, 1)
                    link(dve.tensor_tensor(by_parity[0], sums, by_parity[1], ALU.add))
                    link(dve.tensor_reduce(cmx[:, :], rows, AX.X, ALU.min))
                    dve.tensor_tensor(rows, rows, cmx[:, :].unsqueeze(2).broadcast_to((P, NH * TT, NC)), ALU.subtract).then_inc(cs_sub, 1)
                    dve.wait_ge(cs_exp, 1)
                    link(dve.tensor_reduce(cden[:, :], rows, AX.X, ALU.add))
                    link(dve.reciprocal(cden[:, :], cden[:, :]))
                    link(dve.tensor_tensor(cden[:, :], cden[:, :], cgate[:, :, :].rearrange("p h t -> p (h t)"), ALU.mult))
                    dve.tensor_tensor(rows, rows, cden[:, :].unsqueeze(2).broadcast_to((P, NH * TT, NC)), ALU.mult).then_inc(pc_ok, 1)
            add_attention(0, 1, 4, WO_N - 1)
            mean_square(1, rn[:, :])

            def turned_lo(k):
                dve.wait_ge(ht_hi, k + 1)
                low(xT[:, 1, k, :], bank(4 + k % 4, T), xT[:, 0, k, :], wcols[:, PRM["mlp"] + k:PRM["mlp"] + k + 1]).then_inc(ht_lo, 1)

            for c in range(WO_N, MLP0):
                if c == WO_N + 4:
                    add_attention(1, 0, 5, WO_N + 3)
                split_lo(c + 1)
                if c >= WO_N + 5:
                    for k in TURNS[c - WO_N - 5]:
                        turned_lo(k)
            add_attention(1, 1, 6, MLP0 - 1)
            for k in range(8, KT):
                turned_lo(k)
            for c in range(MLP0 + 1, LOOP0):
                split_lo(c)
            split_lo_loop(0, 1)
            dve.wait_ge(ssq_ok, 8)
            link(dve.tensor_scalar(r1q[:, :], ssq[:, 10:12], 1.0 / D, EPS, ALU.mult, ALU.add))
            link(dve.reciprocal(r1[:, :], r1q[:, :]))
            dve.wait_ge(acc0, 1)

            def hidden_lo(done):
                for q in range(4):
                    dve.wait_ge(hd_hi, done + q + 1)
                    low(hidT[:, 1, 2 * q:2 * q + 2, :], pairs(bank(4 + q)), hidT[:, 0, 2 * q:2 * q + 2, :]).then_inc(hd_lo, 1)

            def add_down(n, group, last, before):
                for t in range(TT):
                    sums_ready(dve, t, group, last)
                    dve.wait_ge(dve_free, before + 2 * n + t + 1)
                    o = acc[:, t, 1024 * n:1024 * n + 1024]
                    c0 = 2048 - 2048 * n + 1024 * t
                    dve.tensor_tensor(o, flat[:, c0:c0 + 1024], o, ALU.add).then_inc(dve_free, 1)

            hidden_lo(0)
            with dve.Fori(1, G) as g:
                for j in range(1, GC + 1):
                    split_lo_loop(j, g) if j < GC else split_lo_loop(0, g + 1)
                    if j == 13:
                        add_down(0, 9 - 3 + 3 * g, LOOP0 - GC + 11 + GC * g, 4 * g)
                add_down(1, 10 - 3 + 3 * g, LOOP0 - GC + 15 + GC * g, 4 * g)
                hidden_lo(4 * g)
            END = LOOP0 + GC * (G - 1)
            for j in range(1, 6):
                split_lo_loop(j, G)
            add_down(0, 8 + 3 * (G - 1), END + 3, 4 * G)
            for j in range(6, 8):
                split_lo_loop(j, G)
            add_down(1, 9 + 3 * (G - 1), END + 7, 4 * G)
            dve.wait_ge(dve_free, 8 + 4 * G)
            for t in range(TT):
                dve.scalar_tensor_tensor(out=h_sb[:, t, :], in0=acc[:, t, :], scalar=r1[:, t:t + 1], in1=h_sb[:, t, :],
                                         op0=ALU.mult, op1=ALU.add).then_inc(added, 1)
            dve.wait_ge(fw_in, 16)
            for t in range(TT):
                dve.wait_ge(fsq, t + 1)
                square, y, w = ssq[:, 12 + t:13 + t], rc[:, t:t + 1], rc[:, 2 + t:3 + t]
                link(dve.tensor_scalar(square, square, 1.0 / D, EPS, ALU.mult, ALU.add))
                link(guess(y, square))
                for _ in range(3):
                    link(dve.scalar_tensor_tensor(out=w, in0=y, scalar=y, in1=square, op0=ALU.mult, op1=ALU.mult))
                    link(dve.tensor_scalar(w, w, -0.5, 1.5, ALU.mult, ALU.add))
                    link(dve.tensor_tensor(y, y, w, ALU.mult))
                dve.scalar_tensor_tensor(out=h_sb[:, t, :], in0=h_sb[:, t, :], scalar=y, in1=fw[:, :],
                                         op0=ALU.mult, op1=ALU.mult).then_inc(normed, 1)

        @block.tensor
        def _(pe):
            def products(slot, shape, stationary, base, start, stop, free=None):
                blocks, width = shape
                cols = [(n, min(width, n + 512)) for n in range(0, width, 512)]
                for b in range(blocks):
                    for t in range(TT):
                        if start and b == 0 and free is not None:
                            free(t)
                        first, last = start and b == 0, stop and b == blocks - 1
                        for n0, n1 in cols:
                            o = flat[:, base[t] + n0:base[t] + n1]
                            w = slice(b * width + n0, b * width + n1)
                            pe.matmul(o, stationary(0, b, t), w_hi[:, slot, w], start=first, stop=False)
                            pe.matmul(o, stationary(0, b, t), w_lo[:, slot, w], start=False, stop=False)
                        for n0, n1 in cols:
                            o = flat[:, base[t] + n0:base[t] + n1]
                            m = pe.matmul(o, stationary(1, b, t), w_hi[:, slot, b * width + n0:b * width + n1], start=False, stop=last)
                        if last and t == 0:
                            m.then_inc(first_done, 1)
                m.then_inc(w_used, 1)

            LOW, HIGH = (0, 1024), (2048, 3072)

            def stream(c, tiles, k0, base, start, stop, free=None):
                pe.wait_ge(lo_done, c + 1)
                products(split_slot(c), chunk(c)[1], lambda part, b, t: tiles(part, k0 + b, t), base, start, stop, free)

            def of_x(part, k, t):
                return xT[:, part, k, P * t:P * t + P]

            def of_c(part, k, t):
                return cT[:, part, k, P * t:P * t + P]

            def of_y(part, k, t):
                return yT[:, k, part, P * t:P * t + P]

            pe.wait_ge(prm_in, 16 * 8)
            pe.wait_ge(consts, 1)
            pe.transpose(bank(7, NPRM), prm[:, :], ident[0:NPRM, 0:NPRM]).then_inc(prm_t, 1)
            for t in range(TT):
                pe.wait_ge(x_in[t], 16)
            for k in range(KT):
                if k == 7:
                    pe.wait_ge(wcols_ok, 1)
                if k >= 8:
                    pe.wait_ge(xt_lo, k - 7)
                for t in range(TT):
                    m = pe.transpose(ps[:, k % 8, P * t:P * t + P], x_sb[:, t, P * k:P * k + P], ident[:, :])
                m.then_inc(xt_t, 1)
            pe.wait_ge(xt_lo, KT)
            for c in range(8):
                stream(c, of_x, 2 * c, LOW, c == 0, c == 7)
            for c in range(8):
                stream(B_IN + c, of_x, 2 * c, HIGH, c == 0, c == 7)

            pe.wait_ge(c_norm, 1)
            for k in range(6):
                if k >= 4:
                    pe.wait_ge(ct_lo, k - 3)
                for t in range(TT):
                    m = pe.transpose(ps[:, k % 4, P * t:P * t + P], c_sb[:, t, P * k:P * k + P], ident[:, :])
                m.then_inc(ct_t, 1)

            def heads(c, banks, nheads, k0, nk):
                pe.wait_ge(lo_done, c + 1)
                width = chunk(c)[1][1]
                s = split_slot(c)
                for h in range(nheads):
                    o = ps[:, banks[h // 2], T * (h % 2):T * (h % 2) + T]
                    for b in range(nk):
                        w = slice(b * width + P * h, b * width + P * h + P)
                        pe.matmul(o, w_hi[:, s, w], cT[:, 0, k0 + b, :], start=b == 0, stop=False)
                        pe.matmul(o, w_hi[:, s, w], cT[:, 1, k0 + b, :], start=False, stop=False)
                        m = pe.matmul(o, w_lo[:, s, w], cT[:, 0, k0 + b, :], start=False, stop=b == nk - 1)
                m.then_inc(w_used, 1)

            pe.wait_ge(ct_lo, 6)
            pe.wait_ge(act_free, 4)
            pe.wait_ge(lo_done, UQ_PE + 1)
            for b in range(4):
                for t in range(TT):
                    o = bank(6 + t)
                    w = slice(512 * b, 512 * b + 512)
                    s = split_slot(UQ_PE)
                    pe.matmul(o, of_c(0, b, t), w_hi[:, s, w], start=b == 0, stop=False)
                    pe.matmul(o, of_c(0, b, t), w_lo[:, s, w], start=False, stop=False)
                    m = pe.matmul(o, of_c(1, b, t), w_hi[:, s, w], start=False, stop=b == 3)
            m.then_inc(w_used, 1)
            heads(UQ_NOPE, (4, 5), 4, 0, 4)
            heads(UQ_NOPE + 1, (2, 3), 4, 0, 4)
            pe.wait_ge(qpe_out, 2)
            heads(UKV_K, (0, 1, 6, 7), 8, 4, 2)
            pe.wait_ge(qn_out, 4)
            pe.wait_ge(lo_done, UKV_V + 1)
            s = split_slot(UKV_V)
            for b in range(2):
                for t, col in ((0, 2048), (1, 1024)):
                    for n in range(2):
                        o = flat[:, col + 512 * n:col + 512 * n + 512]
                        w = slice(1024 * b + 512 * n, 1024 * b + 512 * n + 512)
                        pe.matmul(o, of_c(0, 4 + b, t), w_hi[:, s, w], start=b == 0, stop=False)
                        pe.matmul(o, of_c(0, 4 + b, t), w_lo[:, s, w], start=False, stop=False)
                        m = pe.matmul(o, of_c(1, 4 + b, t), w_hi[:, s, w], start=False, stop=b == 1)
            m.then_inc(w_used, 1)

            pe.wait_ge(kn_out, 4)
            for j, b in enumerate((0, 1, 6, 7)):
                pe.wait_ge(kd_ok, 2 * j + 2)
                for n in range(2):
                    for t in range(TT):
                        o = T * n + P * t
                        m = pe.transpose(ps[:, b, o:o + P], kd[:, 2 * j + n, t, :, :].rearrange("p c d -> p (c d)"), ident[:, :])
                m.then_inc(kv_t, 1)
            pe.wait_ge(v_out, 2)
            pe.wait_ge(qpr_ok, 2)
            pe.wait_ge(kpe_ok, 2)
            for c in range(4):
                for t in range(TT):
                    o = T * (c % 2) + P * t
                    m = pe.transpose(ps[:, 4 + c // 2, o:o + P], qpr[:, t, P * c:P * c + P], ident[:, :])
                if c % 2:
                    m.then_inc(qp_t, 1)
            for t in range(TT):
                m = pe.transpose(ps[:, 2, P * t:P * t + P], kpe[:, t, :], ident[:, :])
            m.then_inc(qp_t, 1)

            SPANS = ((0, 0, P), (P, P, SEEN))

            def slot(i, lo, hi):
                if lo <= i < hi and i in SOFT:
                    n = SOFT[i]
                    kind, u, h, branch = STEPS[i]
                    if n >= 2:
                        pe.wait_ge(score_m, n - 1)
                    p0 = 64 * (h % 2)
                    for q, c0, c1 in SPANS:
                        o = ps[:, 4 + n % 2, c0:c1]
                        if kind == "mla":
                            pe.matmul(o, qnT[:, h, q:q + P], knT[:, h, 0:c1 - c0], start=True, stop=False)
                            m = pe.matmul(o, qpT[p0:p0 + 64, h // 2, q:q + P], kpT[p0:p0 + 64, 0:c1 - c0], start=False, stop=True)
                        else:
                            m = pe.matmul(o, qT[p0:p0 + 64, h // 2, q:q + P], kT[p0:p0 + 64, 2 * branch + h // 8, 0:c1 - c0],
                                          start=True, stop=True)
                    m.then_inc(score_t, 1)
                j = i - 2
                if lo <= j < hi:
                    if j >= 1:
                        pe.wait_ge(pt_out, j)
                    kind, u, h, branch = STEPS[j]
                    if kind == "cmp":
                        pe.wait_ge(pc_ok, 1)
                        for e in range(2):
                            for t in range(TT):
                                o = T * e + P * t
                                m = pe.transpose(ps[0:NC, 6, o:o + P], pc[:, h + e, t, :], ident[:, :])
                    else:
                        n = SOFT[j]
                        pe.wait_ge(prob_ok, n + 1)
                        for c in range(3):
                            m = pe.transpose(ps[:, 6, P * c:P * c + P], prob[:, n % 3, P * c:P * c + P], ident[:, :])
                    m.then_inc(pt_t, 1)
                j = i - 3
                if lo <= j < hi:
                    kind, u, h, branch = STEPS[j]
                    pe.wait_ge(pt_out, j + 1)
                    if u and (kind == "mla" or (branch == 0 and h % 2 == 0)):
                        pe.wait_ge(y_lo, u)
                        if u == MH:
                            pe.wait_ge(ysum_ok, 1)
                    p = probT[:, j % 2, :]
                    if kind == "cmp":
                        for e in range(2):
                            m = pe.matmul(ps[64 * e:64 * e + 64, 7, 0:T], vcmp[:, h // 8, :], p[0:NC, T * e:T * e + T], start=False, stop=True)
                    else:
                        if kind == "mla":
                            o, first, last = ps[:, 7, 0:T], True, True
                            v = [v_sb[:, t, MV * h:MV * h + MV] for t in range(TT)]
                        else:
                            e = h % 2
                            o, first, last = ps[64 * e:64 * e + 64, 7, 0:T], branch == 0, False
                            off = 256 * (1 + branch) + 128 * (h // 8) + DK
                            v = [kv_sb[:, t, off:off + DK] for t in range(TT)]
                        pe.matmul(o, v[0], p[:, 0:T], start=first, stop=False)
                        m = pe.matmul(o[:, P:T], v[1], p[:, T:SEEN], start=False, stop=last)
                    m.then_inc(o_t, 1)

            def sum_over_features(part):
                pe.wait_ge(sq_sum, MH * (part + 1))
                pe.wait_ge(y_lo, MH * (part + 1))
                for t in range(TT):
                    m = pe.matmul(ps[:, 7, 256 + t:257 + t], sqacc[:, part, P * t:P * t + P], ones[:, :], start=True, stop=True)
                m.then_inc(ysum_t, 1)

            pe.wait_ge(kv_out, 4)
            pe.wait_ge(qp_out, 3)
            for kind, i in MLA_PLAN:
                if kind == "w":
                    stream(i, of_x, 2 * (i - A_IN), LOW, i == A_IN, i == CMP - 1)
                elif kind == "s":
                    slot(i, 0, NMLA)
            sum_over_features(0)

            pe.wait_ge(act_free, 6)
            for j in range(4):
                for c in (2 * j, 2 * j + 1):
                    for t in range(TT):
                        o = T * (c % 2) + P * t
                        m = pe.transpose(ps[:, j, o:o + P], q_sb[:, t, P * c:P * c + P], ident[:, :])
                m.then_inc(q_t, 1)
            pe.wait_ge(q_out, 4)
            pe.wait_ge(blk_ok, 1)
            for kind, i in NSA_PLAN:
                if kind == "w" and i < WO_M:
                    pe.wait_ge(lo_done, i + 1)
                    y, half, s = (i - CMP) // 2, (i - CMP) % 2, split_slot(i)
                    o = ps[0:2 * NC, y, 0:CMP_HID]
                    for b in range(8):
                        k = 8 * half + b
                        w = slice(CMP_HID * b, CMP_HID * b + CMP_HID)
                        pe.matmul(o, blk[:, 0, y, k, :], w_hi[:, s, w], start=k == 0, stop=False)
                        pe.matmul(o, blk[:, 0, y, k, :], w_lo[:, s, w], start=False, stop=False)
                        m = pe.matmul(o, blk[:, 1, y, k, :], w_hi[:, s, w], start=False, stop=k == 15)
                    m.then_inc(w_used, 1)
                elif kind == "w":
                    n, j = (i - WO_M) // 4, (i - WO_M) % 4

                    def free(t, n=n):
                        if n:
                            pe.wait_ge(dve_free, t + 1)
                        else:
                            pe.wait_ge(cs_sub, 1)
                    stream(i, of_y, 2 * j, LOW, j == 0, j == 3, free)
                elif kind == "s":
                    slot(i, NMLA, len(STEPS))
                elif i == "turn":
                    pe.wait_ge(g_ok, 1)
                    for y in range(2):
                        for k in range(2):
                            o = 2 * NC * (2 * y + k)
                            m = pe.transpose(ps[:, 2, o:o + 2 * NC], h1a[:, y, P * k:P * k + P], ident[0:2 * NC, 0:2 * NC])
                    m.then_inc(g_t, 1)
                elif i == "project":
                    pe.wait_ge(g_turned, 1)
                    pe.wait_ge(w2_in, 48)
                    for k in range(2):
                        pe.matmul(ps[:, 3, 0:2 * NC], w2k[:, k, :, :].rearrange("p c d -> p (c d)"), h1T[:, k, :],
                                  start=k == 0, stop=k == 1)
                    for g in range(NG):
                        for k in range(2):
                            m = pe.matmul(ps[0:NC, 3, 64 + DK * g:64 + DK * g + DK], h1T[:, 2 + k, NC * g:NC * g + NC], w2v[:, k, :],
                                          start=k == 0, stop=k == 1)
                    m.then_inc(k_t, 1)
                elif i == "scores":
                    pe.wait_ge(k_ok, 1)
                    for h in range(NH):
                        p0 = 64 * (h % 2)
                        for t in range(TT):
                            o = NC * (TT * (h // 2) + t)
                            m = pe.matmul(ps[:, 2 + h % 2, o:o + NC], qT[p0:p0 + 64, h // 2, P * t:P * t + P],
                                          kcmpT[p0:p0 + 64, NC * (h // 8):NC * (h // 8) + NC], start=True, stop=True)
                    m.then_inc(cs_t, 1)
            sum_over_features(1)

            def turn_h(k):
                if k >= 4:
                    pe.wait_ge(ht_lo, k - 3)
                for t in range(TT):
                    m = pe.transpose(ps[:, 4 + k % 4, P * t:P * t + P], h_sb[:, t, P * k:P * k + P], ident[:, :])
                m.then_inc(ht_t, 1)

            pe.wait_ge(y_lo, 16)
            for c in range(WO_N, MLP0):
                n, j = (c - WO_N) // 4, (c - WO_N) % 4
                stream(c, of_y, 8 + 2 * j, LOW, j == 0, j == 3, lambda t: pe.wait_ge(dve_free, 2 + 2 * n + t + 1))
                if c >= WO_N + 5:
                    if c == WO_N + 5:
                        pe.wait_ge(dve_free, 6)
                        pe.wait_ge(ysum_ok, 2)
                    for k in TURNS[c - WO_N - 5]:
                        turn_h(k)
            pe.wait_ge(dve_free, 8)
            for k in range(8, KT):
                turn_h(k)

            def stream_loop(j, g, tiles, k0, base, start, stop, free=None):
                pe.wait_ge(lo_done, LOOP0 - GC + j + 1 + GC * g)
                products(j % SPLIT, (2, 1024), lambda part, b, t: tiles(part, k0 + b, t), base, start, stop, free)

            def of_hidden(part, k, t):
                return hidT[:, part, k, P * t:P * t + P]

            def turn_hidden(squared, added_before):
                pe.wait_ge(hid_ok, squared)
                if added_before is not None:
                    pe.wait_ge(dve_free, added_before)
                for q in range(4):
                    for c in (2 * q, 2 * q + 1):
                        for t in range(TT):
                            o = T * (c % 2) + P * t
                            m = pe.transpose(ps[:, 4 + q, o:o + P], hid[:, t, P * c:P * c + P], ident[:, :])
                    m.then_inc(hd_t, 1)

            for j in range(8):
                pe.wait_ge(ht_lo, 2 * j + 2)
                stream(MLP0 + j, of_x, 2 * j, LOW, j == 0, j == 7)
            pe.wait_ge(ht_lo, KT)
            turn_hidden(2, None)

            def free_up(g):
                def free(t):
                    pe.wait_ge(relu_ok, 2 * g)
                    pe.wait_ge(dve_free, 3 + t + 4 * g)
                return free

            with pe.Fori(1, G) as g:
                for j in range(8):
                    stream_loop(j, g, of_x, 2 * j, LOW, j == 0, j == 7, free_up(g))
                for j in range(8, 12):
                    pe.wait_ge(hd_lo, 4 * g - 4 + j - 7)
                    if j == 8:
                        pe.wait_ge(hd_lo, 4 * g)
                    stream_loop(j, g, of_hidden, 2 * (j - 8), HIGH, j == 8, j == 11)
                for j in range(12, 16):
                    stream_loop(j, g, of_hidden, 2 * (j - 12), LOW, j == 12, j == 15, lambda t: pe.wait_ge(relu_ok, 2 * g + t + 1))
                turn_hidden(2 * g + 2, 4 * g + 6)
            pe.wait_ge(hd_lo, 4 * G)
            for j in range(4):
                stream_loop(j, G, of_hidden, 2 * j, HIGH, j == 0, j == 3)
            for j in range(4, 8):
                stream_loop(j, G, of_hidden, 2 * (j - 4), LOW, j == 4, j == 7, lambda t: pe.wait_ge(dve_free, 3 + t + 4 * G))


_INS = ["x", "positions", "attn_norm_w", "w_in", "mla_q_norm_w", "mla_w_uq", "mla_kv_norm_w", "mla_w_ukv",
        "cmp_pos_k", "cmp_pos_v", "cmp_w1_k", "cmp_w2_k", "cmp_w1_v", "cmp_w2_v", "mla_out_norm_w",
        "nsa_out_norm_w", "w_o", "mlp_norm_w", "w_up", "w_down", "final_norm_w"]


def kernel(**inputs):
    import concourse.bacc as bacc
    from concourse.bass_utils import run_bass_kernel_spmd

    nc = bacc.Bacc("TRN2", target_bir_lowering=False, num_devices=1)
    freq = (1.0 / (np.float32(10000.0) ** (np.arange(0, ROPE, 2, dtype=np.float32) / np.float32(ROPE)))).astype(np.float32)
    arrays, args = {}, {}
    for name in _INS + ["inv_freq"]:
        v = freq if name == "inv_freq" else np.ascontiguousarray(inputs[name])
        arrays[f"in_{name}"] = v
        args[name] = nc.dram_tensor(f"in_{name}", v.shape, mybir.dt.from_np(v.dtype), kind="ExternalInput").ap()
    out = nc.dram_tensor("out", (1, T, D), F32, kind="ExternalOutput").ap()
    build(nc, args, out)
    result = run_bass_kernel_spmd(nc, [arrays], core_ids=[0])
    return result.results[0]["out"]
```

```python
from contextlib import ExitStack

import numpy as np

import concourse.bass as bass
from concourse import mybir

F32 = mybir.dt.float32
F32R = mybir.dt.float32r
I32 = mybir.dt.int32
ALU = mybir.AluOpType
ACT = mybir.ActivationFunctionType
AX = mybir.AxisListType

P = 128
T, D = 256, 2048
TT = T // P
KT = D // P
EPS = 1e-6
QR, KVR, NOPE, ROPE, MH, MV = 512, 256, 128, 64, 8, 128
NH, NG, DK = 16, 2, 64
CMP_LEN, CMP_STRIDE, CMP_HID = 32, 16, 256
NC = (T - CMP_LEN) // CMP_STRIDE + 1
WINDOW, SEL_LEN, SEL_TOPK = 512, 64, 16
assert T // SEL_LEN <= SEL_TOPK and WINDOW >= T
HID = 4 * D
CW = 832
BW = 816
OFF_Q = CW
OFF_B = CW + NH * DK
MLA_SCALE = float(NOPE + ROPE) ** -0.5
NSA_SCALE = float(DK) ** -0.5
HALF = ROPE // 2
SLOPE = [float(np.float32(2.0 ** (-8.0 / NH)) ** (h + 1)) for h in range(NH)]
BIG = 1e30
SEEN = 3 * P
TWO_PI = 2.0 * np.pi
C1 = 6.28125
C2 = float(np.float32(int((TWO_PI - C1) * 2 ** 20) / 2 ** 20))
C3 = float(TWO_PI - C1 - C2)
PI_IN = float(np.nextafter(np.float32(np.pi), np.float32(0)))
MAGIC = float(1.5 * 2 ** 23)

PRM = dict(attn=0, mlp=16, c=32, y=38, posk=54, posv=70)
NPRM = 86

C_IN, B_IN, UQ_PE, UQ_NOPE, UKV_K, UKV_V, CMP = 0, 8, 16, 17, 19, 20, 21
A_IN, WO_M, WO_N, MLP0 = 25, 33, 41, 49
RAW, SPLIT = 4, 2
G = 8
GC = 16


def raw_slot(c):
    return (c + 3) % RAW


def split_slot(c):
    return (c + 1) % SPLIT


STEPS = [("mla", h, h, 0) for h in range(MH)]
for _u in range(MH, 16):
    _a = 2 * (_u - MH)
    STEPS += [("slc", _u, _a, 0), ("win", _u, _a, 1), ("slc", _u, _a + 1, 0), ("win", _u, _a + 1, 1), ("cmp", _u, _a, 2)]
NMLA = MH
LASTSTEP = {s[1]: i for i, s in enumerate(STEPS)}
SOFT = {i: n for n, i in enumerate([i for i, s in enumerate(STEPS) if s[0] != "cmp"])}


PLAN = [("k", "keys"), ("w", CMP), ("split", CMP + 1), ("w", CMP + 1), ("split", CMP + 2), ("k", "rotary"),
        ("w", CMP + 2), ("split", CMP + 3), ("w", CMP + 3), ("split", CMP + 4), ("k", "gelu")]
for _i in range(8):
    PLAN += [("w", A_IN + _i), ("split", A_IN + _i + 1)]
    PLAN += {0: [("k", "turn")], 1: [("k", "project")], 7: [("k", "queries")]}.get(_i, [])
    PLAN += [("s", _i)]
PLAN += [("k", "turn_q"), ("s", NMLA), ("k", "scores")]
_s = NMLA + 1
for _c in range(WO_M, WO_N + 4):
    for _n in range(4):
        PLAN += [("q", (_c, _n))]
        if _n == 0:
            PLAN += [("split", _c + 1)]
        if _s < len(STEPS) + 3:
            PLAN += [("s", _s)]
            if _s == NMLA + 1:
                PLAN += [("k", "soft")]
            if _s == LASTSTEP[MH] + 4:
                PLAN += [("k", "norm")]
            if _s == len(STEPS) + 2:
                PLAN += [("k", "norm_n")]
            _s += 1
assert _s == len(STEPS) + 3


TURNS = ((0, 1, 2), (3, 4, 5), (6, 7))


def build(nc, a, out):
    with ExitStack() as ctx:
        def seq(base, *specs):
            made = []
            for name, shape, dt in specs:
                made.append(nc.alloc_sbuf_tensor_at(name, shape, dt, offset=base))
                base += (4 * int(np.prod(shape[1:])) + 31) // 32 * 32
            return (*made, base)

        X_AT = (nc.sbuf_base + 31) // 32 * 32
        xT, Y_AT = seq(X_AT, ("xT", [P, 2, KT, T], F32R))
        yT, W_AT = seq(Y_AT, ("yT", [P, 16, 2, T], F32R))
        w_hi, w_lo, raw, F_AT = seq(W_AT, ("w_hi", [P, SPLIT, 2048], F32R), ("w_lo", [P, SPLIT, 2048], F32R),
                                    ("raw", [P, RAW, 2048], F32))
        YN_AT = Y_AT + 4 * 8 * 2 * T
        cT, _ = seq(YN_AT, ("cT", [P, 2, 6, T], F32R))
        blk, h1c, h1T, e = seq(YN_AT, ("blk", [P, 2, 2, 16, 2 * NC], F32R), ("h1c", [2 * NC, 2, CMP_HID], F32),
                               ("h1T", [P, 4, 2 * NC], F32))
        KC_AT = YN_AT + 4 * 2 * 6 * T
        assert e <= KC_AT
        kcT, e = seq(KC_AT, ("kcT", [P, 4, T], F32))
        assert e <= W_AT
        h1a, h1b, e = seq(KC_AT, ("h1a", [2 * NC, 2, CMP_HID], F32), ("h1b", [2 * NC, 2, CMP_HID], F32))
        assert e <= W_AT
        sink, kd, e = seq(Y_AT, ("sink", [P, D], F32), ("kd", [P, 8, TT, 2, DK], F32))
        assert e <= YN_AT
        hidT, _ = seq(Y_AT, ("hidT", [P, 2, 8, T], F32R))
        q_sb, qT, bias_h, cbias, pc, e = seq(
            X_AT, ("q_sb", [P, TT, NH * DK], F32), ("qT", [P, 8, T], F32), ("bias_h", [P, 2, SEEN], F32),
            ("cbias", [P, NH // 2, TT, 2, NC], F32), ("pc", [P, NH // 2, TT, 2, NC], F32))
        assert e <= Y_AT
        ident, wcols, ones, r1, r1q, rc, rm, rn, ssq, root_w, A_AT = seq(
            F_AT, ("ident", [P, P], F32), ("wcols", [P, NPRM], F32), ("ones", [P, 1], F32), ("r1", [P, TT], F32),
            ("r1q", [P, TT], F32), ("rc", [P, 4], F32), ("rm", [P, TT], F32), ("rn", [P, TT], F32),
            ("ssq", [P, 16], F32), ("root_w", [P, 4], F32))
        (posf, posi, den, scl, nmax, cden, cmx, cgate, valid, invf, gates, dist, mask, cdist, cdi, kv_sb, kT, prob, probT,
         sq, sqacc, w2k, w2v, kcmp, vcmp, prm, M_AT) = seq(
            A_AT, ("posf", [P, TT], F32), ("posi", [P, TT], I32), ("den", [P, 40, 2], F32), ("scl", [P, 40, 2], F32),
            ("nmax", [P, 40, 2], F32), ("cden", [P, NH * TT], F32), ("cmx", [P, NH * TT], F32),
            ("cgate", [P, NH // 2, TT, 2], F32), ("valid", [P, TT], F32), ("invf", [P, HALF], F32),
            ("gates", [P, TT, 3 * NH], F32), ("dist", [P, SEEN], F32), ("mask", [P, SEEN], F32),
            ("cdist", [P, TT, NC], F32), ("cdi", [P, TT, NC], I32), ("kv_sb", [P, TT, BW], F32), ("kT", [P, 4, T], F32),
            ("prob", [P, 3, SEEN], F32), ("probT", [P, 2, 512], F32), ("sq", [P, 2, T], F32),
            ("sqacc", [P, 2, T], F32), ("w2k", [P, 2, 2, DK], F32), ("w2v", [P, 2, DK], F32),
            ("kcmp", [P, NG, 2, NC], F32), ("vcmp", [NC, NG, DK], F32), ("prm", [NPRM, P], F32))
        cs, angs, angk, L_AT = seq(M_AT, ("cs", [P, 2, TT * HALF], F32), ("angs", [P, 2, TT * HALF], F32),
                                   ("angk", [P, 2, TT * HALF], F32))
        c_sb, qpr, v_sb, qnT, knT, qpT, kpT, kpe, rtmp, e = seq(
            L_AT, ("c_sb", [P, TT, CW], F32), ("qpr", [P, TT, MH * ROPE], F32), ("v_sb", [P, TT, MH * MV], F32),
            ("qnT", [P, MH, T], F32), ("knT", [P, MH, T], F32), ("qpT", [P, 4, T], F32), ("kpT", [P, T], F32),
            ("kpe", [P, TT, 2 * ROPE], F32), ("rtmp", [P, 2, MH * HALF], F32))
        blkf, e = seq(e, ("blkf", [P, 2, 16, 2 * NC], F32))
        assert e <= nc.sbuf_usable_end, (e, nc.sbuf_usable_end)
        di, _ = seq(L_AT, ("di", [P, SEEN], I32))
        qpe, _ = seq(L_AT, ("qpe", [P, TT, MH * ROPE], F32))
        x_sb, _ = seq(L_AT + 4 * 1664, ("x_sb", [P, TT, D], F32))
        h_sb, H_END = seq(L_AT, ("h_sb", [P, TT, D], F32))
        sink2, e = seq(H_END, ("sink2", [P, D], F32))
        assert e <= nc.sbuf_usable_end
        acc, hid, e = seq(A_AT, ("acc", [P, TT, D], F32), ("hid", [P, TT, 1024], F32))
        assert e <= M_AT, (e, M_AT)
        fw, _ = seq(X_AT, ("fw", [P, D], F32))

        ps = ctx.enter_context(nc.psum_tensor("ps", [P, 8, 512], F32))
        flat = ps[:, :, :].rearrange("p b n -> p (b n)")

        def bank(b, n=512, p0=0, p1=P):
            return ps[p0:p1, b, 0:n]

        def pairs(ap):
            return ap.rearrange("p (k t) -> p k t", k=2)

        def sems(*names):
            return [ctx.enter_context(nc.semaphore(n)) for n in names]

        x_in = sems("x_in0", "x_in1")
        raw_in = sems(*[f"raw_in{n}" for n in range(RAW)])
        prm_in, cst_in, w2_in, h_in, fw_in, stored = sems("prm_in", "cst_in", "w2_in", "h_in", "fw_in", "stored")
        hi_done, lo_done, w_used = sems("hi_done", "lo_done", "w_used")
        first_done, = sems("first_done")
        act_free, dve_free = sems("act_free", "dve_free")
        pool_c, dve_c = sems("pool_c", "dve_c")
        consts, tables, prm_t, wcols_ok = sems("consts", "tables", "prm_t", "wcols_ok")
        xt_t, xt_hi, xt_lo, ct_t, ct_hi, ct_lo = sems("xt_t", "xt_hi", "xt_lo", "ct_t", "ct_hi", "ct_lo")
        ssq_ok, rs_ok, ang_ok, sin_ok = sems("ssq_ok", "rs_ok", "ang_ok", "sin_ok")
        c_norm, kpe_ok, qpe_out, qpr_ok, qn_out, kn_out, v_out = sems(
            "c_norm", "kpe_ok", "qpe_out", "qpr_ok", "qn_out", "kn_out", "v_out")
        kv_t, kv_out, qp_t, qp_out, blk_f, blk_hi, blk_ok = sems(
            "kv_t", "kv_out", "qp_t", "qp_out", "blk_f", "blk_hi", "blk_ok")
        kd_ok, gexp, gate_ok, q_in, q_t, q_out = sems("kd_ok", "gexp", "gate_ok", "q_in", "q_t", "q_out")
        g_sq, g_in, g_th, g_ok, g_t, g_turned, k_t, k_ok = sems(
            "g_sq", "g_in", "g_th", "g_ok", "g_t", "g_turned", "k_t", "k_ok")
        cs_t, cs_sub, cs_exp, pc_ok, cb_ok = sems("cs_t", "cs_sub", "cs_exp", "pc_ok", "cb_ok")
        bias_ok, score_t, score_m, exp_ok, prob_ok, pt_t, pt_out, o_t = sems(
            "bias_ok", "score_t", "score_m", "exp_ok", "prob_ok", "pt_t", "pt_out", "o_t")
        y_sq, y_hi, y_lo, sq_sum, ysum_t, ysum_ok, yr_ok, guessed = sems(
            "y_sq", "y_hi", "y_lo", "sq_sum", "ysum_t", "ysum_ok", "yr_ok", "guessed")
        relu_ok, hid_ok, acc0, added, normed, fsq = sems("relu_ok", "hid_ok", "acc0", "added", "normed", "fsq")
        ht_t, ht_hi, ht_lo, hd_t, hd_hi, hd_lo = sems("ht_t", "ht_hi", "ht_lo", "hd_t", "hd_hi", "hd_lo")

        win = a["w_in"][0].rearrange("(k p) n -> p k n", p=P)
        uq = a["mla_w_uq"][0].rearrange("(k p) (h e) -> p k h e", p=P, e=NOPE + ROPE)
        ukv = a["mla_w_ukv"][0].rearrange("(k p) (h e) -> p k h e", p=P, e=NOPE + MV)
        wo = a["w_o"][0].rearrange("(k p) n -> p k n", p=P)
        up = a["w_up"][0].rearrange("(k p) (g n) -> p k g n", p=P, g=G)
        dn = a["w_down"][0].rearrange("(g k p) n -> p g k n", p=P, g=G)
        cw1 = [a[n][0].rearrange("(k p) n -> p k n", p=P) for n in ("cmp_w1_k", "cmp_w1_v")]

        def chunk(c):
            if c < B_IN:
                return [win[:, 2 * c:2 * c + 2, 0:CW]], (2, CW)
            if c < UQ_PE:
                k = 2 * (c - B_IN)
                return [win[:, k:k + 2, OFF_B:OFF_B + BW]], (2, BW)
            if c == UQ_PE:
                return [uq[:, k, :, NOPE:] for k in range(4)], (4, 512)
            if c < UKV_K:
                h = 4 * (c - UQ_NOPE)
                return [uq[:, k, h:h + 4, 0:NOPE] for k in range(4)], (4, 512)
            if c < CMP:
                o = 0 if c == UKV_K else NOPE
                return [ukv[:, k, :, o:o + NOPE] for k in range(2)], (2, 1024)
            if c < A_IN:
                j = c - CMP
                return [cw1[j // 2][:, 8 * (j % 2):8 * (j % 2) + 8, :]], (8, CMP_HID)
            if c < WO_M:
                k = 2 * (c - A_IN)
                return [win[:, k:k + 2, OFF_Q:OFF_B]], (2, 1024)
            if c < MLP0:
                part, n, j = (c - WO_M) // 8, (c - WO_M) // 4 % 2, (c - WO_M) % 4
                k = 8 * part + 2 * j
                return [wo[:, k:k + 2, 1024 * n:1024 * n + 1024]], (2, 1024)
            j = c - MLP0
            return [up[:, 2 * j:2 * j + 2, 0, :]], (2, 1024)

        LOOP0 = MLP0 + 8
        assert raw_slot(LOOP0) == 0 and split_slot(LOOP0) == 0

        def loads(c):
            return sum(len(chunk(k)[0]) for k in range(c % RAW, c + 1, RAW))

        LOADS0 = [loads(LOOP0 - RAW + s) for s in range(RAW)]

        x_rows = a["x"][0].rearrange("(t p) d -> t p d", p=P)
        o_rows = out[0].rearrange("(t p) d -> t p d", p=P)
        block = ctx.enter_context(nc.Block())

        TABLE = [(a[name][0].rearrange("(r p) -> r p", p=P), row, n) for name, row, n in (
            ("attn_norm_w", 0, 16), ("mlp_norm_w", 16, 16), ("mla_q_norm_w", 32, 4), ("mla_kv_norm_w", 36, 2),
            ("mla_out_norm_w", 38, 8), ("nsa_out_norm_w", 46, 8))]
        TABLE += [(a[name][0].rearrange("(r two) d -> r (two d)", two=2), PRM[at], 16)
                  for name, at in (("cmp_pos_k", "posk"), ("cmp_pos_v", "posv"))]

        def load_table(queue, rows):
            for src, row, n in rows:
                queue.dma_start(prm[row:row + n, :], src).then_inc(prm_in, 16)

        @block.sync
        def _(sp):
            load_table(sp, TABLE[0:4])
            sp.dma_start(x_sb[:, 0, 0:D // 2], x_rows[0][:, 0:D // 2]).then_inc(x_in[0], 16)
            sp.dma_start(x_sb[:, 1, 0:D // 2], x_rows[1][:, 0:D // 2]).then_inc(x_in[0], 16)
            for c in range(LOOP0):
                if c >= RAW:
                    sp.wait_ge(lo_done, c - RAW + 1)
                src, (b, w) = chunk(c)
                dst = raw[:, raw_slot(c), 0:b * w].rearrange("p (b w) -> p b w", b=b)
                if len(src) == 1:
                    sp.dma_start(dst, src[0]).then_inc(raw_in[raw_slot(c)], 16)
                else:
                    for k, piece in enumerate(src):
                        sp.dma_start(dst[:, k, :].rearrange("p (h e) -> p h e", h=piece.shape[1]), piece)\
                            .then_inc(raw_in[raw_slot(c)], 16)
                if c == WO_M + 4:
                    sp.wait_ge(y_lo, MH)
                    for t in range(TT):
                        sp.dma_start(h_sb[:, t, :], x_rows[t]).then_inc(h_in, 16)
            with sp.Fori(1, G) as g:
                for j in range(GC):
                    sp.wait_ge(lo_done, LOOP0 - GC + j - RAW + 1 + GC * g)
                    dst = raw[:, j % RAW, :].rearrange("p (a n) -> p a n", a=2)
                    if j < 8:
                        src = up[:, 2 * j:2 * j + 2, bass.ds(g, 1), :].rearrange("p a g n -> p a (g n)")
                    else:
                        k, n = 2 * (j % 4), (j - 8) // 4
                        src = dn[:, bass.ds(g - 1, 1), k:k + 2, 1024 * n:1024 * n + 1024].rearrange("p g a n -> p (g a) n")
                    sp.dma_start(dst, src).then_inc(raw_in[j % RAW], 16)
            for j in range(8):
                k, n = 2 * (j % 4), j // 4
                sp.wait_ge(lo_done, LOOP0 + GC * (G - 1) + j - RAW + 1)
                sp.dma_start(raw[:, j % RAW, :].rearrange("p (a n) -> p a n", a=2),
                             dn[:, G - 1, k:k + 2, 1024 * n:1024 * n + 1024]).then_inc(raw_in[j % RAW], 16)
            sp.wait_ge(w_used, LOOP0 + GC * (G - 1))
            sp.dma_start(fw[:, :], a["final_norm_w"].rearrange("(o d) -> o d", o=1).broadcast_to((P, D))).then_inc(fw_in, 16)
            for t in range(TT):
                sp.wait_ge(normed, t + 1)
                sp.dma_start(o_rows[t], h_sb[:, t, :]).then_inc(stored, 16)
            sp.wait_ge(stored, 16 * TT)

        @block.gpsimd
        def _(pool):
            chain = [0]

            def link(ins):
                chain[0] += 1
                ins.then_inc(pool_c, 1)
                pool.wait_ge(pool_c, chain[0])

            link(pool.memset(ident[:, :], 0.0))
            link(pool.affine_select(out=ident[:, :], in_=ident[:, :], compare_op=ALU.not_equal, fill=1.0, base=0,
                                    pattern=[[-1, P]], channel_multiplier=1))
            pool.memset(ones[:, :], 1.0).then_inc(consts, 1)
            link(pool.memset(kcmp[:, :, :, :], 0.0))
            pool.iota(di[:, 0:P], [[-1, P]], base=0, channel_multiplier=1)
            link(pool.iota(di[:, P:SEEN], [[-1, T]], base=P, channel_multiplier=1))
            link(pool.iota(cdi[:, :, :], [[P, TT], [-CMP_STRIDE, NC]], base=1 - CMP_LEN, channel_multiplier=1))
            link(pool.tensor_copy(dist[:, :], di[:, :]))
            link(pool.tensor_scalar(mask[:, :], dist[:, :], 0.0, BIG, ALU.is_lt, ALU.mult))
            link(pool.tensor_tensor(dist[:, :], dist[:, :], mask[:, :], ALU.add))
            link(pool.tensor_copy(cdist[:, :, :], cdi[:, :, :]))
            link(pool.tensor_scalar(valid[:, :], cdist[:, :, 0], 0.0, None, ALU.is_ge))
            cm = cden[:, 0:TT * NC].rearrange("p (t n) -> p t n", t=TT)
            link(pool.tensor_scalar(cm, cdist[:, :, :], 0.0, BIG, ALU.is_lt, ALU.mult))
            pool.tensor_tensor(cdist[:, :, :], cdist[:, :, :], cm, ALU.add).then_inc(tables, 1)
            pool.wait_ge(tables, 1)

            def improve(y, square, w):
                for _ in range(3):
                    link(pool.tensor_tensor(w, y, y, ALU.mult))
                    link(pool.tensor_tensor(w, w, square, ALU.mult))
                    link(pool.tensor_scalar(w, w, -0.5, 1.5, ALU.mult, ALU.add))
                    link(pool.tensor_tensor(y, y, w, ALU.mult))

            pool.wait_ge(guessed, 1)
            improve(r1[:, :], ssq[:, 0:2], root_w[:, 0:2])
            pool.tensor_scalar(r1q[:, :], r1[:, :], -NSA_SCALE, None, ALU.mult).then_inc(rs_ok, 1)
            pool.wait_ge(guessed, 2)
            improve(rc[:, :], ssq[:, 2:6], root_w[:, :])
            pool.tensor_copy(root_w[:, :], rc[:, :]).then_inc(rs_ok, 1)

            def rotate(src, dst, heads, t):
                x = src.rearrange("p (h c e) -> p h c e", h=heads, c=2)
                y = dst.rearrange("p (h c e) -> p h c e", h=heads, c=2)
                sin, cos = [cs[:, i, t * HALF:(t + 1) * HALF].unsqueeze(1).broadcast_to((P, heads, HALF)) for i in range(2)]
                u, v = [rtmp[:, i, 0:heads * HALF].rearrange("p (h e) -> p h e", h=heads) for i in range(2)]
                pool.tensor_tensor(u, x[:, :, 0, :], cos, ALU.mult)
                link(pool.tensor_tensor(v, x[:, :, 1, :], sin, ALU.mult))
                link(pool.tensor_tensor(y[:, :, 0, :], u, v, ALU.subtract))
                pool.tensor_tensor(u, x[:, :, 1, :], cos, ALU.mult)
                link(pool.tensor_tensor(v, x[:, :, 0, :], sin, ALU.mult))
                return pool.tensor_tensor(y[:, :, 1, :], u, v, ALU.add)

            pool.wait_ge(sin_ok, 1)
            pool.wait_ge(act_free, 2)
            for t in range(TT):
                link(rotate(c_sb[:, t, QR + KVR:CW], kpe[:, t, 0:ROPE], 1, t))
                pool.tensor_copy(kpe[:, t, ROPE:2 * ROPE], kpe[:, t, 0:ROPE]).then_inc(kpe_ok, 1)
            pool.wait_ge(act_free, 4)
            for i, off in enumerate((0, 128, 64, 192, 256, 384, 512, 640)):
                src = kv_sb[:, :, off:off + DK].unsqueeze(2).broadcast_to((P, TT, 2, DK))
                pool.tensor_copy(kd[:, i, :, :, :], src).then_inc(kd_ok, 1)
            for t in range(TT):
                pool.wait_ge(qpe_out, t + 1)
                link(rotate(qpe[:, t, :], qpr[:, t, :], MH, t))
                pool.tensor_copy(scl[:, 0, :], ones[:, 0:1].broadcast_to((P, 2))).then_inc(qpr_ok, 1)

            def sum_squares(u):
                part = u // MH
                s = sqacc[:, part, :]
                pool.wait_ge(y_sq, u + 1)
                if u % MH == 0:
                    pool.tensor_copy(s, sq[:, u % 2, :]).then_inc(sq_sum, 1)
                else:
                    pool.wait_ge(sq_sum, u)
                    pool.tensor_tensor(s, s, sq[:, u % 2, :], ALU.add).then_inc(sq_sum, 1)

            def root_of_sums(part, dst):
                pool.wait_ge(guessed, 3 + part)
                improve(dst, ssq[:, 6 + 2 * part:8 + 2 * part], root_w[:, 0:2])
                pool.tensor_copy(root_w[:, 0:2], dst).then_inc(yr_ok, 1)

            made = 0
            for i in range(len(STEPS) + 3):
                if i == NMLA:
                    pool.wait_ge(w_used, WO_M)
                if i < len(STEPS) and STEPS[i][0] == "slc":
                    while made < min(NH, STEPS[i][2] + 2):
                        if made >= 2:
                            pool.wait_ge(score_m, NMLA + 2 * made - 2)
                        pool.tensor_scalar(bias_h[:, made % 2, :], dist[:, :], SLOPE[made], None, ALU.mult).then_inc(bias_ok, 1)
                        made += 1
                if i == NMLA:
                    for h in range(NH):
                        m = pool.tensor_scalar(cbias[:, h // 2, :, h % 2, :], cdist[:, :, :], SLOPE[h], None, ALU.mult)
                    m.then_inc(cb_ok, 1)
                for u in range(16):
                    if LASTSTEP[u] + 3 == i:
                        sum_squares(u)
                if i == LASTSTEP[MH] + 4:
                    root_of_sums(0, rm[:, :])
            root_of_sums(1, rn[:, :])
            pool.wait_ge(y_lo, 16)
            pool.memset(acc[:, :, :], 0.0).then_inc(acc0, 1)

            def square(t, n):
                pool.wait_ge(relu_ok, n)
                pool.tensor_tensor(hid[:, t, :], hid[:, t, :], hid[:, t, :], ALU.mult).then_inc(hid_ok, 1)

            for t in range(TT):
                square(t, t + 1)
            with pool.Fori(1, G) as g:
                for t in range(TT):
                    square(t, 2 * g + t + 1)

        def sums_ready(eng, t, group, last):
            if t == 0:
                eng.wait_ge(first_done, group + 1)
            else:
                eng.wait_ge(w_used, last + 1)

        @block.scalar
        def _(act):
            load_table(act, TABLE[4:8])
            for t in range(TT):
                act.dma_start(x_sb[:, t, D // 2:D], x_rows[t][:, D // 2:D]).then_inc(x_in[1], 16)
            act.dma_start(posi[:, :], a["positions"].rearrange("b (t p) -> p (b t)", p=P),
                          allow_slow_non_contiguous=True).then_inc(cst_in, 16)
            act.dma_start(invf[:, :], a["inv_freq"].rearrange("(o d) -> o d", o=1).broadcast_to((P, HALF))).then_inc(cst_in, 16)
            for twice in range(2):
                act.dma_start(w2k[:, :, twice, :], a["cmp_w2_k"][0].rearrange("(k p) n -> p k n", p=P)).then_inc(w2_in, 16)
            act.dma_start(w2v[:, :, :], a["cmp_w2_v"][0].rearrange("(k p) n -> p k n", p=P)).then_inc(w2_in, 16)

            def split_hi(c):
                act.wait_ge(raw_in[raw_slot(c)], 16 * loads(c))
                if c >= SPLIT:
                    act.wait_ge(w_used, c - SPLIT + 1)
                b, w = chunk(c)[1]
                act.activation(w_hi[:, split_slot(c), 0:b * w], raw[:, raw_slot(c), 0:b * w], ACT.Copy).then_inc(hi_done, 1)

            def split_hi_loop(j, g):
                act.wait_ge(raw_in[j % RAW], 16 * (LOADS0[j % RAW] + j // RAW + 1 - GC // RAW) + 16 * (GC // RAW) * g)
                act.wait_ge(w_used, LOOP0 + j - GC - SPLIT + 1 + GC * g)
                act.activation(w_hi[:, j % SPLIT, :], raw[:, j % RAW, :], ACT.Copy).then_inc(hi_done, 1)

            def x_hi(k):
                act.wait_ge(xt_t, k + 1)
                act.activation(xT[:, 0, k, :], bank(4 + k % 4, T), ACT.Copy, scale=wcols[:, k:k + 1]).then_inc(xt_hi, 1)

            def c_hi(k):
                act.wait_ge(ct_t, k + 1)
                act.activation(cT[:, 0, k, :], bank(k % 4, T), ACT.Copy,
                               scale=wcols[:, PRM["c"] + k:PRM["c"] + k + 1]).then_inc(ct_hi, 1)

            act.wait_ge(wcols_ok, 1)
            for c in range(8):
                if c:
                    split_hi(c)
                x_hi(2 * c)
                x_hi(2 * c + 1)
                if c == 0:
                    split_hi(0)
                if c in (3, 4):
                    t = c - 3
                    act.wait_ge(x_in[0], 16 * TT)
                    act.wait_ge(x_in[1], 16 * TT)
                    if t:
                        act.wait_ge(ssq_ok, t)
                    act.activation(sink[:, :], x_sb[:, t, :], ACT.Square, accum_out=ssq[:, t:t + 1]).then_inc(ssq_ok, 1)
            split_hi(8)
            act.wait_ge(ang_ok, 1)
            act.activation(cs[:, :, :], angs[:, :, :], ACT.Sin).then_inc(sin_ok, 1)
            split_hi(9)
            act.wait_ge(rs_ok, 1)
            for t in range(TT):
                sums_ready(act, t, 0, B_IN - 1)
                act.activation(c_sb[:, t, :], flat[:, 1024 * t:1024 * t + CW], ACT.Copy, scale=r1[:, t:t + 1]).then_inc(act_free, 1)
            n = 2
            for t in range(TT):
                act.wait_ge(act_free, t + 1)
                for i, (lo, hi) in enumerate(((0, QR), (QR, QR + KVR))):
                    act.wait_ge(ssq_ok, n)
                    n += 1
                    act.activation(sink[:, lo:hi], c_sb[:, t, lo:hi], ACT.Square,
                                   accum_out=ssq[:, 2 + 2 * i + t:3 + 2 * i + t]).then_inc(ssq_ok, 1)
            for c in range(10, 18):
                split_hi(c)
                if c == 14:
                    for k in range(4):
                        c_hi(k)
                if c == 15:
                    for k in range(4, 6):
                        c_hi(k)
            for t in range(TT):
                sums_ready(act, t, 1, UQ_PE - 1)
                act.activation(kv_sb[:, t, :], flat[:, 2048 + 1024 * t:2048 + 1024 * t + BW], ACT.Copy,
                               scale=r1[:, t:t + 1]).then_inc(act_free, 1)
            act.wait_ge(act_free, 4)
            act.activation(gates[:, :, :], kv_sb[:, :, 768:BW], ACT.Exp, scale=-1.0).then_inc(gexp, 1)
            split_hi(18)
            act.wait_ge(kpe_ok, 2)
            act.wait_ge(w_used, UQ_PE + 1)
            for t in range(TT):
                act.activation(qpe[:, t, :], bank(t), ACT.Copy, scale=-MLA_SCALE).then_inc(qpe_out, 1)
            split_hi(19)
            for i, b0 in ((0, 2), (1, 4)):
                act.wait_ge(w_used, UQ_NOPE + i + 1)
                for j in range(2):
                    act.activation(qnT[:, 4 * i + 2 * j:4 * i + 2 * j + 2, :], pairs(bank(b0 + j)), ACT.Copy,
                                   scale=-MLA_SCALE).then_inc(qn_out, 1)
                split_hi(20 + i)
            act.wait_ge(blk_f, 1)
            act.wait_ge(w_used, UKV_V + 1)
            act.activation(blk[:, 0, :, :, :].rearrange("p y k n -> p (y k n)"),
                           blkf[:, :, :, :].rearrange("p y k n -> p (y k n)"), ACT.Copy).then_inc(blk_hi, 1)

            def slot(i):
                j = i - 2
                if 0 <= j < len(STEPS):
                    act.wait_ge(pt_t, j + 1)
                    if j >= 2:
                        act.wait_ge(o_t, j - 1)
                    r, w = (NC, 512) if STEPS[j][0] == "cmp" else (P, SEEN)
                    act.activation(probT[0:r, j % 2, 0:w], bank(6, w, 0, r), ACT.Copy).then_inc(pt_out, 1)
                if i in SOFT:
                    n = SOFT[i]
                    act.wait_ge(score_m, n + 1)
                    p = prob[:, n % 3, :]
                    act.activation(p[:, 0:P], p[:, 0:P], ACT.Exp, scale=-1.0, bias=nmax[:, n, 0:1], accum_out=den[:, n, 0:1])
                    act.activation(p[:, P:SEEN], p[:, P:SEEN], ACT.Exp, scale=-1.0, bias=nmax[:, n, 1:2],
                                   accum_out=den[:, n, 1:2]).then_inc(exp_ok, 1)
                j = i - 3
                if j >= 0 and LASTSTEP[STEPS[j][1]] == j:
                    u = STEPS[j][1]
                    act.wait_ge(o_t, j + 1)
                    if u >= 2:
                        act.wait_ge(sq_sum, u - 1)
                    act.activation(sq[:, u % 2, :], bank(7, T), ACT.Square).then_inc(y_sq, 1)
                    act.activation(yT[:, u, 0, :], bank(7, T), ACT.Copy,
                                   scale=wcols[:, PRM["y"] + u:PRM["y"] + u + 1]).then_inc(y_hi, 1)

            for kind, i in PLAN:
                if kind == "split":
                    split_hi(i)
                elif kind == "s":
                    slot(i)
                elif i == "rotary":
                    for j in range(2):
                        act.wait_ge(qp_t, j + 1)
                        act.activation(qpT[:, 2 * j:2 * j + 2, :], pairs(bank(2 + j)), ACT.Copy).then_inc(qp_out, 1)
                    act.wait_ge(qp_t, 3)
                    act.activation(kpT[:, :], bank(6, T), ACT.Copy).then_inc(qp_out, 1)
                elif i == "gelu":
                    act.wait_ge(w_used, CMP + 4)
                    act.activation(h1a[:, :, :], ps[0:2 * NC, 4:6, 0:CMP_HID], ACT.Square).then_inc(g_sq, 1)
                    act.wait_ge(g_in, 1)
                    act.activation(h1c[:, :, :], h1b[:, :, :], ACT.Tanh, scale=float(np.sqrt(2 / np.pi))).then_inc(g_th, 1)
                elif i == "queries":
                    sums_ready(act, 0, 2, WO_M - 1)
                    act.activation(q_sb[:, 0, :], flat[:, 0:1024], ACT.Copy, scale=r1q[:, 0:1]).then_inc(q_in, 1)
                elif i == "turn_q":
                    for j in range(2):
                        act.wait_ge(q_t, j + 1)
                        act.activation(qT[:, 2 * j:2 * j + 2, :], pairs(bank(j)), ACT.Copy).then_inc(q_out, 1)
                elif i == "soft":
                    act.wait_ge(cs_sub, 1)
                    act.activation(pc[:, :, :, :, :].rearrange("p i t e n -> p (i t e n)"),
                                   pc[:, :, :, :, :].rearrange("p i t e n -> p (i t e n)"), ACT.Exp, scale=-1.0).then_inc(cs_exp, 1)

            def turned_hi(k):
                act.wait_ge(ht_t, k + 1)
                act.activation(xT[:, 0, k, :], bank(4 + k % 4, T), ACT.Copy,
                               scale=wcols[:, PRM["mlp"] + k:PRM["mlp"] + k + 1]).then_inc(ht_hi, 1)

            for c in range(WO_N + 4, MLP0):
                split_hi(c + 1)
                if c >= WO_N + 5:
                    for k in TURNS[c - WO_N - 5]:
                        turned_hi(k)
            for k in range(8, KT):
                turned_hi(k)
            for t in range(TT):
                act.wait_ge(ssq_ok, 6 + t)
                act.activation(sink2[:, :], h_sb[:, t, :], ACT.Square, accum_out=ssq[:, 10 + t:11 + t]).then_inc(ssq_ok, 1)

            def relu(group, last):
                for t in range(TT):
                    sums_ready(act, t, group, last)
                    act.activation(hid[:, t, :], flat[:, 1024 * t:1024 * t + 1024], ACT.Relu).then_inc(relu_ok, 1)

            def hidden_hi(done):
                for q in range(4):
                    act.wait_ge(hd_t, done + q + 1)
                    act.activation(hidT[:, 0, 2 * q:2 * q + 2, :], pairs(bank(4 + q)), ACT.Copy).then_inc(hd_hi, 1)

            for c in range(MLP0 + 1, LOOP0):
                split_hi(c)
            split_hi_loop(0, 1)
            relu(7, LOOP0 - 1)
            hidden_hi(0)
            with act.Fori(1, G) as g:
                for j in range(1, GC + 1):
                    split_hi_loop(j, g) if j < GC else split_hi_loop(0, g + 1)
                    if j == 9:
                        relu(8 - 3 + 3 * g, LOOP0 - GC + 7 + GC * g)
                hidden_hi(4 * g)
            for j in range(1, 8):
                split_hi_loop(j, G)
            for t in range(TT):
                act.wait_ge(added, t + 1)
                if t:
                    act.wait_ge(fsq, t)
                act.activation(sink2[:, :], h_sb[:, t, :], ACT.Square, accum_out=ssq[:, 12 + t:13 + t]).then_inc(fsq, 1)

        @block.vector
        def _(dve):
            chain = [0]

            def link(ins):
                chain[0] += 1
                ins.then_inc(dve_c, 1)
                dve.wait_ge(dve_c, chain[0])

            def low(dst, src, high, scale=None):
                if scale is None:
                    return dve.tensor_tensor(dst, src, high.bitcast(F32), ALU.subtract)
                return dve.scalar_tensor_tensor(out=dst, in0=src, scalar=scale, in1=high.bitcast(F32), op0=ALU.mult, op1=ALU.subtract)

            def split_lo(c):
                dve.wait_ge(hi_done, c + 1)
                b, w = chunk(c)[1]
                low(w_lo[:, split_slot(c), 0:b * w], raw[:, raw_slot(c), 0:b * w], w_hi[:, split_slot(c), 0:b * w]).then_inc(lo_done, 1)

            def split_lo_loop(j, g):
                dve.wait_ge(hi_done, LOOP0 - GC + j + 1 + GC * g)
                low(w_lo[:, j % SPLIT, :], raw[:, j % RAW, :], w_hi[:, j % SPLIT, :]).then_inc(lo_done, 1)

            def guess(y, square):
                yi = y.bitcast(I32)
                link(dve.tensor_scalar(yi, square.bitcast(I32), 1, None, ALU.logical_shift_right))
                return dve.tensor_scalar(yi, yi, -1.0, float(0x5F3759DF), ALU.mult, ALU.add)

            def x_lo(k):
                dve.wait_ge(xt_hi, k + 1)
                low(xT[:, 1, k, :], bank(4 + k % 4, T), xT[:, 0, k, :], wcols[:, k:k + 1]).then_inc(xt_lo, 1)

            def c_lo(k):
                dve.wait_ge(ct_hi, k + 1)
                low(cT[:, 1, k, :], bank(k % 4, T), cT[:, 0, k, :], wcols[:, PRM["c"] + k:PRM["c"] + k + 1]).then_inc(ct_lo, 1)

            dve.wait_ge(prm_t, 1)
            dve.tensor_copy(wcols[:, :], bank(7, NPRM)).then_inc(wcols_ok, 1)
            dve.wait_ge(wcols_ok, 1)
            for c in range(8):
                if c:
                    split_lo(c)
                x_lo(2 * c)
                x_lo(2 * c + 1)
                if c == 0:
                    split_lo(0)
                if c == 5:
                    dve.wait_ge(ssq_ok, 2)
                    link(dve.tensor_scalar(ssq[:, 0:2], ssq[:, 0:2], 1.0 / D, EPS, ALU.mult, ALU.add))
                    guess(r1[:, :], ssq[:, 0:2]).then_inc(guessed, 1)
            dve.wait_ge(cst_in, 32)
            link(dve.tensor_copy(posf[:, :], posi[:, :]))
            for v in range(2):
                for t in range(TT):
                    m = dve.tensor_scalar(angs[:, v, t * HALF:(t + 1) * HALF], invf[:, :], posf[:, t:t + 1], None, ALU.mult)
            link(m)
            for v, quarter in ((0, 0.0), (1, 0.25)):
                m = dve.tensor_scalar(angk[:, v, :], angs[:, v, :], 1.0 / TWO_PI, quarter, ALU.mult, ALU.add)
            link(m)
            link(dve.tensor_scalar(angk[:, :, :], angk[:, :, :], MAGIC, None, ALU.add))
            link(dve.tensor_scalar(angk[:, :, :], angk[:, :, :], -MAGIC, None, ALU.add))
            for c in (C1, C2, C3):
                link(dve.scalar_tensor_tensor(out=angs[:, :, :], in0=angk[:, :, :], scalar=-c, in1=angs[:, :, :],
                                              op0=ALU.mult, op1=ALU.add))
            link(dve.tensor_scalar(angs[:, 1, :], angs[:, 1, :], float(np.pi / 2), None, ALU.add))
            dve.tensor_scalar(angs[:, :, :], angs[:, :, :], PI_IN, -PI_IN, ALU.min, ALU.max).then_inc(ang_ok, 1)

            split_lo(8)
            split_lo(9)
            dve.wait_ge(ssq_ok, 6)
            link(dve.tensor_scalar(ssq[:, 2:4], ssq[:, 2:4], 1.0 / QR, EPS, ALU.mult, ALU.add))
            link(dve.tensor_scalar(ssq[:, 4:6], ssq[:, 4:6], 1.0 / KVR, EPS, ALU.mult, ALU.add))
            guess(rc[:, :], ssq[:, 2:6]).then_inc(guessed, 1)
            for c in range(10, 18):
                split_lo(c)
                if c == 11:
                    dve.wait_ge(rs_ok, 2)
                    for t in range(TT):
                        dve.tensor_scalar(c_sb[:, t, 0:QR], c_sb[:, t, 0:QR], rc[:, t:t + 1], None, ALU.mult)
                        m = dve.tensor_scalar(c_sb[:, t, QR:QR + KVR], c_sb[:, t, QR:QR + KVR], rc[:, 2 + t:3 + t], None, ALU.mult)
                    m.then_inc(c_norm, 1)
                if c == 14:
                    for k in range(4):
                        c_lo(k)
                if c == 15:
                    for k in range(4, 6):
                        c_lo(k)
            dve.wait_ge(gexp, 1)
            link(dve.tensor_scalar(gates[:, :, :], gates[:, :, :], 1.0, None, ALU.add))
            link(dve.reciprocal(gates[:, :, :], gates[:, :, :]))
            by_head = gates[:, :, :].rearrange("p t (h b) -> p b h t", b=3)
            by_pair = gates[:, :, :].rearrange("p t (i e b) -> p b e i t", e=2, b=3)
            dve.wait_ge(tables, 1)
            for e in range(2):
                m = dve.tensor_tensor(cgate[:, :, :, e], by_pair[:, 0, e, :, :],
                                      valid[:, :].unsqueeze(1).broadcast_to((P, NH // 2, TT)), ALU.mult)
            m.then_inc(gate_ok, 1)
            for c in range(18, 21):
                split_lo(c)
            for j in range(2):
                dve.wait_ge(kv_t, 1 + j)
                src = pairs(bank(6 + j))
                dve.tensor_copy(kcT[0:64, 2 * j:2 * j + 2, :], src[0:64, :, :])
                dve.tensor_copy(kcT[64:P, 2 * j:2 * j + 2, 0:T - 1], src[64:P, :, 1:T]).then_inc(kv_out, 1)
            dve.wait_ge(kv_out, 2)
            for y in range(2):
                for g in range(NG):
                    for half in range(2):
                        src = kcT[:, 2 * y + g, 16 * half:16 * half + 16 * NC].rearrange("p (n k two) -> p k n two", n=NC, two=2)[:, :, :, 0]
                        o = PRM["posk"] + 16 * y + 8 * half
                        m = dve.tensor_tensor(blkf[:, y, 8 * half:8 * half + 8, NC * g:NC * g + NC], src,
                                              wcols[:, o:o + 8].unsqueeze(2).broadcast_to((P, 8, NC)), ALU.add)
            m.then_inc(blk_f, 1)
            split_lo(21)
            dve.wait_ge(w_used, UKV_K + 1)
            for j in range(4):
                dve.tensor_copy(knT[:, 2 * j:2 * j + 2, :], pairs(bank(j))).then_inc(kn_out, 1)
            dve.wait_ge(w_used, UKV_V + 1)
            dve.tensor_copy(v_sb[:, 0, :], flat[:, 2048:3072]).then_inc(v_out, 1)
            dve.wait_ge(blk_hi, 1)
            low(blk[:, 1, :, :, :].rearrange("p y k n -> p (y k n)"), blkf[:, :, :, :].rearrange("p y k n -> p (y k n)"),
                blk[:, 0, :, :, :].rearrange("p y k n -> p (y k n)")).then_inc(blk_ok, 1)
            dve.tensor_copy(v_sb[:, 1, :], flat[:, 3072:4096]).then_inc(v_out, 1)

            STEP_OF = {n: i for i, n in SOFT.items()}

            def slot(i):
                if i in SOFT:
                    n = SOFT[i]
                    kind, u, h, branch = STEPS[i]
                    dve.wait_ge(score_t, n + 1)
                    if n >= 3:
                        dve.wait_ge(pt_t, STEP_OF[n - 3] + 1)
                    if kind == "mla":
                        bias = mask[:, :]
                    else:
                        dve.wait_ge(bias_ok, h + 1)
                        bias = bias_h[:, h % 2, :]
                    for q, (x, y) in enumerate(((0, P), (P, SEEN))):
                        m = dve.tensor_tensor_reduce(prob[:, n % 3, x:y], ps[:, 4 + n % 2, x:y], bias[:, x:y], 1.0, 3e38,
                                                     ALU.add, ALU.min, nmax[:, n, q:q + 1])
                    m.then_inc(score_m, 1)
                if i - 1 in SOFT:
                    n = SOFT[i - 1]
                    kind, u, h, branch = STEPS[i - 1]
                    dve.wait_ge(exp_ok, n + 1)
                    link(dve.reciprocal(scl[:, n, :], den[:, n, :]))
                    if kind != "mla":
                        b = 1 if kind == "slc" else 2
                        link(dve.tensor_tensor(scl[:, n, :], scl[:, n, :], by_head[:, b, h, :], ALU.mult))
                    p = prob[:, n % 3, :]
                    dve.tensor_scalar(p[:, 0:P], p[:, 0:P], scl[:, n, 0:1], None, ALU.mult)
                    dve.tensor_scalar(p[:, P:SEEN], p[:, P:SEEN], scl[:, n, 1:2], None, ALU.mult).then_inc(prob_ok, 1)
                j = i - 3
                if j >= 0 and LASTSTEP[STEPS[j][1]] == j:
                    u = STEPS[j][1]
                    dve.wait_ge(y_hi, u + 1)
                    low(yT[:, u, 1, :], bank(7, T), yT[:, u, 0, :], wcols[:, PRM["y"] + u:PRM["y"] + u + 1]).then_inc(y_lo, 1)

            def mean_square(part, dst):
                dve.wait_ge(ysum_t, part + 1)
                square = ssq[:, 6 + 2 * part:8 + 2 * part]
                dve.tensor_scalar(square, ps[:, 7, 256:258], 1.0 / (MH * MV), EPS, ALU.mult, ALU.add).then_inc(ysum_ok, 1)
                dve.wait_ge(ysum_ok, part + 1)
                guess(dst, square).then_inc(guessed, 1)

            def add_attention(part, n, group, last):
                dve.wait_ge(yr_ok, part + 1)
                dve.wait_ge(h_in, 32)
                r = (rm, rn)[part]
                for t in range(TT):
                    sums_ready(dve, t, group, last)
                    if part:
                        dve.wait_ge(dve_free, 2 * n + t + 1)
                    o = h_sb[:, t, 1024 * n:1024 * n + 1024]
                    dve.scalar_tensor_tensor(out=o, in0=flat[:, 1024 * t:1024 * t + 1024], scalar=r[:, t:t + 1], in1=o,
                                             op0=ALU.mult, op1=ALU.add).then_inc(dve_free, 1)

            for kind, i in PLAN:
                if (kind, i) == ("q", (WO_M + 4, 0)):
                    add_attention(0, 0, 3, WO_M + 3)
                elif (kind, i) == ("q", (WO_N, 0)):
                    add_attention(0, 1, 4, WO_N - 1)
                elif kind == "split":
                    split_lo(i)
                elif kind == "s":
                    slot(i)
                elif i == "keys":
                    for j in range(2):
                        dve.wait_ge(kv_t, j + 3)
                        dve.tensor_copy(kT[:, 2 * j:2 * j + 2, :], pairs(bank(j))).then_inc(kv_out, 1)
                elif i == "gelu":
                    u = ps[0:2 * NC, 4:6, 0:CMP_HID]
                    dve.wait_ge(g_sq, 1)
                    link(dve.tensor_scalar(h1b[:, :, :], h1a[:, :, :], 0.044715, 1.0, ALU.mult, ALU.add))
                    dve.tensor_tensor(h1b[:, :, :], u, h1b[:, :, :], ALU.mult).then_inc(g_in, 1)
                    dve.wait_ge(g_th, 1)
                    dve.scalar_tensor_tensor(out=h1a[:, :, :], in0=h1c[:, :, :], scalar=1.0, in1=u, op0=ALU.add,
                                             op1=ALU.mult).then_inc(g_ok, 1)
                elif i == "turn":
                    dve.wait_ge(g_t, 1)
                    dve.tensor_scalar(h1T[:, :, :].rearrange("p k n -> p (k n)"), bank(6, 4 * 2 * NC), 0.5, None, ALU.mult).then_inc(g_turned, 1)
                elif i == "project":
                    dve.wait_ge(k_t, 1)
                    for e in range(2):
                        dve.tensor_copy(kcmp[64 * e:64 * e + 64, :, e, :],
                                        ps[64 * e:64 * e + 64, 7, 0:2 * NC].rearrange("p (g n) -> p g n", g=NG))
                    dve.tensor_copy(vcmp[:, :, :], ps[0:NC, 7, 64:64 + NG * DK].rearrange("p (g d) -> p g d", g=NG)).then_inc(k_ok, 1)
                elif i == "queries":
                    sums_ready(dve, 1, 2, WO_M - 1)
                    dve.wait_ge(rs_ok, 2)
                    dve.tensor_scalar(q_sb[:, 1, :], flat[:, 1024:2048], r1q[:, 1:2], None, ALU.mult).then_inc(q_in, 1)
                elif i == "turn_q":
                    for j in range(2, 4):
                        dve.wait_ge(q_t, j + 1)
                        dve.tensor_copy(qT[:, 2 * j:2 * j + 2, :], pairs(bank(j))).then_inc(q_out, 1)
                elif i == "soft":
                    every = pc[:, :, :, :, :].rearrange("p i t e n -> p (i t e n)")
                    rows = pc[:, :, :, :, :].rearrange("p i t e n -> p (i t e) n")
                    dve.wait_ge(cs_t, 1)
                    dve.wait_ge(cb_ok, 1)
                    link(dve.tensor_tensor(every, bank(3, NH * TT * NC), cbias[:, :, :, :, :].rearrange("p i t e n -> p (i t e n)"), ALU.add))
                    link(dve.tensor_reduce(cmx[:, :], rows, AX.X, ALU.min))
                    dve.tensor_tensor(rows, rows, cmx[:, :].unsqueeze(2).broadcast_to((P, NH * TT, NC)), ALU.subtract).then_inc(cs_sub, 1)
                    dve.wait_ge(cs_exp, 1)
                    link(dve.tensor_reduce(cden[:, :], rows, AX.X, ALU.add))
                    link(dve.reciprocal(cden[:, :], cden[:, :]))
                    link(dve.tensor_tensor(cden[:, :], cden[:, :], cgate[:, :, :, :].rearrange("p i t e -> p (i t e)"), ALU.mult))
                    dve.tensor_tensor(rows, rows, cden[:, :].unsqueeze(2).broadcast_to((P, NH * TT, NC)), ALU.mult).then_inc(pc_ok, 1)
                elif i == "norm":
                    mean_square(0, rm[:, :])
                elif i == "norm_n":
                    mean_square(1, rn[:, :])

            def turned_lo(k):
                dve.wait_ge(ht_hi, k + 1)
                low(xT[:, 1, k, :], bank(4 + k % 4, T), xT[:, 0, k, :], wcols[:, PRM["mlp"] + k:PRM["mlp"] + k + 1]).then_inc(ht_lo, 1)

            for c in range(WO_N + 4, MLP0):
                if c == WO_N + 4:
                    add_attention(1, 0, 5, WO_N + 3)
                split_lo(c + 1)
                if c >= WO_N + 5:
                    for k in TURNS[c - WO_N - 5]:
                        turned_lo(k)
            add_attention(1, 1, 6, MLP0 - 1)
            for k in range(8, KT):
                turned_lo(k)
            for c in range(MLP0 + 1, LOOP0):
                split_lo(c)
            split_lo_loop(0, 1)
            dve.wait_ge(ssq_ok, 8)
            link(dve.tensor_scalar(r1q[:, :], ssq[:, 10:12], 1.0 / D, EPS, ALU.mult, ALU.add))
            link(dve.reciprocal(r1[:, :], r1q[:, :]))
            dve.wait_ge(acc0, 1)

            def hidden_lo(done):
                for q in range(4):
                    dve.wait_ge(hd_hi, done + q + 1)
                    low(hidT[:, 1, 2 * q:2 * q + 2, :], pairs(bank(4 + q)), hidT[:, 0, 2 * q:2 * q + 2, :]).then_inc(hd_lo, 1)

            def add_down(n, group, last, before):
                for t in range(TT):
                    sums_ready(dve, t, group, last)
                    dve.wait_ge(dve_free, before + 2 * n + t + 1)
                    o = acc[:, t, 1024 * n:1024 * n + 1024]
                    c0 = 2048 - 2048 * n + 1024 * t
                    dve.tensor_tensor(o, flat[:, c0:c0 + 1024], o, ALU.add).then_inc(dve_free, 1)

            hidden_lo(0)
            with dve.Fori(1, G) as g:
                for j in range(1, GC + 1):
                    split_lo_loop(j, g) if j < GC else split_lo_loop(0, g + 1)
                    if j == 13:
                        add_down(0, 9 - 3 + 3 * g, LOOP0 - GC + 11 + GC * g, 4 * g)
                add_down(1, 10 - 3 + 3 * g, LOOP0 - GC + 15 + GC * g, 4 * g)
                hidden_lo(4 * g)
            END = LOOP0 + GC * (G - 1)
            for j in range(1, 6):
                split_lo_loop(j, G)
            add_down(0, 8 + 3 * (G - 1), END + 3, 4 * G)
            for j in range(6, 8):
                split_lo_loop(j, G)
            add_down(1, 9 + 3 * (G - 1), END + 7, 4 * G)
            dve.wait_ge(dve_free, 8 + 4 * G)
            for t in range(TT):
                dve.scalar_tensor_tensor(out=h_sb[:, t, :], in0=acc[:, t, :], scalar=r1[:, t:t + 1], in1=h_sb[:, t, :],
                                         op0=ALU.mult, op1=ALU.add).then_inc(added, 1)
            dve.wait_ge(fw_in, 16)
            for t in range(TT):
                dve.wait_ge(fsq, t + 1)
                square, y, w = ssq[:, 12 + t:13 + t], rc[:, t:t + 1], rc[:, 2 + t:3 + t]
                link(dve.tensor_scalar(square, square, 1.0 / D, EPS, ALU.mult, ALU.add))
                link(guess(y, square))
                for _ in range(3):
                    link(dve.scalar_tensor_tensor(out=w, in0=y, scalar=y, in1=square, op0=ALU.mult, op1=ALU.mult))
                    link(dve.tensor_scalar(w, w, -0.5, 1.5, ALU.mult, ALU.add))
                    link(dve.tensor_tensor(y, y, w, ALU.mult))
                dve.scalar_tensor_tensor(out=h_sb[:, t, :], in0=h_sb[:, t, :], scalar=y, in1=fw[:, :],
                                         op0=ALU.mult, op1=ALU.mult).then_inc(normed, 1)

        @block.tensor
        def _(pe):
            def products(slot, shape, stationary, base, start, stop, free=None, only=None):
                blocks, width = shape
                cols = [(n, min(width, n + 512)) for n in range(0, width, 512)]
                for b in range(blocks):
                    for t in range(TT):
                        if only not in (None, TT * b + t):
                            continue
                        if start and b == 0 and free is not None:
                            free(t)
                        first, last = start and b == 0, stop and b == blocks - 1
                        for n0, n1 in cols:
                            o = flat[:, base[t] + n0:base[t] + n1]
                            w = slice(b * width + n0, b * width + n1)
                            pe.matmul(o, stationary(0, b, t), w_hi[:, slot, w], start=first, stop=False)
                            pe.matmul(o, stationary(0, b, t), w_lo[:, slot, w], start=False, stop=False)
                        for n0, n1 in cols:
                            o = flat[:, base[t] + n0:base[t] + n1]
                            m = pe.matmul(o, stationary(1, b, t), w_hi[:, slot, b * width + n0:b * width + n1], start=False, stop=last)
                        if last and t == 0:
                            m.then_inc(first_done, 1)
                if only in (None, blocks * TT - 1):
                    m.then_inc(w_used, 1)

            LOW, HIGH = (0, 1024), (2048, 3072)

            def stream(c, tiles, k0, base, start, stop, free=None, only=None):
                pe.wait_ge(lo_done, c + 1)
                products(split_slot(c), chunk(c)[1], lambda part, b, t: tiles(part, k0 + b, t), base, start, stop, free, only)

            def of_x(part, k, t):
                return xT[:, part, k, P * t:P * t + P]

            def of_c(part, k, t):
                return cT[:, part, k, P * t:P * t + P]

            def of_y(part, k, t):
                return yT[:, k, part, P * t:P * t + P]

            pe.wait_ge(prm_in, 16 * 8)
            pe.wait_ge(consts, 1)
            pe.transpose(bank(7, NPRM), prm[:, :], ident[0:NPRM, 0:NPRM]).then_inc(prm_t, 1)
            pe.wait_ge(x_in[0], 16 * TT)
            def turn_x(k):
                if k == 3:
                    pe.wait_ge(wcols_ok, 1)
                if k >= 4:
                    pe.wait_ge(xt_lo, k - 3)
                if k == KT // 2:
                    pe.wait_ge(x_in[1], 16 * TT)
                for t in range(TT):
                    m = pe.transpose(ps[:, 4 + k % 4, P * t:P * t + P], x_sb[:, t, P * k:P * k + P], ident[:, :])
                m.then_inc(xt_t, 1)

            def turn_c(k):
                if k >= 4:
                    pe.wait_ge(ct_lo, k - 3)
                for t in range(TT):
                    m = pe.transpose(ps[:, k % 4, P * t:P * t + P], c_sb[:, t, P * k:P * k + P], ident[:, :])
                m.then_inc(ct_t, 1)

            for k in range(4):
                turn_x(k)
            for c in range(8):
                pe.wait_ge(xt_lo, 2 * c + 2)
                stream(c, of_x, 2 * c, LOW, c == 0, c == 7)
                for k in (2 * c + 4, 2 * c + 5):
                    if k < KT:
                        turn_x(k)
            for c in range(8):
                stream(B_IN + c, of_x, 2 * c, HIGH, c == 0, c == 7)
                if c == 4:
                    pe.wait_ge(c_norm, 1)
                    for k in range(4):
                        turn_c(k)
                if c == 5:
                    for k in range(4, 6):
                        turn_c(k)

            def heads(c, banks, nheads, k0, nk):
                pe.wait_ge(lo_done, c + 1)
                width = chunk(c)[1][1]
                s = split_slot(c)
                for h in range(nheads):
                    o = ps[:, banks[h // 2], T * (h % 2):T * (h % 2) + T]
                    for b in range(nk):
                        w = slice(b * width + P * h, b * width + P * h + P)
                        pe.matmul(o, w_hi[:, s, w], cT[:, 0, k0 + b, :], start=b == 0, stop=False)
                        pe.matmul(o, w_hi[:, s, w], cT[:, 1, k0 + b, :], start=False, stop=False)
                        m = pe.matmul(o, w_lo[:, s, w], cT[:, 0, k0 + b, :], start=False, stop=b == nk - 1)
                m.then_inc(w_used, 1)

            pe.wait_ge(ct_lo, 6)
            pe.wait_ge(lo_done, UQ_PE + 1)
            for b in range(4):
                for t in range(TT):
                    o = bank(t)
                    w = slice(512 * b, 512 * b + 512)
                    s = split_slot(UQ_PE)
                    pe.matmul(o, of_c(0, b, t), w_hi[:, s, w], start=b == 0, stop=False)
                    pe.matmul(o, of_c(0, b, t), w_lo[:, s, w], start=False, stop=False)
                    m = pe.matmul(o, of_c(1, b, t), w_hi[:, s, w], start=False, stop=b == 3)
            m.then_inc(w_used, 1)
            heads(UQ_NOPE, (2, 3), 4, 0, 4)
            pe.wait_ge(act_free, 4)
            heads(UQ_NOPE + 1, (4, 5), 4, 0, 4)

            def turn_kd(j, b):
                pe.wait_ge(kd_ok, 2 * j + 2)
                for n in range(2):
                    for t in range(TT):
                        o = T * n + P * t
                        m = pe.transpose(ps[:, b, o:o + P], kd[:, 2 * j + n, t, :, :].rearrange("p c d -> p (c d)"), ident[:, :])
                m.then_inc(kv_t, 1)

            turn_kd(0, 6)
            turn_kd(1, 7)
            pe.wait_ge(qpe_out, 2)
            pe.wait_ge(qn_out, 2)
            heads(UKV_K, (0, 1, 2, 3), 8, 4, 2)
            pe.wait_ge(qn_out, 4)
            pe.wait_ge(kv_out, 2)
            pe.wait_ge(lo_done, UKV_V + 1)
            s = split_slot(UKV_V)
            for b in range(2):
                for t, col in ((0, 2048), (1, 3072)):
                    for n in range(2):
                        o = flat[:, col + 512 * n:col + 512 * n + 512]
                        w = slice(1024 * b + 512 * n, 1024 * b + 512 * n + 512)
                        pe.matmul(o, of_c(0, 4 + b, t), w_hi[:, s, w], start=b == 0, stop=False)
                        pe.matmul(o, of_c(0, 4 + b, t), w_lo[:, s, w], start=False, stop=False)
                        m = pe.matmul(o, of_c(1, 4 + b, t), w_hi[:, s, w], start=False, stop=b == 1)
            m.then_inc(w_used, 1)

            def sum_over_features(part):
                pe.wait_ge(sq_sum, MH * (part + 1))
                pe.wait_ge(y_lo, MH * (part + 1))
                for t in range(TT):
                    m = pe.matmul(ps[:, 7, 256 + t:257 + t], sqacc[:, part, P * t:P * t + P], ones[:, :], start=True, stop=True)
                m.then_inc(ysum_t, 1)

            SPANS = ((0, 0, P), (P, P, SEEN))

            def slot(i):
                if i in SOFT:
                    n = SOFT[i]
                    kind, u, h, branch = STEPS[i]
                    if n >= 2:
                        pe.wait_ge(score_m, n - 1)
                    if i == NMLA:
                        pe.wait_ge(q_out, 4)
                    p0 = 64 * (h % 2)
                    for q, c0, c1 in SPANS:
                        o = ps[:, 4 + n % 2, c0:c1]
                        if kind == "mla":
                            pe.matmul(o, qnT[:, h, q:q + P], knT[:, h, 0:c1 - c0], start=True, stop=False)
                            m = pe.matmul(o, qpT[p0:p0 + 64, h // 2, q:q + P], kpT[p0:p0 + 64, 0:c1 - c0], start=False, stop=True)
                        else:
                            m = pe.matmul(o, qT[p0:p0 + 64, h // 2, q:q + P], kT[p0:p0 + 64, 2 * branch + h // 8, 0:c1 - c0],
                                          start=True, stop=True)
                    m.then_inc(score_t, 1)
                j = i - 2
                if 0 <= j < len(STEPS):
                    if j >= 1:
                        pe.wait_ge(pt_out, j)
                    kind, u, h, branch = STEPS[j]
                    if kind == "cmp":
                        pe.wait_ge(pc_ok, 1)
                        for e in range(2):
                            for t in range(TT):
                                o = T * e + P * t
                                m = pe.transpose(ps[0:NC, 6, o:o + P], pc[:, h // 2, t, e, :], ident[:, :])
                    else:
                        n = SOFT[j]
                        pe.wait_ge(prob_ok, n + 1)
                        for c in range(3):
                            m = pe.transpose(ps[:, 6, P * c:P * c + P], prob[:, n % 3, P * c:P * c + P], ident[:, :])
                    m.then_inc(pt_t, 1)
                j = i - 3
                if 0 <= j < len(STEPS):
                    kind, u, h, branch = STEPS[j]
                    pe.wait_ge(pt_out, j + 1)
                    if u and (kind == "mla" or (branch == 0 and h % 2 == 0)):
                        pe.wait_ge(y_lo, u)
                        if u == MH + 1:
                            sum_over_features(0)
                            pe.wait_ge(ysum_ok, 1)
                    elif u == 0:
                        pe.wait_ge(k_ok, 1)
                    p = probT[:, j % 2, :]
                    if kind == "cmp":
                        for e in range(2):
                            m = pe.matmul(ps[64 * e:64 * e + 64, 7, 0:T], vcmp[:, h // 8, :], p[0:NC, T * e:T * e + T], start=False, stop=True)
                    else:
                        if kind == "mla":
                            o, first, last = ps[:, 7, 0:T], True, True
                            v = [v_sb[:, t, MV * h:MV * h + MV] for t in range(TT)]
                        else:
                            e = h % 2
                            o, first, last = ps[64 * e:64 * e + 64, 7, 0:T], branch == 0, False
                            off = 256 * (1 + branch) + 128 * (h // 8) + DK
                            v = [kv_sb[:, t, off:off + DK] for t in range(TT)]
                        pe.matmul(o, v[0], p[:, 0:T], start=first, stop=False)
                        m = pe.matmul(o[:, P:T], v[1], p[:, T:SEEN], start=False, stop=last)
                    m.then_inc(o_t, 1)

            for kind, i in PLAN:
                if kind == "w" and i >= A_IN:
                    if i == A_IN:
                        pe.wait_ge(kv_out, 4)
                        pe.wait_ge(qp_out, 2)
                    stream(i, of_x, 2 * (i - A_IN), LOW, i == A_IN, i == WO_M - 1)
                elif kind == "w":
                    if i == CMP:
                        pe.wait_ge(blk_ok, 1)
                        pe.wait_ge(v_out, 1)
                    pe.wait_ge(lo_done, i + 1)
                    y, half, s = (i - CMP) // 2, (i - CMP) % 2, split_slot(i)
                    o = ps[0:2 * NC, 4 + y, 0:CMP_HID]
                    for b in range(8):
                        k = 8 * half + b
                        w = slice(CMP_HID * b, CMP_HID * b + CMP_HID)
                        pe.matmul(o, blk[:, 0, y, k, :], w_hi[:, s, w], start=k == 0, stop=False)
                        pe.matmul(o, blk[:, 0, y, k, :], w_lo[:, s, w], start=False, stop=False)
                        m = pe.matmul(o, blk[:, 1, y, k, :], w_hi[:, s, w], start=False, stop=k == 15)
                    m.then_inc(w_used, 1)
                elif kind == "q":
                    c, quarter = i
                    n, j, part = (c - WO_M) // 4, (c - WO_M) % 4, (c - WO_M) // 8

                    def free(t, n=n):
                        if n:
                            pe.wait_ge(dve_free, 2 * n - 1 + t)
                        elif t:
                            pe.wait_ge(cs_sub, 1)
                    if n % 2 == 0 and quarter == 0:
                        pe.wait_ge(y_lo, 8 * part + 2 * j + 2)
                    stream(c, of_y, 8 * part + 2 * j, LOW, j == 0, j == 3, free, quarter)
                elif kind == "s":
                    slot(i)
                elif i == "keys":
                    for j in range(2):
                        pe.wait_ge(kn_out, j + 1)
                        turn_kd(2 + j, j)
                elif i == "rotary":
                    pe.wait_ge(kn_out, 4)
                    pe.wait_ge(v_out, 2)
                    pe.wait_ge(qpr_ok, 2)
                    pe.wait_ge(kpe_ok, 2)
                    for c in range(4):
                        for t in range(TT):
                            o = T * (c % 2) + P * t
                            m = pe.transpose(ps[:, 2 + c // 2, o:o + P], qpr[:, t, P * c:P * c + P], ident[:, :])
                        if c % 2:
                            m.then_inc(qp_t, 1)
                    for t in range(TT):
                        m = pe.transpose(ps[:, 6, P * t:P * t + P], kpe[:, t, :], ident[:, :])
                    m.then_inc(qp_t, 1)
                elif i == "turn":
                    pe.wait_ge(g_ok, 1)
                    pe.wait_ge(qp_out, 3)
                    for y in range(2):
                        for k in range(2):
                            o = 2 * NC * (2 * y + k)
                            m = pe.transpose(ps[:, 6, o:o + 2 * NC], h1a[:, y, P * k:P * k + P], ident[0:2 * NC, 0:2 * NC])
                    m.then_inc(g_t, 1)
                elif i == "project":
                    pe.wait_ge(g_turned, 1)
                    pe.wait_ge(w2_in, 48)
                    for k in range(2):
                        pe.matmul(ps[:, 7, 0:2 * NC], w2k[:, k, :, :].rearrange("p c d -> p (c d)"), h1T[:, k, :],
                                  start=k == 0, stop=k == 1)
                    for g in range(NG):
                        for k in range(2):
                            m = pe.matmul(ps[0:NC, 7, 64 + DK * g:64 + DK * g + DK], h1T[:, 2 + k, NC * g:NC * g + NC], w2v[:, k, :],
                                          start=k == 0, stop=k == 1)
                    m.then_inc(k_t, 1)
                elif i == "turn_q":
                    pe.wait_ge(q_in, 2)
                    for j in range(4):
                        for c in (2 * j, 2 * j + 1):
                            for t in range(TT):
                                o = T * (c % 2) + P * t
                                m = pe.transpose(ps[:, j, o:o + P], q_sb[:, t, P * c:P * c + P], ident[:, :])
                        m.then_inc(q_t, 1)
                elif i == "scores":
                    for c in range(NH // 2):
                        for t in range(TT):
                            o = 2 * NC * (TT * c + t)
                            m = pe.matmul(ps[:, 3, o:o + 2 * NC], qT[:, c, P * t:P * t + P],
                                          kcmp[:, c // 4, :, :].rearrange("p e n -> p (e n)"), start=True, stop=True)
                    m.then_inc(cs_t, 1)
                elif i == "norm_n":
                    sum_over_features(1)

            def turn_h(k):
                if k >= 4:
                    pe.wait_ge(ht_lo, k - 3)
                for t in range(TT):
                    m = pe.transpose(ps[:, 4 + k % 4, P * t:P * t + P], h_sb[:, t, P * k:P * k + P], ident[:, :])
                m.then_inc(ht_t, 1)

            for c in range(WO_N + 4, MLP0):
                n, j = (c - WO_N) // 4, (c - WO_N) % 4
                stream(c, of_y, 8 + 2 * j, LOW, j == 0, j == 3, lambda t: pe.wait_ge(dve_free, 2 + 2 * n + t + 1))
                if c >= WO_N + 5:
                    if c == WO_N + 5:
                        pe.wait_ge(dve_free, 6)
                        pe.wait_ge(ysum_ok, 2)
                    for k in TURNS[c - WO_N - 5]:
                        turn_h(k)
            pe.wait_ge(dve_free, 8)
            for k in range(8, KT):
                turn_h(k)

            def stream_loop(j, g, tiles, k0, base, start, stop, free=None):
                pe.wait_ge(lo_done, LOOP0 - GC + j + 1 + GC * g)
                products(j % SPLIT, (2, 1024), lambda part, b, t: tiles(part, k0 + b, t), base, start, stop, free)

            def of_hidden(part, k, t):
                return hidT[:, part, k, P * t:P * t + P]

            def turn_hidden(squared, added_before):
                pe.wait_ge(hid_ok, squared)
                if added_before is not None:
                    pe.wait_ge(dve_free, added_before)
                for q in range(4):
                    for c in (2 * q, 2 * q + 1):
                        for t in range(TT):
                            o = T * (c % 2) + P * t
                            m = pe.transpose(ps[:, 4 + q, o:o + P], hid[:, t, P * c:P * c + P], ident[:, :])
                    m.then_inc(hd_t, 1)

            for j in range(8):
                pe.wait_ge(ht_lo, 2 * j + 2)
                stream(MLP0 + j, of_x, 2 * j, LOW, j == 0, j == 7)
            pe.wait_ge(ht_lo, KT)
            turn_hidden(2, None)

            def free_up(g):
                def free(t):
                    pe.wait_ge(relu_ok, 2 * g)
                    pe.wait_ge(dve_free, 3 + t + 4 * g)
                return free

            with pe.Fori(1, G) as g:
                for j in range(8):
                    stream_loop(j, g, of_x, 2 * j, LOW, j == 0, j == 7, free_up(g))
                for j in range(8, 12):
                    pe.wait_ge(hd_lo, 4 * g - 4 + j - 7)
                    if j == 8:
                        pe.wait_ge(hd_lo, 4 * g)
                    stream_loop(j, g, of_hidden, 2 * (j - 8), HIGH, j == 8, j == 11)
                for j in range(12, 16):
                    stream_loop(j, g, of_hidden, 2 * (j - 12), LOW, j == 12, j == 15, lambda t: pe.wait_ge(relu_ok, 2 * g + t + 1))
                turn_hidden(2 * g + 2, 4 * g + 6)
            pe.wait_ge(hd_lo, 4 * G)
            for j in range(4):
                stream_loop(j, G, of_hidden, 2 * j, HIGH, j == 0, j == 3)
            for j in range(4, 8):
                stream_loop(j, G, of_hidden, 2 * (j - 4), LOW, j == 4, j == 7, lambda t: pe.wait_ge(dve_free, 3 + t + 4 * G))


_INS = ["x", "positions", "attn_norm_w", "w_in", "mla_q_norm_w", "mla_w_uq", "mla_kv_norm_w", "mla_w_ukv",
        "cmp_pos_k", "cmp_pos_v", "cmp_w1_k", "cmp_w2_k", "cmp_w1_v", "cmp_w2_v", "mla_out_norm_w",
        "nsa_out_norm_w", "w_o", "mlp_norm_w", "w_up", "w_down", "final_norm_w"]


def kernel(**inputs):
    import concourse.bacc as bacc
    from concourse.bass_utils import run_bass_kernel_spmd

    nc = bacc.Bacc("TRN2", target_bir_lowering=False, num_devices=1)
    freq = (1.0 / (np.float32(10000.0) ** (np.arange(0, ROPE, 2, dtype=np.float32) / np.float32(ROPE)))).astype(np.float32)
    arrays, args = {}, {}
    for name in _INS + ["inv_freq"]:
        v = freq if name == "inv_freq" else np.ascontiguousarray(inputs[name])
        arrays[f"in_{name}"] = v
        args[name] = nc.dram_tensor(f"in_{name}", v.shape, mybir.dt.from_np(v.dtype), kind="ExternalInput").ap()
    out = nc.dram_tensor("out", (1, T, D), F32, kind="ExternalOutput").ap()
    build(nc, args, out)
    result = run_bass_kernel_spmd(nc, [arrays], core_ids=[0])
    return result.results[0]["out"]
```

```python
from contextlib import ExitStack

import numpy as np

import concourse.bass as bass
from concourse import mybir

F32 = mybir.dt.float32
F32R = mybir.dt.float32r
I32 = mybir.dt.int32
ALU = mybir.AluOpType
ACT = mybir.ActivationFunctionType
AX = mybir.AxisListType

P = 128
T, D = 256, 2048
TT = T // P
KT = D // P
EPS = 1e-6
QR, KVR, NOPE, ROPE, MH, MV = 512, 256, 128, 64, 8, 128
NH, NG, DK = 16, 2, 64
CMP_LEN, CMP_STRIDE, CMP_HID = 32, 16, 256
NC = (T - CMP_LEN) // CMP_STRIDE + 1
WINDOW, SEL_LEN, SEL_TOPK = 512, 64, 16
assert T // SEL_LEN <= SEL_TOPK and WINDOW >= T
HID = 4 * D
CW = 832
BW = 816
OFF_Q = CW
OFF_B = CW + NH * DK
MLA_SCALE = float(NOPE + ROPE) ** -0.5
NSA_SCALE = float(DK) ** -0.5
HALF = ROPE // 2
SLOPE = [float(np.float32(2.0 ** (-8.0 / NH)) ** (h + 1)) for h in range(NH)]
BIG = 1e30
SEEN = 3 * P
TWO_PI = 2.0 * np.pi
C1 = 6.28125
C2 = float(np.float32(int((TWO_PI - C1) * 2 ** 20) / 2 ** 20))
C3 = float(TWO_PI - C1 - C2)
PI_IN = float(np.nextafter(np.float32(np.pi), np.float32(0)))
MAGIC = float(1.5 * 2 ** 23)

PRM = dict(attn=0, mlp=16, c=32, y=38, posk=54, posv=70)
NPRM = 86

C_IN, B_IN, UQ_PE, UQ_NOPE, UKV_K, UKV_V, WO_M, WO_N, MLP0 = 0, 8, 16, 17, 19, 20, 33, 41, 49
CMP = (21, 23, 25, 27)
A_IN = (22, 24, 26, 28, 29, 30, 31, 32)
RAW, SPLIT = 4, 2
G = 8
GC = 16


def raw_slot(c):
    return (c + 3) % RAW


def split_slot(c):
    return (c + 1) % SPLIT


STEPS = [("mla", h, h, 0) for h in range(MH)]
for _u in range(MH, 16):
    _a = 2 * (_u - MH)
    STEPS += [("slc", _u, _a, 0), ("win", _u, _a, 1), ("slc", _u, _a + 1, 0), ("win", _u, _a + 1, 1), ("cmp", _u, _a, 2)]
NMLA = MH
LAG = 3
LASTSTEP = {s[1]: i for i, s in enumerate(STEPS)}
SOFT = {i: n for n, i in enumerate([i for i, s in enumerate(STEPS) if s[0] != "cmp"])}


PLAN = [("k", "keys"), ("k", "rotary")]
for _c in range(CMP[0], A_IN[3] + 1):
    PLAN += [("w", _c)] + [(part, (_c + 1, half)) for half in range(2) for part in ("hi", "lo")]
    PLAN += {CMP[1]: [("k", "rotary_k")], CMP[3]: [("k", "gelu")], A_IN[3]: [("k", "turn")]}.get(_c, [])
_s = 0
for _c in A_IN[4:]:
    PLAN += [("q", (_c, 0)), ("q", (_c, 1)), ("hi", (_c + 1, None))]
    PLAN += [("k", "project")] if _s == 0 else []
    PLAN += [("s", _s), ("q", (_c, 2)), ("q", (_c, 3)), ("lo", (_c + 1, None))]
    PLAN += [("k", "queries")] if _c == WO_M - 1 else []
    PLAN += [("s", _s + 1)]
    _s += 2
assert _s == NMLA
PLAN += [("k", "turn_q"), ("s", NMLA), ("k", "scores"), ("s", NMLA + 1), ("k", "soft")]
_s = NMLA + 2


def _step(s):
    if s > len(STEPS) + LAG:
        return [("k", "norm_n")] if s == len(STEPS) + LAG + 1 else []
    return [("s", s)] + ([("k", "weigh")] if s == NMLA + 3 else [])


for _c in range(WO_M, WO_N + 4):
    if _c in (WO_M + 4, WO_N):
        PLAN += [("k", "add")] + _step(_s)
        _s += 1
    for _n in range(4):
        PLAN += [("q", (_c, _n))] + {0: [("hi", (_c + 1, 0))], 1: [("lo", (_c + 1, 0)), ("hi", (_c + 1, 1))],
                                     2: [("lo", (_c + 1, 1))]}.get(_n, []) + _step(_s)
        _s += 1
assert _s > len(STEPS) + LAG + 1


HALVED = [i[0] for kind, i in PLAN if kind == "hi" and i[1] == 0]
FREED = list(range(CMP[0], A_IN[3]))

TURNS = ((0, 1, 2, 3), (4, 5, 6, 7))


def build(nc, a, out):
    with ExitStack() as ctx:
        def seq(base, *specs):
            made = []
            for name, shape, dt in specs:
                made.append(nc.alloc_sbuf_tensor_at(name, shape, dt, offset=base))
                base += (4 * int(np.prod(shape[1:])) + 31) // 32 * 32
            return (*made, base)

        X_AT = (nc.sbuf_base + 31) // 32 * 32
        xT, Y_AT = seq(X_AT, ("xT", [P, 2, KT, T], F32R))
        yT, W_AT = seq(Y_AT, ("yT", [P, 16, 2, T], F32R))
        w_hi, w_lo, raw, F_AT = seq(W_AT, ("w_hi", [P, SPLIT, 2048], F32R), ("w_lo", [P, SPLIT, 2048], F32R),
                                    ("raw", [P, RAW, 2048], F32))
        YN_AT = Y_AT + 4 * 8 * 2 * T
        cT, _ = seq(YN_AT, ("cT", [P, 2, 6, T], F32R))
        blk, h1c, h1T, e = seq(YN_AT, ("blk", [P, 2, 2, 16, 2 * NC], F32R), ("h1c", [2 * NC, 2, CMP_HID], F32),
                               ("h1T", [P, 4, 2 * NC], F32))
        KC_AT = YN_AT + 4 * 2 * 6 * T
        assert e <= KC_AT
        kcT, e = seq(KC_AT, ("kcT", [P, 4, T], F32))
        assert e <= W_AT
        h1a, h1b, e = seq(KC_AT, ("h1a", [2 * NC, 2, CMP_HID], F32), ("h1b", [2 * NC, 2, CMP_HID], F32))
        assert e <= W_AT
        sink, kd, e = seq(Y_AT, ("sink", [P, D], F32), ("kd", [P, 8, TT, 2, DK], F32))
        assert e <= YN_AT
        hidT, _ = seq(Y_AT, ("hidT", [P, 2, 8, T], F32R))
        q_sb, qT, bias_h, cbias, pc, e = seq(
            X_AT, ("q_sb", [P, TT, NH * DK], F32), ("qT", [P, 8, T], F32), ("bias_h", [P, 2, SEEN], F32),
            ("cbias", [P, NH // 2, TT, 2, NC], F32), ("pc", [P, NH // 2, TT, 2, NC], F32))
        assert e <= Y_AT
        ident, wcols, ones, r1, r1q, rc, rm, rn, ssq, root_w, A_AT = seq(
            F_AT, ("ident", [P, P], F32), ("wcols", [P, NPRM], F32), ("ones", [P, 1], F32), ("r1", [P, TT], F32),
            ("r1q", [P, TT], F32), ("rc", [P, 4], F32), ("rm", [P, TT], F32), ("rn", [P, TT], F32),
            ("ssq", [P, 16], F32), ("root_w", [P, 4], F32))
        (posf, posi, den, scl, nmax, cden, cmx, cgate, valid, invf, gates, dist, mask, cdist, cdi, kv_sb, kT, probT,
         sq, sqacc, w2k, w2v, kcmp, vcmp, prm, M_AT) = seq(
            A_AT, ("posf", [P, TT], F32), ("posi", [P, TT], I32), ("den", [P, 40, 2], F32), ("scl", [P, 40, 2], F32),
            ("nmax", [P, 40, 2], F32), ("cden", [P, NH * TT], F32), ("cmx", [P, NH * TT], F32),
            ("cgate", [P, NH // 2, TT, 2], F32), ("valid", [P, TT], F32), ("invf", [P, HALF], F32),
            ("gates", [P, TT, 3 * NH], F32), ("dist", [P, SEEN], F32), ("mask", [P, SEEN], F32),
            ("cdist", [P, TT, NC], F32), ("cdi", [P, TT, NC], I32), ("kv_sb", [P, TT, BW], F32), ("kT", [P, 4, T], F32),
            ("probT", [P, 2, 512], F32), ("sq", [P, 2, T], F32),
            ("sqacc", [P, 2, T], F32), ("w2k", [P, 2, 2, DK], F32), ("w2v", [P, 2, DK], F32),
            ("kcmp", [P, NG, 2, NC], F32), ("vcmp", [NC, NG, DK], F32), ("prm", [NPRM - KT, P], F32))
        cs, angs, angk, L_AT = seq(M_AT, ("cs", [P, 2, TT * HALF], F32), ("angs", [P, 2, TT * HALF], F32),
                                   ("angk", [P, 2, TT * HALF], F32))
        c_sb, qpr, v_sb, qnT, knT, qpT, kpT, kpe, R_AT = seq(
            L_AT, ("c_sb", [P, TT, CW], F32), ("qpr", [P, TT, MH * ROPE], F32), ("v_sb", [P, TT, MH * MV], F32),
            ("qnT", [P, MH, T], F32), ("knT", [P, MH, T], F32), ("qpT", [P, 4, T], F32), ("kpT", [P, T], F32),
            ("kpe", [P, TT, 2 * ROPE], F32))
        rtmp, blkf, e = seq(R_AT, ("rtmp", [P, 2, MH * HALF], F32), ("blkf", [P, 2, 16, 2 * NC], F32))
        assert e <= nc.sbuf_usable_end
        ysb, prob, e = seq(R_AT, ("ysb", [P, 2, T], F32), ("prob", [P, LAG + 1, SEEN], F32))
        assert e <= nc.sbuf_usable_end, (e, nc.sbuf_usable_end)
        di, prm0, _ = seq(L_AT, ("di", [P, SEEN], I32), ("prm0", [KT, P], F32))
        qpe, _ = seq(L_AT, ("qpe", [P, TT, MH * ROPE], F32))
        x_sb, _ = seq(L_AT + 4 * 1664, ("x_sb", [P, TT, D], F32))
        h_sb, H_END = seq(L_AT, ("h_sb", [P, TT, D], F32))
        sink2, e = seq(H_END, ("sink2", [P, D], F32))
        assert e <= nc.sbuf_usable_end
        acc, hid, e = seq(A_AT, ("acc", [P, TT, D], F32), ("hid", [P, 8, T], F32))
        assert e <= M_AT, (e, M_AT)
        fw, _ = seq(X_AT, ("fw", [P, D], F32))

        ps = ctx.enter_context(nc.psum_tensor("ps", [P, 8, 512], F32))
        flat = ps[:, :, :].rearrange("p b n -> p (b n)")

        def bank(b, n=512, p0=0, p1=P):
            return ps[p0:p1, b, 0:n]

        def pairs(ap):
            return ap.rearrange("p (k t) -> p k t", k=2)

        def sems(*names):
            return [ctx.enter_context(nc.semaphore(n)) for n in names]

        x_in = sems("x_in0", "x_in1")
        raw_in = sems(*[f"raw_in{n}" for n in range(RAW)])
        prm0_in, prm_in, cst_in, w2_in, h_in, fw_in, stored = sems("prm0_in", "prm_in", "cst_in", "w2_in", "h_in", "fw_in", "stored")
        hi_done, half_hi, lo_done, w_used, w_half = sems("hi_done", "half_hi", "lo_done", "w_used", "w_half")
        first_done, = sems("first_done")
        act_free, dve_free = sems("act_free", "dve_free")
        pool_c, dve_c = sems("pool_c", "dve_c")
        consts, warm, tables, prm_t, wcols_ok = sems("consts", "warm", "tables", "prm_t", "wcols_ok")
        xt_t, xt_hi, xt_lo, ct_t, ct_hi, ct_lo = sems("xt_t", "xt_hi", "xt_lo", "ct_t", "ct_hi", "ct_lo")
        ssq_ok, rs_ok, ang_ok, sin_ok = sems("ssq_ok", "rs_ok", "ang_ok", "sin_ok")
        c_norm, kpe_ok, qpe_out, qpr_ok, qn_out, kn_out, v_out = sems(
            "c_norm", "kpe_ok", "qpe_out", "qpr_ok", "qn_out", "kn_out", "v_out")
        kv_t, kv_out, qp_t, qp_out, blk_f, blk_hi, blk_ok = sems(
            "kv_t", "kv_out", "qp_t", "qp_out", "blk_f", "blk_hi", "blk_ok")
        kd_ok, gexp, gate_ok, q_in, q_t, q_out, q_out2 = sems(
            "kd_ok", "gexp", "gate_ok", "q_in", "q_t", "q_out", "q_out2")
        g_sq, g_in, g_th, g_ok, g_t, g_turned, k_t, k_ok = sems(
            "g_sq", "g_in", "g_th", "g_ok", "g_t", "g_turned", "k_t", "k_ok")
        cs_t, cs_in, cs_sub, cs_exp, pc_ok, cb_ok = sems("cs_t", "cs_in", "cs_sub", "cs_exp", "pc_ok", "cb_ok")
        bias_ok, score_t, score_m, exp_ok, prob_ok, pt_t, pt_out, o_t = sems(
            "bias_ok", "score_t", "score_m", "exp_ok", "prob_ok", "pt_t", "pt_out", "o_t")
        y_out, y_sq, y_hi, y_lo, sq_sum, ysum_t, ysum_ok, yr_ok, guessed = sems(
            "y_out", "y_sq", "y_hi", "y_lo", "sq_sum", "ysum_t", "ysum_ok", "yr_ok", "guessed")
        up_half, up_ok, up_high, hid_ok, acc0, merged, added, weighted, normed0, normed1, fsq, root_ok = sems(
            "up_half", "up_ok", "up_high", "hid_ok", "acc0", "merged", "added", "weighted", "normed0", "normed1", "fsq", "root_ok")
        ht_t, ht_hi, ht_lo, hd_hi, hd_lo = sems("ht_t", "ht_hi", "ht_lo", "hd_hi", "hd_lo")

        win = a["w_in"][0].rearrange("(k p) n -> p k n", p=P)
        uq = a["mla_w_uq"][0].rearrange("(k p) (h e) -> p k h e", p=P, e=NOPE + ROPE)
        ukv = a["mla_w_ukv"][0].rearrange("(k p) (h e) -> p k h e", p=P, e=NOPE + MV)
        wo = a["w_o"][0].rearrange("(k p) n -> p k n", p=P)
        up = a["w_up"][0].rearrange("(k p) (g m n) -> p k g m n", p=P, g=G, m=2)
        dn = a["w_down"][0].rearrange("(g k p) n -> p g k n", p=P, g=G)
        cw1 = [a[n][0].rearrange("(k p) n -> p k n", p=P) for n in ("cmp_w1_k", "cmp_w1_v")]

        def chunk(c):
            if c < B_IN:
                return [win[:, 2 * c:2 * c + 2, 0:CW]], (2, CW)
            if c < UQ_PE:
                k = 2 * (c - B_IN)
                return [win[:, k:k + 2, OFF_B:OFF_B + BW]], (2, BW)
            if c == UQ_PE:
                return [uq[:, k, :, NOPE:] for k in range(4)], (4, 512)
            if c < UKV_K:
                h = 4 * (c - UQ_NOPE)
                return [uq[:, k, h:h + 4, 0:NOPE] for k in range(4)], (4, 512)
            if c <= UKV_V:
                o = 0 if c == UKV_K else NOPE
                return [ukv[:, k, :, o:o + NOPE] for k in range(2)], (2, 1024)
            if c in CMP:
                j = CMP.index(c)
                return [cw1[j // 2][:, 8 * (j % 2):8 * (j % 2) + 8, :]], (8, CMP_HID)
            if c < WO_M:
                k = 2 * A_IN.index(c)
                return [win[:, k:k + 2, OFF_Q:OFF_B]], (2, 1024)
            if c < MLP0:
                part, n, j = (c - WO_M) // 8, (c - WO_M) // 4 % 2, (c - WO_M) % 4
                k = 8 * part + 2 * j
                return [wo[:, k:k + 2, 1024 * n:1024 * n + 1024]], (2, 1024)
            m, j = (c - MLP0) // 4, (c - MLP0) % 4
            return [up[:, 4 * j:4 * j + 4, 0, m, :]], (4, 512)

        def columns(c, half):
            n = int(np.prod(chunk(c)[1]))
            return (0, n) if half is None else (half * n // 2, (half + 1) * n // 2)

        LOOP0 = MLP0 + 8
        assert raw_slot(LOOP0) == 0 and split_slot(LOOP0) == 0

        def loads(c):
            return sum(len(chunk(k)[0]) for k in range(c % RAW, c + 1, RAW))

        LOADS0 = [loads(LOOP0 - RAW + s) for s in range(RAW)]

        x_rows = a["x"][0].rearrange("(t p) d -> t p d", p=P)
        o_rows = out[0].rearrange("(t p) d -> t p d", p=P)
        block = ctx.enter_context(nc.Block())

        TABLE = [(a[name][0].rearrange("(r p) -> r p", p=P), row, n) for name, row, n in (
            ("mlp_norm_w", 16, 16), ("mla_q_norm_w", 32, 4), ("mla_kv_norm_w", 36, 2),
            ("mla_out_norm_w", 38, 8), ("nsa_out_norm_w", 46, 8))]
        TABLE += [(a[name][0].rearrange("(r two) d -> r (two d)", two=2), PRM[at], 16)
                  for name, at in (("cmp_pos_k", "posk"), ("cmp_pos_v", "posv"))]

        @block.sync
        def _(sp):
            sp.dma_start(prm0[:, :], a["attn_norm_w"][0].rearrange("(r p) -> r p", p=P)).then_inc(prm0_in, 16)
            for t in range(TT):
                sp.dma_start(x_sb[:, t, 0:D // 2], x_rows[t][:, 0:D // 2]).then_inc(x_in[0], 16)
            for c in range(LOOP0):
                if c >= RAW:
                    sp.wait_ge(lo_done, c - RAW + 1)
                src, (b, w) = chunk(c)
                dst = raw[:, raw_slot(c), 0:b * w].rearrange("p (b w) -> p b w", b=b)
                if len(src) == 1:
                    sp.dma_start(dst, src[0]).then_inc(raw_in[raw_slot(c)], 16)
                else:
                    for k, piece in enumerate(src):
                        sp.dma_start(dst[:, k, :].rearrange("p (h e) -> p h e", h=piece.shape[1]), piece)\
                            .then_inc(raw_in[raw_slot(c)], 16)
                if c == 0:
                    for t in range(TT):
                        sp.dma_start(x_sb[:, t, D // 2:D], x_rows[t][:, D // 2:D]).then_inc(x_in[1], 16)
                if c == RAW - 1:
                    for src, row, n in TABLE:
                        sp.dma_start(prm[row - KT:row - KT + n, :], src).then_inc(prm_in, 16)
                    sp.dma_start(posi[:, :], a["positions"].rearrange("b (t p) -> p (b t)", p=P),
                                  allow_slow_non_contiguous=True).then_inc(cst_in, 16)
                    sp.dma_start(invf[:, :], a["inv_freq"].rearrange("(o d) -> o d", o=1).broadcast_to((P, HALF))).then_inc(cst_in, 16)
                    for twice in range(2):
                        sp.dma_start(w2k[:, :, twice, :], a["cmp_w2_k"][0].rearrange("(k p) n -> p k n", p=P)).then_inc(w2_in, 16)
                    sp.dma_start(w2v[:, :, :], a["cmp_w2_v"][0].rearrange("(k p) n -> p k n", p=P)).then_inc(w2_in, 16)
                if c == WO_M + 4:
                    sp.wait_ge(y_lo, MH)
                    for t in range(TT):
                        sp.dma_start(h_sb[:, t, :], x_rows[t]).then_inc(h_in, 16)
            with sp.Fori(1, G) as g:
                for j in range(GC):
                    sp.wait_ge(lo_done, LOOP0 - GC + j - RAW + 1 + GC * g)
                    half, k = j // 8, j % 4
                    dst = raw[:, j % RAW, :].rearrange("p (a n) -> p a n", a=2 if j // 4 % 2 else 4)
                    if j // 4 % 2 == 0:
                        src = up[:, 4 * k:4 * k + 4, bass.ds(g, 1), half, :].rearrange("p a g n -> p a (g n)")
                    else:
                        k, n = 2 * k, half
                        src = dn[:, bass.ds(g - 1, 1), k:k + 2, 1024 * n:1024 * n + 1024].rearrange("p g a n -> p (g a) n")
                    sp.dma_start(dst, src).then_inc(raw_in[j % RAW], 16)
            for j in range(8):
                k, n = 2 * (j % 4), j // 4
                sp.wait_ge(lo_done, LOOP0 + GC * (G - 1) + j - RAW + 1)
                sp.dma_start(raw[:, j % RAW, :].rearrange("p (a n) -> p a n", a=2),
                             dn[:, G - 1, k:k + 2, 1024 * n:1024 * n + 1024]).then_inc(raw_in[j % RAW], 16)
            sp.wait_ge(w_used, LOOP0 + GC * (G - 1))
            sp.dma_start(fw[:, :], a["final_norm_w"].rearrange("(o d) -> o d", o=1).broadcast_to((P, D))).then_inc(fw_in, 16)
            for t in range(TT):
                for n, done in enumerate((normed0, normed1)):
                    sp.wait_ge(done, t + 1)
                    half = slice(1024 * n, 1024 * n + 1024)
                    sp.dma_start(o_rows[t][:, half], h_sb[:, t, half]).then_inc(stored, 16)
            sp.wait_ge(stored, 16 * TT * 2)

        @block.gpsimd
        def _(pool):
            chain = [0]

            def link(ins):
                chain[0] += 1
                ins.then_inc(pool_c, 1)
                pool.wait_ge(pool_c, chain[0])

            link(pool.memset(ident[:, :], 0.0))
            link(pool.affine_select(out=ident[:, :], in_=ident[:, :], compare_op=ALU.not_equal, fill=1.0, base=0,
                                    pattern=[[-1, P]], channel_multiplier=1))
            pool.memset(ones[:, :], 1.0).then_inc(consts, 1)
            link(pool.memset(kcmp[:, :, :, :], 0.0))
            pool.iota(di[:, 0:P], [[-1, P]], base=0, channel_multiplier=1)
            link(pool.iota(di[:, P:SEEN], [[-1, T]], base=P, channel_multiplier=1))
            link(pool.iota(cdi[:, :, :], [[P, TT], [-CMP_STRIDE, NC]], base=1 - CMP_LEN, channel_multiplier=1))
            link(pool.tensor_copy(dist[:, :], di[:, :]))
            link(pool.tensor_scalar(mask[:, :], dist[:, :], 0.0, BIG, ALU.is_lt, ALU.mult))
            link(pool.tensor_tensor(dist[:, :], dist[:, :], mask[:, :], ALU.add))
            link(pool.tensor_copy(cdist[:, :, :], cdi[:, :, :]))
            link(pool.tensor_scalar(valid[:, :], cdist[:, :, 0], 0.0, None, ALU.is_ge))
            cm = cden[:, 0:TT * NC].rearrange("p (t n) -> p t n", t=TT)
            link(pool.tensor_scalar(cm, cdist[:, :, :], 0.0, BIG, ALU.is_lt, ALU.mult))
            pool.tensor_tensor(cdist[:, :, :], cdist[:, :, :], cm, ALU.add).then_inc(tables, 1)
            pool.wait_ge(tables, 1)

            def improve(y, square, w):
                for _ in range(3):
                    link(pool.tensor_tensor(w, y, y, ALU.mult))
                    link(pool.tensor_tensor(w, w, square, ALU.mult))
                    link(pool.tensor_scalar(w, w, -0.5, 1.5, ALU.mult, ALU.add))
                    link(pool.tensor_tensor(y, y, w, ALU.mult))

            pool.wait_ge(guessed, 1)
            improve(r1[:, :], ssq[:, 0:2], root_w[:, 0:2])
            pool.tensor_scalar(r1q[:, :], r1[:, :], -NSA_SCALE, None, ALU.mult).then_inc(rs_ok, 1)
            pool.wait_ge(guessed, 2)
            improve(rc[:, :], ssq[:, 2:6], root_w[:, :])
            pool.tensor_copy(root_w[:, :], rc[:, :]).then_inc(rs_ok, 1)

            def rotate(src, dst, heads, t):
                x = src.rearrange("p (h c e) -> p h c e", h=heads, c=2)
                y = dst.rearrange("p (h c e) -> p h c e", h=heads, c=2)
                sin, cos = [cs[:, i, t * HALF:(t + 1) * HALF].unsqueeze(1).broadcast_to((P, heads, HALF)) for i in range(2)]
                u, v = [rtmp[:, i, 0:heads * HALF].rearrange("p (h e) -> p h e", h=heads) for i in range(2)]
                pool.tensor_tensor(u, x[:, :, 0, :], cos, ALU.mult)
                link(pool.tensor_tensor(v, x[:, :, 1, :], sin, ALU.mult))
                link(pool.tensor_tensor(y[:, :, 0, :], u, v, ALU.subtract))
                pool.tensor_tensor(u, x[:, :, 1, :], cos, ALU.mult)
                link(pool.tensor_tensor(v, x[:, :, 0, :], sin, ALU.mult))
                return pool.tensor_tensor(y[:, :, 1, :], u, v, ALU.add)

            pool.wait_ge(sin_ok, 1)
            pool.wait_ge(act_free, 2)
            for t in range(TT):
                link(rotate(c_sb[:, t, QR + KVR:CW], kpe[:, t, 0:ROPE], 1, t))
                pool.tensor_copy(kpe[:, t, ROPE:2 * ROPE], kpe[:, t, 0:ROPE]).then_inc(kpe_ok, 1)
            pool.wait_ge(act_free, 4)
            for i, off in enumerate((0, 128, 64, 192, 256, 384, 512, 640)):
                src = kv_sb[:, :, off:off + DK].unsqueeze(2).broadcast_to((P, TT, 2, DK))
                pool.tensor_copy(kd[:, i, :, :, :], src).then_inc(kd_ok, 1)
            for t in range(TT):
                pool.wait_ge(qpe_out, t + 1)
                link(rotate(qpe[:, t, :], qpr[:, t, :], MH, t))
                pool.tensor_copy(scl[:, 0, :], ones[:, 0:1].broadcast_to((P, 2))).then_inc(qpr_ok, 1)

            def sum_squares(u):
                part = u // MH
                s = sqacc[:, part, :]
                pool.wait_ge(y_sq, u + 1)
                if u % MH == 0:
                    pool.tensor_copy(s, sq[:, u % 2, :]).then_inc(sq_sum, 1)
                else:
                    pool.wait_ge(sq_sum, u)
                    pool.tensor_tensor(s, s, sq[:, u % 2, :], ALU.add).then_inc(sq_sum, 1)

            def root_of_sums(part, dst):
                pool.wait_ge(guessed, 3 + part)
                improve(dst, ssq[:, 6 + 2 * part:8 + 2 * part], root_w[:, 0:2])
                pool.tensor_copy(root_w[:, 0:2], dst).then_inc(yr_ok, 1)

            made = 0
            for i in range(len(STEPS) + LAG + 1):
                if i == NMLA:
                    pool.wait_ge(w_used, WO_M)
                if i < len(STEPS) and STEPS[i][0] == "slc":
                    while made < min(NH, STEPS[i][2] + 2):
                        if made >= 2:
                            pool.wait_ge(score_m, NMLA + 2 * made - 2)
                        pool.tensor_scalar(bias_h[:, made % 2, :], dist[:, :], SLOPE[made], None, ALU.mult).then_inc(bias_ok, 1)
                        made += 1
                if i == NMLA:
                    for h in range(NH):
                        m = pool.tensor_scalar(cbias[:, h // 2, :, h % 2, :], cdist[:, :, :], SLOPE[h], None, ALU.mult)
                    m.then_inc(cb_ok, 1)
                for u in range(16):
                    if LASTSTEP[u] + LAG + 1 == i:
                        sum_squares(u)
                if i == LASTSTEP[MH] + LAG + 2:
                    root_of_sums(0, rm[:, :])
            root_of_sums(1, rn[:, :])
            pool.wait_ge(y_lo, 16)
            pool.memset(acc[:, :, :], 0.0).then_inc(acc0, 1)

            pool.wait_ge(fw_in, 16)
            for t in range(TT):
                pool.wait_ge(fsq, t + 1)
                pool.tensor_tensor(h_sb[:, t, 0:1024], h_sb[:, t, 0:1024], fw[:, 0:1024], ALU.mult).then_inc(weighted, 1)

        def sums_ready(eng, t, group, last):
            if t == 0:
                eng.wait_ge(first_done, group + 1)
            else:
                eng.wait_ge(w_used, last + 1)

        @block.scalar
        def _(act):
            act.wait_ge(consts, 1)
            act.activation(sink[:, 0:1], ones[:, :], ACT.Copy).then_inc(warm, 1)
            act.wait_ge(warm, 1)

            def split_hi(c, half=None):
                act.wait_ge(raw_in[raw_slot(c)], 16 * loads(c))
                if half == 0 and c - SPLIT in FREED:
                    act.wait_ge(w_half, c - SPLIT - FREED[0] + 1)
                elif c >= SPLIT:
                    act.wait_ge(w_used, c - SPLIT + 1)
                w0, w1 = columns(c, half)
                act.activation(w_hi[:, split_slot(c), w0:w1], raw[:, raw_slot(c), w0:w1], ACT.Copy)\
                    .then_inc(half_hi if half == 0 else hi_done, 1)

            def split_hi_loop(j, g):
                act.wait_ge(raw_in[j % RAW], 16 * (LOADS0[j % RAW] + j // RAW + 1 - GC // RAW) + 16 * (GC // RAW) * g)
                act.wait_ge(w_used, LOOP0 + j - GC - SPLIT + 1 + GC * g)
                act.activation(w_hi[:, j % SPLIT, :], raw[:, j % RAW, :], ACT.Copy).then_inc(hi_done, 1)

            def x_hi(k):
                act.wait_ge(xt_t, k + 1)
                act.activation(xT[:, 0, k, :], bank(4 + k % 4, T), ACT.Copy, scale=wcols[:, k:k + 1]).then_inc(xt_hi, 1)

            def c_hi(k):
                act.wait_ge(ct_t, k + 1)
                act.activation(cT[:, 0, k, :], bank(k % 4, T), ACT.Copy,
                               scale=wcols[:, PRM["c"] + k:PRM["c"] + k + 1]).then_inc(ct_hi, 1)

            act.wait_ge(wcols_ok, 1)
            for c in range(8):
                if c:
                    split_hi(c)
                x_hi(2 * c)
                x_hi(2 * c + 1)
                if c == 0:
                    split_hi(0)
                if c in (3, 4):
                    t = c - 3
                    act.wait_ge(x_in[0], 16 * TT)
                    act.wait_ge(x_in[1], 16 * TT)
                    if t:
                        act.wait_ge(ssq_ok, t)
                    act.activation(sink[:, :], x_sb[:, t, :], ACT.Square, accum_out=ssq[:, t:t + 1]).then_inc(ssq_ok, 1)
            split_hi(8)
            act.wait_ge(ang_ok, 1)
            act.activation(cs[:, :, :], angs[:, :, :], ACT.Sin).then_inc(sin_ok, 1)
            split_hi(9)
            act.wait_ge(rs_ok, 1)
            for t in range(TT):
                sums_ready(act, t, 0, B_IN - 1)
                act.activation(c_sb[:, t, :], flat[:, 1024 * t:1024 * t + CW], ACT.Copy, scale=r1[:, t:t + 1]).then_inc(act_free, 1)
            n = 2
            for t in range(TT):
                act.wait_ge(act_free, t + 1)
                for i, (lo, hi) in enumerate(((0, QR), (QR, QR + KVR))):
                    act.wait_ge(ssq_ok, n)
                    n += 1
                    act.activation(sink[:, lo:hi], c_sb[:, t, lo:hi], ACT.Square,
                                   accum_out=ssq[:, 2 + 2 * i + t:3 + 2 * i + t]).then_inc(ssq_ok, 1)
            act.wait_ge(wcols_ok, 2)
            for c in range(10, 18):
                split_hi(c)
                if c == 14:
                    for k in range(4):
                        c_hi(k)
                if c == 15:
                    for k in range(4, 6):
                        c_hi(k)
            for t in range(TT):
                sums_ready(act, t, 1, UQ_PE - 1)
                act.activation(kv_sb[:, t, :], flat[:, 2048 + 1024 * t:2048 + 1024 * t + BW], ACT.Copy,
                               scale=r1[:, t:t + 1]).then_inc(act_free, 1)
            act.wait_ge(act_free, 4)
            act.activation(gates[:, :, :], kv_sb[:, :, 768:BW], ACT.Exp, scale=-1.0).then_inc(gexp, 1)
            split_hi(18)
            act.wait_ge(kpe_ok, 2)
            act.wait_ge(w_used, UQ_PE + 1)
            for t in range(TT):
                act.activation(qpe[:, t, :], bank(t), ACT.Copy, scale=-MLA_SCALE).then_inc(qpe_out, 1)
            split_hi(19)
            for i, b0 in ((0, 2), (1, 4)):
                act.wait_ge(w_used, UQ_NOPE + i + 1)
                for j in range(2):
                    act.activation(qnT[:, 4 * i + 2 * j:4 * i + 2 * j + 2, :], pairs(bank(b0 + j)), ACT.Copy,
                                   scale=-MLA_SCALE).then_inc(qn_out, 1)
                split_hi(20 + i)
            act.wait_ge(blk_f, 1)
            act.wait_ge(w_used, UKV_V + 1)
            act.activation(blk[:, 0, :, :, :].rearrange("p y k n -> p (y k n)"),
                           blkf[:, :, :, :].rearrange("p y k n -> p (y k n)"), ACT.Copy).then_inc(blk_hi, 1)

            def slot(i):
                j = i - LAG
                if 0 <= j < len(STEPS):
                    act.wait_ge(pt_t, j + 1)
                    if j >= 2:
                        act.wait_ge(o_t, j - 1)
                    r, w = (NC, 512) if STEPS[j][0] == "cmp" else (P, SEEN)
                    act.activation(probT[0:r, j % 2, 0:w], bank(6, w, 0, r), ACT.Copy).then_inc(pt_out, 1)
                j = i - LAG - 1
                if j >= 0 and LASTSTEP[STEPS[j][1]] == j:
                    u = STEPS[j][1]
                    act.wait_ge(o_t, j + 1)
                    if u == 0:
                        act.wait_ge(blk_ok, 1)
                    if u >= 2:
                        act.wait_ge(y_lo, u - 1)
                        act.wait_ge(sq_sum, u - 1)
                    act.activation(ysb[:, u % 2, :], bank(7, T), ACT.Copy).then_inc(y_out, 1)
                    act.wait_ge(y_out, u + 1)
                    act.activation(yT[:, u, 0, :], ysb[:, u % 2, :], ACT.Copy,
                                   scale=wcols[:, PRM["y"] + u:PRM["y"] + u + 1]).then_inc(y_hi, 1)
                    act.activation(sq[:, u % 2, :], ysb[:, u % 2, :], ACT.Square).then_inc(y_sq, 1)
                if i in SOFT:
                    n = SOFT[i]
                    act.wait_ge(score_m, n + 1)
                    p = prob[:, n % (LAG + 1), :]
                    act.activation(p[:, 0:P], p[:, 0:P], ACT.Exp, scale=-1.0, bias=nmax[:, n, 0:1], accum_out=den[:, n, 0:1])
                    act.activation(p[:, P:SEEN], p[:, P:SEEN], ACT.Exp, scale=-1.0, bias=nmax[:, n, 1:2],
                                   accum_out=den[:, n, 1:2]).then_inc(exp_ok, 1)

            for kind, i in PLAN:
                if kind == "hi":
                    split_hi(*i)
                elif kind == "s":
                    slot(i)
                elif i == "rotary":
                    for j in range(2):
                        act.wait_ge(qp_t, j + 1)
                        act.activation(qpT[:, 2 * j:2 * j + 2, :], pairs(bank(2 + j)), ACT.Copy).then_inc(qp_out, 1)
                elif i == "rotary_k":
                    act.wait_ge(qp_t, 3)
                    act.activation(kpT[:, :], bank(6, T), ACT.Copy).then_inc(qp_out, 1)
                elif i == "gelu":
                    act.wait_ge(w_used, CMP[3] + 1)
                    act.activation(h1a[:, :, :], ps[0:2 * NC, 4:6, 0:CMP_HID], ACT.Square).then_inc(g_sq, 1)
                    act.wait_ge(g_in, 1)
                    act.activation(h1c[:, :, :], h1b[:, :, :], ACT.Tanh, scale=float(np.sqrt(2 / np.pi))).then_inc(g_th, 1)
                elif i == "queries":
                    sums_ready(act, 0, 2, WO_M - 1)
                    act.activation(q_sb[:, 0, :], flat[:, 0:1024], ACT.Copy, scale=r1q[:, 0:1]).then_inc(q_in, 1)
                elif i == "turn_q":
                    for j in range(2):
                        act.wait_ge(q_t, j + 1)
                        act.activation(qT[:, 2 * j:2 * j + 2, :], pairs(bank(j)), ACT.Copy).then_inc(q_out, 1)
                elif i == "soft":
                    act.wait_ge(cs_sub, 1)
                    act.activation(pc[:, :, :, :, :].rearrange("p i t e n -> p (i t e n)"),
                                   pc[:, :, :, :, :].rearrange("p i t e n -> p (i t e n)"), ACT.Exp, scale=-1.0).then_inc(cs_exp, 1)

            def turned_hi(k):
                act.wait_ge(ht_t, k + 1)
                act.activation(xT[:, 0, k, :], bank(4 + k % 4, T), ACT.Copy,
                               scale=wcols[:, PRM["mlp"] + k:PRM["mlp"] + k + 1]).then_inc(ht_hi, 1)

            for c in range(WO_N + 4, MLP0):
                split_hi(c + 1)
                if WO_N + 5 <= c < MLP0 - 1:
                    for k in TURNS[c - WO_N - 5]:
                        turned_hi(k)
            def move_up(half, b, last, before):
                act.wait_ge(w_used, last + 1)
                if before is not None:
                    act.wait_ge(hd_lo, before)
                act.activation(hid[:, 4 * half:4 * half + 4, :], ps[:, b:b + 4, 0:T], ACT.Copy).then_inc(up_half, 1)

            def hidden_hi(pair, n, before):
                act.wait_ge(hid_ok, n)
                act.wait_ge(w_used, before)
                act.activation(hidT[:, 0, 2 * pair:2 * pair + 2, :], hid[:, 2 * pair:2 * pair + 2, :], ACT.Copy).then_inc(hd_hi, 1)

            for c in range(MLP0 + 1, LOOP0):
                split_hi(c)
                if c <= MLP0 + 2:
                    for k in range(4 * (c - MLP0) + 4, 4 * (c - MLP0) + 8):
                        turned_hi(k)
                if c in (MLP0 + 3, MLP0 + 4):
                    t = c - MLP0 - 3
                    act.wait_ge(ssq_ok, 6 + t)
                    act.activation(sink2[:, :], h_sb[:, t, :], ACT.Square, accum_out=ssq[:, 10 + t:11 + t]).then_inc(ssq_ok, 1)
                if c == MLP0 + 5:
                    act.wait_ge(acc0, 1)
                    move_up(0, 0, MLP0 + 3, None)
            split_hi_loop(0, 1)
            move_up(1, 4, LOOP0 - 1, None)
            with act.Fori(1, G) as g:
                for j in range(1, GC + 1):
                    split_hi_loop(j, g) if j < GC else split_hi_loop(0, g + 1)
                    if j <= 2:
                        for pair in (2 * j - 2, 2 * j - 1):
                            hidden_hi(pair, 2 * g - 2 + j, LOOP0 - GC + GC * g)
                    if j in (5, 13):
                        move_up(j // 8, 0, LOOP0 - GC + j - 2 + GC * g, 4 * g)
            for pair in range(4):
                hidden_hi(pair, 2 * G - 1 + pair // 2, LOOP0 - GC + GC * G)
            def square_sums(n):
                for t in range(TT):
                    act.wait_ge(added, TT * n + t + 1)
                    if n or t:
                        act.wait_ge(fsq, TT * n + t)
                    act.activation(sink2[:, 0:1024], h_sb[:, t, 1024 * n:1024 * n + 1024], ACT.Square,
                                   accum_out=ssq[:, 12 + TT * n + t:13 + TT * n + t]).then_inc(fsq, 1)

            for j in range(1, 8):
                split_hi_loop(j, G)
                if j == 6:
                    square_sums(0)
            square_sums(1)
            act.wait_ge(root_ok, 1)
            act.wait_ge(weighted, TT)
            for t in range(TT):
                act.activation(h_sb[:, t, 0:1024], h_sb[:, t, 0:1024], ACT.Copy, scale=rc[:, t:t + 1]).then_inc(normed0, 1)

        @block.vector
        def _(dve):
            chain = [0]

            def link(ins):
                chain[0] += 1
                ins.then_inc(dve_c, 1)
                dve.wait_ge(dve_c, chain[0])

            def low(dst, src, high, scale=None):
                if scale is None:
                    return dve.tensor_tensor(dst, src, high.bitcast(F32), ALU.subtract)
                return dve.scalar_tensor_tensor(out=dst, in0=src, scalar=scale, in1=high.bitcast(F32), op0=ALU.mult, op1=ALU.subtract)

            def split_lo(c, half=None):
                if half == 0:
                    dve.wait_ge(half_hi, HALVED.index(c) + 1)
                else:
                    dve.wait_ge(hi_done, c + 1)
                w0, w1 = columns(c, half)
                m = low(w_lo[:, split_slot(c), w0:w1], raw[:, raw_slot(c), w0:w1], w_hi[:, split_slot(c), w0:w1])
                if half != 0:
                    m.then_inc(lo_done, 1)

            def split_lo_loop(j, g):
                dve.wait_ge(hi_done, LOOP0 - GC + j + 1 + GC * g)
                low(w_lo[:, j % SPLIT, :], raw[:, j % RAW, :], w_hi[:, j % SPLIT, :]).then_inc(lo_done, 1)

            def guess(y, square):
                yi = y.bitcast(I32)
                link(dve.tensor_scalar(yi, square.bitcast(I32), 1, None, ALU.logical_shift_right))
                return dve.tensor_scalar(yi, yi, -1.0, float(0x5F3759DF), ALU.mult, ALU.add)

            def x_lo(k):
                dve.wait_ge(xt_hi, k + 1)
                low(xT[:, 1, k, :], bank(4 + k % 4, T), xT[:, 0, k, :], wcols[:, k:k + 1]).then_inc(xt_lo, 1)

            def c_lo(k):
                dve.wait_ge(ct_hi, k + 1)
                low(cT[:, 1, k, :], bank(k % 4, T), cT[:, 0, k, :], wcols[:, PRM["c"] + k:PRM["c"] + k + 1]).then_inc(ct_lo, 1)

            dve.wait_ge(prm_t, 1)
            dve.tensor_copy(wcols[:, 0:KT], bank(7, KT)).then_inc(wcols_ok, 1)
            dve.wait_ge(wcols_ok, 1)
            for c in range(8):
                if c:
                    split_lo(c)
                x_lo(2 * c)
                x_lo(2 * c + 1)
                if c == 0:
                    split_lo(0)
                if c == 5:
                    dve.wait_ge(ssq_ok, 2)
                    link(dve.tensor_scalar(ssq[:, 0:2], ssq[:, 0:2], 1.0 / D, EPS, ALU.mult, ALU.add))
                    guess(r1[:, :], ssq[:, 0:2]).then_inc(guessed, 1)
            dve.wait_ge(cst_in, 32)
            link(dve.tensor_copy(posf[:, :], posi[:, :]))
            for v in range(2):
                for t in range(TT):
                    m = dve.tensor_scalar(angs[:, v, t * HALF:(t + 1) * HALF], invf[:, :], posf[:, t:t + 1], None, ALU.mult)
            link(m)
            for v, quarter in ((0, 0.0), (1, 0.25)):
                m = dve.tensor_scalar(angk[:, v, :], angs[:, v, :], 1.0 / TWO_PI, quarter, ALU.mult, ALU.add)
            link(m)
            link(dve.tensor_scalar(angk[:, :, :], angk[:, :, :], MAGIC, None, ALU.add))
            link(dve.tensor_scalar(angk[:, :, :], angk[:, :, :], -MAGIC, None, ALU.add))
            for c in (C1, C2, C3):
                link(dve.scalar_tensor_tensor(out=angs[:, :, :], in0=angk[:, :, :], scalar=-c, in1=angs[:, :, :],
                                              op0=ALU.mult, op1=ALU.add))
            link(dve.tensor_scalar(angs[:, 1, :], angs[:, 1, :], float(np.pi / 2), None, ALU.add))
            dve.tensor_scalar(angs[:, :, :], angs[:, :, :], PI_IN, -PI_IN, ALU.min, ALU.max).then_inc(ang_ok, 1)

            split_lo(8)
            dve.wait_ge(prm_t, 2)
            dve.tensor_copy(wcols[:, KT:NPRM], bank(4, NPRM - KT)).then_inc(wcols_ok, 1)
            dve.wait_ge(wcols_ok, 2)
            split_lo(9)
            dve.wait_ge(ssq_ok, 6)
            link(dve.tensor_scalar(ssq[:, 2:4], ssq[:, 2:4], 1.0 / QR, EPS, ALU.mult, ALU.add))
            link(dve.tensor_scalar(ssq[:, 4:6], ssq[:, 4:6], 1.0 / KVR, EPS, ALU.mult, ALU.add))
            guess(rc[:, :], ssq[:, 2:6]).then_inc(guessed, 1)
            for c in range(10, 18):
                split_lo(c)
                if c == 11:
                    dve.wait_ge(rs_ok, 2)
                    for t in range(TT):
                        dve.tensor_scalar(c_sb[:, t, 0:QR], c_sb[:, t, 0:QR], rc[:, t:t + 1], None, ALU.mult)
                        m = dve.tensor_scalar(c_sb[:, t, QR:QR + KVR], c_sb[:, t, QR:QR + KVR], rc[:, 2 + t:3 + t], None, ALU.mult)
                    m.then_inc(c_norm, 1)
                if c == 14:
                    for k in range(4):
                        c_lo(k)
                if c == 15:
                    for k in range(4, 6):
                        c_lo(k)
            dve.wait_ge(gexp, 1)
            link(dve.tensor_scalar(gates[:, :, :], gates[:, :, :], 1.0, None, ALU.add))
            link(dve.reciprocal(gates[:, :, :], gates[:, :, :]))
            by_head = gates[:, :, :].rearrange("p t (h b) -> p b h t", b=3)
            by_pair = gates[:, :, :].rearrange("p t (i e b) -> p b e i t", e=2, b=3)
            dve.wait_ge(tables, 1)
            for e in range(2):
                m = dve.tensor_tensor(cgate[:, :, :, e], by_pair[:, 0, e, :, :],
                                      valid[:, :].unsqueeze(1).broadcast_to((P, NH // 2, TT)), ALU.mult)
            m.then_inc(gate_ok, 1)
            dve.wait_ge(gate_ok, 1)
            for c in range(18, 21):
                split_lo(c)
            for j in range(2):
                dve.wait_ge(kv_t, 1 + j)
                src = pairs(bank(6 + j))
                dve.tensor_copy(kcT[0:64, 2 * j:2 * j + 2, :], src[0:64, :, :])
                dve.tensor_copy(kcT[64:P, 2 * j:2 * j + 2, 0:T - 1], src[64:P, :, 1:T]).then_inc(kv_out, 1)
            dve.wait_ge(kv_out, 2)
            for y in range(2):
                for g in range(NG):
                    for half in range(2):
                        src = kcT[:, 2 * y + g, 16 * half:16 * half + 16 * NC].rearrange("p (n k two) -> p k n two", n=NC, two=2)[:, :, :, 0]
                        o = PRM["posk"] + 16 * y + 8 * half
                        m = dve.tensor_tensor(blkf[:, y, 8 * half:8 * half + 8, NC * g:NC * g + NC], src,
                                              wcols[:, o:o + 8].unsqueeze(2).broadcast_to((P, 8, NC)), ALU.add)
            m.then_inc(blk_f, 1)
            split_lo(21)
            dve.wait_ge(w_used, UKV_K + 1)
            for j in range(4):
                dve.tensor_copy(knT[:, 2 * j:2 * j + 2, :], pairs(bank(j))).then_inc(kn_out, 1)
            dve.wait_ge(w_used, UKV_V + 1)
            dve.tensor_copy(v_sb[:, 0, :], flat[:, 2048:3072]).then_inc(v_out, 1)
            dve.wait_ge(blk_hi, 1)
            low(blk[:, 1, :, :, :].rearrange("p y k n -> p (y k n)"), blkf[:, :, :, :].rearrange("p y k n -> p (y k n)"),
                blk[:, 0, :, :, :].rearrange("p y k n -> p (y k n)")).then_inc(blk_ok, 1)
            dve.tensor_copy(v_sb[:, 1, :], flat[:, 3072:4096]).then_inc(v_out, 1)

            STEP_OF = {n: i for i, n in SOFT.items()}

            def slot(i):
                if i in SOFT:
                    n = SOFT[i]
                    kind, u, h, branch = STEPS[i]
                    dve.wait_ge(score_t, n + 1)
                    if n > LAG:
                        dve.wait_ge(pt_t, STEP_OF[n - LAG - 1] + 1)
                    if kind == "mla":
                        bias = mask[:, :]
                    else:
                        dve.wait_ge(bias_ok, h + 1)
                        bias = bias_h[:, h % 2, :]
                    for q, (x, y) in enumerate(((0, P), (P, SEEN))):
                        m = dve.tensor_tensor_reduce(prob[:, n % (LAG + 1), x:y], ps[:, 4 + n % 2, x:y], bias[:, x:y], 1.0, 3e38,
                                                     ALU.add, ALU.min, nmax[:, n, q:q + 1])
                    m.then_inc(score_m, 1)
                if i == LASTSTEP[MH] + LAG + 2:
                    mean_square(0, rm[:, :])
                if i - 1 in SOFT:
                    n = SOFT[i - 1]
                    kind, u, h, branch = STEPS[i - 1]
                    dve.wait_ge(exp_ok, n + 1)
                    link(dve.reciprocal(scl[:, n, :], den[:, n, :]))
                    if kind != "mla":
                        b = 1 if kind == "slc" else 2
                        link(dve.tensor_tensor(scl[:, n, :], scl[:, n, :], by_head[:, b, h, :], ALU.mult))
                    p = prob[:, n % (LAG + 1), :]
                    dve.tensor_scalar(p[:, 0:P], p[:, 0:P], scl[:, n, 0:1], None, ALU.mult)
                    dve.tensor_scalar(p[:, P:SEEN], p[:, P:SEEN], scl[:, n, 1:2], None, ALU.mult).then_inc(prob_ok, 1)
                j = i - LAG - 1
                if j >= 0 and LASTSTEP[STEPS[j][1]] == j:
                    u = STEPS[j][1]
                    dve.wait_ge(y_hi, u + 1)
                    low(yT[:, u, 1, :], ysb[:, u % 2, :], yT[:, u, 0, :], wcols[:, PRM["y"] + u:PRM["y"] + u + 1]).then_inc(y_lo, 1)

            def mean_square(part, dst):
                dve.wait_ge(ysum_t, part + 1)
                square = ssq[:, 6 + 2 * part:8 + 2 * part]
                dve.tensor_scalar(square, ps[:, 7, 256:258], 1.0 / (MH * MV), EPS, ALU.mult, ALU.add).then_inc(ysum_ok, 1)
                dve.wait_ge(ysum_ok, part + 1)
                guess(dst, square).then_inc(guessed, 1)

            def add_attention(part, n, group, last):
                dve.wait_ge(yr_ok, part + 1)
                dve.wait_ge(h_in, 32)
                r = (rm, rn)[part]
                for t in range(TT):
                    sums_ready(dve, t, group, last)
                    if part:
                        dve.wait_ge(dve_free, 2 * n + t + 1)
                    o = h_sb[:, t, 1024 * n:1024 * n + 1024]
                    dve.scalar_tensor_tensor(out=o, in0=flat[:, 1024 * t:1024 * t + 1024], scalar=r[:, t:t + 1], in1=o,
                                             op0=ALU.mult, op1=ALU.add).then_inc(dve_free, 1)

            added_half = 0
            rows = pc[:, :, :, :, :].rearrange("p i t e n -> p (i t e) n")
            for kind, i in PLAN:
                if kind == "lo":
                    split_lo(*i)
                elif kind == "s":
                    slot(i)
                elif i == "keys":
                    for j in range(2):
                        dve.wait_ge(kv_t, j + 3)
                        dve.tensor_copy(kT[:, 2 * j:2 * j + 2, :], pairs(bank(j))).then_inc(kv_out, 1)
                elif i == "gelu":
                    u = ps[0:2 * NC, 4:6, 0:CMP_HID]
                    dve.wait_ge(g_sq, 1)
                    link(dve.tensor_scalar(h1b[:, :, :], h1a[:, :, :], 0.044715, 1.0, ALU.mult, ALU.add))
                    dve.tensor_tensor(h1b[:, :, :], u, h1b[:, :, :], ALU.mult).then_inc(g_in, 1)
                    dve.wait_ge(g_th, 1)
                    dve.scalar_tensor_tensor(out=h1a[:, :, :], in0=h1c[:, :, :], scalar=1.0, in1=u, op0=ALU.add,
                                             op1=ALU.mult).then_inc(g_ok, 1)
                elif i == "turn":
                    dve.wait_ge(g_t, 1)
                    dve.tensor_scalar(h1T[:, :, :].rearrange("p k n -> p (k n)"), bank(6, 4 * 2 * NC), 0.5, None, ALU.mult).then_inc(g_turned, 1)
                elif i == "project":
                    dve.wait_ge(k_t, 1)
                    for e in range(2):
                        dve.tensor_copy(kcmp[64 * e:64 * e + 64, :, e, :],
                                        ps[64 * e:64 * e + 64, 7, 0:2 * NC].rearrange("p (g n) -> p g n", g=NG))
                    dve.tensor_copy(vcmp[:, :, :], ps[0:NC, 7, 64:64 + NG * DK].rearrange("p (g d) -> p g d", g=NG)).then_inc(k_ok, 1)
                elif i == "queries":
                    sums_ready(dve, 1, 2, WO_M - 1)
                    dve.wait_ge(rs_ok, 2)
                    dve.tensor_scalar(q_sb[:, 1, :], flat[:, 1024:2048], r1q[:, 1:2], None, ALU.mult).then_inc(q_in, 1)
                elif i == "turn_q":
                    for j in range(2, 4):
                        dve.wait_ge(q_t, j + 1)
                        dve.tensor_copy(qT[:, 2 * j:2 * j + 2, :], pairs(bank(j))).then_inc(q_out2, 1)
                elif i == "soft":
                    every = pc[:, :, :, :, :].rearrange("p i t e n -> p (i t e n)")
                    dve.wait_ge(cs_t, 1)
                    dve.wait_ge(cb_ok, 1)
                    dve.tensor_tensor(every, bank(3, NH * TT * NC), cbias[:, :, :, :, :].rearrange("p i t e n -> p (i t e n)"), ALU.add)\
                        .then_inc(cs_in, 1)
                    dve.wait_ge(cs_in, 1)
                    link(dve.tensor_reduce(cmx[:, :], rows, AX.X, ALU.min))
                    dve.tensor_tensor(rows, rows, cmx[:, :].unsqueeze(2).broadcast_to((P, NH * TT, NC)), ALU.subtract).then_inc(cs_sub, 1)
                elif i == "weigh":
                    dve.wait_ge(cs_exp, 1)
                    link(dve.tensor_reduce(cden[:, :], rows, AX.X, ALU.add))
                    link(dve.reciprocal(cden[:, :], cden[:, :]))
                    link(dve.tensor_tensor(cden[:, :], cden[:, :], cgate[:, :, :, :].rearrange("p i t e -> p (i t e)"), ALU.mult))
                    dve.tensor_tensor(rows, rows, cden[:, :].unsqueeze(2).broadcast_to((P, NH * TT, NC)), ALU.mult).then_inc(pc_ok, 1)
                elif i == "add":
                    add_attention(0, added_half, 3 + added_half, WO_M + 3 + 4 * added_half)
                    added_half += 1
                elif i == "norm_n":
                    mean_square(1, rn[:, :])

            def turned_lo(k):
                dve.wait_ge(ht_hi, k + 1)
                low(xT[:, 1, k, :], bank(4 + k % 4, T), xT[:, 0, k, :], wcols[:, PRM["mlp"] + k:PRM["mlp"] + k + 1]).then_inc(ht_lo, 1)

            for c in range(WO_N + 4, MLP0):
                if c == WO_N + 4:
                    add_attention(1, 0, 5, WO_N + 3)
                split_lo(c + 1)
                if WO_N + 5 <= c < MLP0 - 1:
                    for k in TURNS[c - WO_N - 5]:
                        turned_lo(k)
            add_attention(1, 1, 6, MLP0 - 1)
            def hidden_lo(pair, done):
                dve.wait_ge(hd_hi, done + 1)
                low(hidT[:, 1, 2 * pair:2 * pair + 2, :], hid[:, 2 * pair:2 * pair + 2, :], hidT[:, 0, 2 * pair:2 * pair + 2, :])\
                    .then_inc(hd_lo, 1)

            def add_down(n, group, last, before):
                for t in range(TT):
                    sums_ready(dve, t, group, last)
                    dve.wait_ge(dve_free, before + 2 * n + t + 1)
                    o = acc[:, t, 1024 * n:1024 * n + 1024]
                    c0 = 2048 + 1024 * t
                    dve.tensor_tensor(o, flat[:, c0:c0 + 1024], o, ALU.add).then_inc(dve_free, 1)

            def add_up(half, b, n, late=False):
                dve.wait_ge(up_half, n)
                o = hid[:, 4 * half:4 * half + 4, :]
                m = dve.tensor_tensor(o, ps[:, b:b + 4, T:2 * T], o, ALU.add)
                if b:
                    m.then_inc(up_high, 1)
                    dve.wait_ge(up_high, 1)
                else:
                    m.then_inc(up_ok, 1)
                    dve.wait_ge(up_ok, n - (1 if late else 0))
                dve.scalar_tensor_tensor(out=o, in0=o, scalar=0.0, in1=o, op0=ALU.max, op1=ALU.mult).then_inc(hid_ok, 1)

            for c in range(MLP0 + 1, LOOP0):
                split_lo(c)
                if c <= MLP0 + 2:
                    for k in range(4 * (c - MLP0) + 4, 4 * (c - MLP0) + 8):
                        turned_lo(k)
                if c == MLP0 + 5:
                    add_up(0, 0, 1)
            split_lo_loop(0, 1)
            dve.wait_ge(ssq_ok, 8)
            link(dve.tensor_scalar(r1q[:, :], ssq[:, 10:12], 1.0 / D, EPS, ALU.mult, ALU.add))
            link(dve.reciprocal(r1[:, :], r1q[:, :]))
            add_up(1, 4, 2)

            with dve.Fori(1, G) as g:
                for j in range(1, GC + 1):
                    split_lo_loop(j, g) if j < GC else split_lo_loop(0, g + 1)
                    if j <= 2:
                        for pair in (2 * j - 2, 2 * j - 1):
                            hidden_lo(pair, 4 * g - 4 + pair)
                    if j in (5, 13):
                        add_up(j // 8, 0, 2 * g + 1 + j // 8, late=True)
                    if j == 9:
                        add_down(0, 5 + 2 * g, LOOP0 - GC + 7 + GC * g, 4 * g)
                add_down(1, 6 + 2 * g, LOOP0 - GC + 15 + GC * g, 4 * g)
            for pair in range(4):
                hidden_lo(pair, 4 * G - 4 + pair)
            END = LOOP0 + GC * (G - 1)

            def last_down(n, group, last):
                for t in range(TT):
                    sums_ready(dve, t, group, last)
                    o = h_sb[:, t, 1024 * n:1024 * n + 1024]
                    c0 = 2048 * n + 1024 * t
                    dve.scalar_tensor_tensor(out=o, in0=flat[:, c0:c0 + 1024], scalar=r1[:, t:t + 1], in1=o,
                                             op0=ALU.mult, op1=ALU.add).then_inc(added, 1)

            split_lo_loop(1, G)
            dve.wait_ge(dve_free, 4 * G + 4)
            for t in range(TT):
                dve.scalar_tensor_tensor(out=h_sb[:, t, :], in0=acc[:, t, :], scalar=r1[:, t:t + 1], in1=h_sb[:, t, :],
                                         op0=ALU.mult, op1=ALU.add).then_inc(merged, 1)
                split_lo_loop(2 + t, G)
            for j in range(4, 6):
                split_lo_loop(j, G)
            dve.wait_ge(merged, TT)
            last_down(0, 7 + 2 * (G - 1), END + 3)
            for j in range(6, 8):
                split_lo_loop(j, G)
            last_down(1, 8 + 2 * (G - 1), END + 7)
            dve.wait_ge(fsq, 2 * TT)
            square, y, w, minus = ssq[:, 12:14], rc[:, 0:2], rc[:, 2:4], root_w[:, 0:2]
            link(dve.tensor_tensor(square, square, ssq[:, 14:16], ALU.add))
            link(dve.tensor_scalar(square, square, 1.0 / D, EPS, ALU.mult, ALU.add))
            dve.tensor_scalar(minus, square, -0.5, None, ALU.mult)
            link(guess(y, square))
            for step in range(3):
                link(dve.tensor_tensor(w, y, y, ALU.mult))
                link(dve.tensor_tensor(w, w, minus, ALU.mult))
                m = dve.scalar_tensor_tensor(out=y, in0=w, scalar=1.5, in1=y, op0=ALU.add, op1=ALU.mult)
                if step < 2:
                    link(m)
            m.then_inc(root_ok, 1)
            dve.wait_ge(root_ok, 1)
            dve.wait_ge(fw_in, 16)
            for t in range(TT):
                o = h_sb[:, t, 1024:D]
                dve.scalar_tensor_tensor(out=o, in0=o, scalar=y[:, t:t + 1], in1=fw[:, 1024:D],
                                         op0=ALU.mult, op1=ALU.mult).then_inc(normed1, 1)

        @block.tensor
        def _(pe):
            def products(slot, shape, stationary, base, start, stop, free=None, only=None, freed=False):
                blocks, width = shape
                cols = [(n, min(width, n + 512)) for n in range(0, width, 512)]
                for b in range(blocks):
                    for t in range(TT):
                        if only not in (None, TT * b + t):
                            continue
                        if start and b == 0 and free is not None:
                            free(t)
                        first, last = start and b == 0, stop and b == blocks - 1
                        for n0, n1 in cols:
                            o = flat[:, base[t] + n0:base[t] + n1]
                            w = slice(b * width + n0, b * width + n1)
                            pe.matmul(o, stationary(0, b, t), w_hi[:, slot, w], start=first, stop=False)
                            pe.matmul(o, stationary(0, b, t), w_lo[:, slot, w], start=False, stop=False)
                        for n0, n1 in cols:
                            o = flat[:, base[t] + n0:base[t] + n1]
                            m = pe.matmul(o, stationary(1, b, t), w_hi[:, slot, b * width + n0:b * width + n1], start=False, stop=last)
                        if last and t == 0:
                            m.then_inc(first_done, 1)
                        if freed and (b, t) == (blocks // 2 - 1, TT - 1):
                            m.then_inc(w_half, 1)
                if only in (None, blocks * TT - 1):
                    m.then_inc(w_used, 1)

            LOW, HIGH = (0, 1024), (2048, 3072)

            def stream(c, tiles, k0, base, start, stop, free=None, only=None):
                pe.wait_ge(lo_done, c + 1)
                products(split_slot(c), chunk(c)[1], lambda part, b, t: tiles(part, k0 + b, t), base, start, stop, free, only, c in FREED)

            def of_x(part, k, t):
                return xT[:, part, k, P * t:P * t + P]

            def of_c(part, k, t):
                return cT[:, part, k, P * t:P * t + P]

            def of_y(part, k, t):
                return yT[:, k, part, P * t:P * t + P]

            def turn_x(k):
                if k == 3:
                    pe.wait_ge(wcols_ok, 1)
                if k >= 4:
                    pe.wait_ge(xt_lo, k - 3)
                if k == KT // 2:
                    pe.wait_ge(x_in[1], 16 * TT)
                for t in range(TT):
                    m = pe.transpose(ps[:, 4 + k % 4, P * t:P * t + P], x_sb[:, t, P * k:P * k + P], ident[:, :])
                m.then_inc(xt_t, 1)

            def turn_c(k):
                if k >= 4:
                    pe.wait_ge(ct_lo, k - 3)
                for t in range(TT):
                    m = pe.transpose(ps[:, k % 4, P * t:P * t + P], c_sb[:, t, P * k:P * k + P], ident[:, :])
                m.then_inc(ct_t, 1)

            pe.wait_ge(consts, 1)
            pe.wait_ge(x_in[0], 16 * TT)
            for k in range(3):
                turn_x(k)
            pe.wait_ge(prm0_in, 16)
            pe.transpose(bank(7, KT), prm0[:, :], ident[0:KT, 0:KT]).then_inc(prm_t, 1)
            turn_x(3)
            for c in range(8):
                pe.wait_ge(xt_lo, 2 * c + 2)
                stream(c, of_x, 2 * c, LOW, c == 0, c == 7)
                for k in (2 * c + 4, 2 * c + 5):
                    if k < KT:
                        turn_x(k)
                if c == 6:
                    pe.wait_ge(xt_lo, KT)
                    pe.wait_ge(prm_in, 16 * len(TABLE))
                    pe.transpose(bank(4, NPRM - KT), prm[:, :], ident[0:NPRM - KT, 0:NPRM - KT]).then_inc(prm_t, 1)
            pe.wait_ge(wcols_ok, 2)
            for c in range(8):
                stream(B_IN + c, of_x, 2 * c, HIGH, c == 0, c == 7)
                if c == 4:
                    pe.wait_ge(c_norm, 1)
                    for k in range(4):
                        turn_c(k)
                if c == 5:
                    for k in range(4, 6):
                        turn_c(k)

            def heads(c, banks, nheads, k0, nk):
                pe.wait_ge(lo_done, c + 1)
                width = chunk(c)[1][1]
                s = split_slot(c)
                for h in range(nheads):
                    o = ps[:, banks[h // 2], T * (h % 2):T * (h % 2) + T]
                    for b in range(nk):
                        w = slice(b * width + P * h, b * width + P * h + P)
                        pe.matmul(o, w_hi[:, s, w], cT[:, 0, k0 + b, :], start=b == 0, stop=False)
                        pe.matmul(o, w_hi[:, s, w], cT[:, 1, k0 + b, :], start=False, stop=False)
                        m = pe.matmul(o, w_lo[:, s, w], cT[:, 0, k0 + b, :], start=False, stop=b == nk - 1)
                m.then_inc(w_used, 1)

            pe.wait_ge(ct_lo, 6)
            pe.wait_ge(lo_done, UQ_PE + 1)
            for b in range(4):
                for t in range(TT):
                    o = bank(t)
                    w = slice(512 * b, 512 * b + 512)
                    s = split_slot(UQ_PE)
                    pe.matmul(o, of_c(0, b, t), w_hi[:, s, w], start=b == 0, stop=False)
                    pe.matmul(o, of_c(0, b, t), w_lo[:, s, w], start=False, stop=False)
                    m = pe.matmul(o, of_c(1, b, t), w_hi[:, s, w], start=False, stop=b == 3)
            m.then_inc(w_used, 1)
            heads(UQ_NOPE, (2, 3), 4, 0, 4)
            pe.wait_ge(act_free, 4)
            heads(UQ_NOPE + 1, (4, 5), 4, 0, 4)

            def turn_kd(j, b):
                pe.wait_ge(kd_ok, 2 * j + 2)
                for n in range(2):
                    for t in range(TT):
                        o = T * n + P * t
                        m = pe.transpose(ps[:, b, o:o + P], kd[:, 2 * j + n, t, :, :].rearrange("p c d -> p (c d)"), ident[:, :])
                m.then_inc(kv_t, 1)

            turn_kd(0, 6)
            turn_kd(1, 7)
            pe.wait_ge(qpe_out, 2)
            pe.wait_ge(qn_out, 2)
            heads(UKV_K, (0, 1, 2, 3), 8, 4, 2)
            pe.wait_ge(qn_out, 4)
            pe.wait_ge(kv_out, 2)
            pe.wait_ge(lo_done, UKV_V + 1)
            s = split_slot(UKV_V)
            for b in range(2):
                for t, col in ((0, 2048), (1, 3072)):
                    for n in range(2):
                        o = flat[:, col + 512 * n:col + 512 * n + 512]
                        w = slice(1024 * b + 512 * n, 1024 * b + 512 * n + 512)
                        pe.matmul(o, of_c(0, 4 + b, t), w_hi[:, s, w], start=b == 0, stop=False)
                        pe.matmul(o, of_c(0, 4 + b, t), w_lo[:, s, w], start=False, stop=False)
                        m = pe.matmul(o, of_c(1, 4 + b, t), w_hi[:, s, w], start=False, stop=b == 1)
            m.then_inc(w_used, 1)

            def sum_over_features(part):
                pe.wait_ge(sq_sum, MH * (part + 1))
                pe.wait_ge(y_out, MH * (part + 1))
                for t in range(TT):
                    m = pe.matmul(ps[:, 7, 256 + t:257 + t], sqacc[:, part, P * t:P * t + P], ones[:, :], start=True, stop=True)
                m.then_inc(ysum_t, 1)

            SPANS = ((0, 0, P), (P, P, SEEN))

            def score(i):
                if i in SOFT:
                    n = SOFT[i]
                    kind, u, h, branch = STEPS[i]
                    if n >= 2:
                        pe.wait_ge(score_m, n - 1)
                    if i == NMLA:
                        pe.wait_ge(q_out, 1)
                    p0 = 64 * (h % 2)
                    for q, c0, c1 in SPANS:
                        o = ps[:, 4 + n % 2, c0:c1]
                        if kind == "mla":
                            pe.matmul(o, qnT[:, h, q:q + P], knT[:, h, 0:c1 - c0], start=True, stop=False)
                            m = pe.matmul(o, qpT[p0:p0 + 64, h // 2, q:q + P], kpT[p0:p0 + 64, 0:c1 - c0], start=False, stop=True)
                        else:
                            m = pe.matmul(o, qT[p0:p0 + 64, h // 2, q:q + P], kT[p0:p0 + 64, 2 * branch + h // 8, 0:c1 - c0],
                                          start=True, stop=True)
                    m.then_inc(score_t, 1)
            def slot(i):
                if i != NMLA:
                    score(i)
                j = i - LAG
                if 0 <= j < len(STEPS):
                    if j >= 1:
                        pe.wait_ge(pt_out, j)
                    kind, u, h, branch = STEPS[j]
                    if kind == "cmp":
                        pe.wait_ge(pc_ok, 1)
                        for e in range(2):
                            for t in range(TT):
                                o = T * e + P * t
                                m = pe.transpose(ps[0:NC, 6, o:o + P], pc[:, h // 2, t, e, :], ident[:, :])
                    else:
                        n = SOFT[j]
                        pe.wait_ge(prob_ok, n + 1)
                        for c in range(3):
                            m = pe.transpose(ps[:, 6, P * c:P * c + P], prob[:, n % (LAG + 1), P * c:P * c + P], ident[:, :])
                    m.then_inc(pt_t, 1)
                j = i - LAG - 1
                if 0 <= j < len(STEPS):
                    kind, u, h, branch = STEPS[j]
                    pe.wait_ge(pt_out, j + 1)
                    if u and (kind == "mla" or (branch == 0 and h % 2 == 0)):
                        pe.wait_ge(y_out, u)
                        if u == MH + 1:
                            sum_over_features(0)
                            pe.wait_ge(ysum_ok, 1)
                    elif u == 0:
                        pe.wait_ge(k_ok, 1)
                    p = probT[:, j % 2, :]
                    if kind == "cmp":
                        for e in range(2):
                            m = pe.matmul(ps[64 * e:64 * e + 64, 7, 0:T], vcmp[:, h // 8, :], p[0:NC, T * e:T * e + T], start=False, stop=True)
                    else:
                        if kind == "mla":
                            o, first, last = ps[:, 7, 0:T], True, True
                            v = [v_sb[:, t, MV * h:MV * h + MV] for t in range(TT)]
                        else:
                            e = h % 2
                            o, first, last = ps[64 * e:64 * e + 64, 7, 0:T], branch == 0, False
                            off = 256 * (1 + branch) + 128 * (h // 8) + DK
                            v = [kv_sb[:, t, off:off + DK] for t in range(TT)]
                        pe.matmul(o, v[0], p[:, 0:T], start=first, stop=False)
                        m = pe.matmul(o[:, P:T], v[1], p[:, T:SEEN], start=False, stop=last)
                    m.then_inc(o_t, 1)
                if i == NMLA:
                    score(i)

            for kind, i in PLAN:
                if kind in "wq" and (i in A_IN if kind == "w" else i[0] in A_IN):
                    c, quarter = (i, None) if kind == "w" else i
                    j = A_IN.index(c)
                    if j == 0:
                        pe.wait_ge(kv_out, 4)
                        pe.wait_ge(qp_out, 2)
                    stream(c, of_x, 2 * j, LOW, j == 0, j == 7, None, quarter)
                elif kind == "w":
                    if i == CMP[0]:
                        pe.wait_ge(blk_ok, 1)
                        pe.wait_ge(v_out, 1)
                    pe.wait_ge(lo_done, i + 1)
                    y, half, s = CMP.index(i) // 2, CMP.index(i) % 2, split_slot(i)
                    o = ps[0:2 * NC, 4 + y, 0:CMP_HID]
                    for b in range(8):
                        k = 8 * half + b
                        w = slice(CMP_HID * b, CMP_HID * b + CMP_HID)
                        pe.matmul(o, blk[:, 0, y, k, :], w_hi[:, s, w], start=k == 0, stop=False)
                        pe.matmul(o, blk[:, 0, y, k, :], w_lo[:, s, w], start=False, stop=False)
                        m = pe.matmul(o, blk[:, 1, y, k, :], w_hi[:, s, w], start=False, stop=k == 15)
                        if b == 3:
                            m.then_inc(w_half, 1)
                    m.then_inc(w_used, 1)
                elif kind == "q":
                    c, quarter = i
                    n, j, part = (c - WO_M) // 4, (c - WO_M) % 4, (c - WO_M) // 8

                    def free(t, n=n):
                        if n:
                            pe.wait_ge(dve_free, 2 * n - 1 + t)
                        elif t:
                            pe.wait_ge(cs_in, 1)
                    if n % 2 == 0 and quarter == 0:
                        pe.wait_ge(y_lo, 8 * part + 2 * j + 2)
                    stream(c, of_y, 8 * part + 2 * j, LOW, j == 0, j == 3, free, quarter)
                elif kind == "s":
                    slot(i)
                elif i == "keys":
                    for j in range(2):
                        pe.wait_ge(kn_out, j + 1)
                        turn_kd(2 + j, j)
                elif i == "rotary":
                    pe.wait_ge(kn_out, 4)
                    pe.wait_ge(qpr_ok, 2)
                    for c in range(4):
                        for t in range(TT):
                            o = T * (c % 2) + P * t
                            m = pe.transpose(ps[:, 2 + c // 2, o:o + P], qpr[:, t, P * c:P * c + P], ident[:, :])
                        if c % 2:
                            m.then_inc(qp_t, 1)
                elif i == "rotary_k":
                    pe.wait_ge(v_out, 2)
                    pe.wait_ge(kpe_ok, 2)
                    for t in range(TT):
                        m = pe.transpose(ps[:, 6, P * t:P * t + P], kpe[:, t, :], ident[:, :])
                    m.then_inc(qp_t, 1)
                elif i == "turn":
                    pe.wait_ge(g_ok, 1)
                    pe.wait_ge(qp_out, 3)
                    for y in range(2):
                        for k in range(2):
                            o = 2 * NC * (2 * y + k)
                            m = pe.transpose(ps[:, 6, o:o + 2 * NC], h1a[:, y, P * k:P * k + P], ident[0:2 * NC, 0:2 * NC])
                    m.then_inc(g_t, 1)
                elif i == "project":
                    pe.wait_ge(g_turned, 1)
                    pe.wait_ge(w2_in, 48)
                    for k in range(2):
                        pe.matmul(ps[:, 7, 0:2 * NC], w2k[:, k, :, :].rearrange("p c d -> p (c d)"), h1T[:, k, :],
                                  start=k == 0, stop=k == 1)
                    for g in range(NG):
                        for k in range(2):
                            m = pe.matmul(ps[0:NC, 7, 64 + DK * g:64 + DK * g + DK], h1T[:, 2 + k, NC * g:NC * g + NC], w2v[:, k, :],
                                          start=k == 0, stop=k == 1)
                    m.then_inc(k_t, 1)
                elif i == "turn_q":
                    pe.wait_ge(q_in, 2)
                    for j in range(4):
                        for c in (2 * j, 2 * j + 1):
                            for t in range(TT):
                                o = T * (c % 2) + P * t
                                m = pe.transpose(ps[:, j, o:o + P], q_sb[:, t, P * c:P * c + P], ident[:, :])
                        m.then_inc(q_t, 1)
                elif i == "scores":
                    pe.wait_ge(q_out, 2)
                    pe.wait_ge(q_out2, 2)
                    for c in range(NH // 2):
                        for t in range(TT):
                            o = 2 * NC * (TT * c + t)
                            m = pe.matmul(ps[:, 3, o:o + 2 * NC], qT[:, c, P * t:P * t + P],
                                          kcmp[:, c // 4, :, :].rearrange("p e n -> p (e n)"), start=True, stop=True)
                    m.then_inc(cs_t, 1)
                elif i == "norm_n":
                    sum_over_features(1)

            def turn_h(k):
                if k >= 4:
                    pe.wait_ge(ht_lo, k - 3)
                for t in range(TT):
                    m = pe.transpose(ps[:, 4 + k % 4, P * t:P * t + P], h_sb[:, t, P * k:P * k + P], ident[:, :])
                m.then_inc(ht_t, 1)

            for c in range(WO_N + 4, MLP0):
                n, j = (c - WO_N) // 4, (c - WO_N) % 4
                stream(c, of_y, 8 + 2 * j, LOW, j == 0, j == 3, lambda t: pe.wait_ge(dve_free, 2 + 2 * n + t + 1))
                if WO_N + 5 <= c < MLP0 - 1:
                    if c == WO_N + 5:
                        pe.wait_ge(dve_free, 6)
                        pe.wait_ge(ysum_ok, 2)
                    for k in TURNS[c - WO_N - 5]:
                        turn_h(k)
            def stream_loop(j, g, tiles, k0, base, start, stop, free=None):
                pe.wait_ge(lo_done, LOOP0 - GC + j + 1 + GC * g)
                products(j % SPLIT, (2, 1024), lambda part, b, t: tiles(part, k0 + b, t), base, start, stop, free)

            def of_hidden(part, k, t):
                return hidT[:, part, k, P * t:P * t + P]

            def up_products(slot, k0, b0, start, stop, free=None):
                for f in range(4):
                    if free is not None:
                        free(f)
                    for b in range(4):
                        w = slice(512 * b + P * f, 512 * b + P * f + P)
                        pe.matmul(ps[:, b0 + f, :].rearrange("p (c t) -> p c t", c=2), w_hi[:, slot, w], xT[:, :, k0 + b, :],
                                  start=start and b == 0, stop=False)
                        m = pe.matmul(ps[:, b0 + f, 0:T], w_lo[:, slot, w], xT[:, 0, k0 + b, :], start=False, stop=stop and b == 3)
                m.then_inc(w_used, 1)

            for j in range(8):
                if j < 4:
                    pe.wait_ge(ht_lo, 4 * j + 4)
                pe.wait_ge(lo_done, MLP0 + j + 1)
                up_products(split_slot(MLP0 + j), 4 * (j % 4), 4 * (j // 4), j % 4 == 0, j % 4 == 3,
                            lambda f: pe.wait_ge(dve_free, 7 + f // 2))
                if j < 2:
                    for k in range(4 * j + 8, 4 * j + 12):
                        turn_h(k)

            with pe.Fori(1, G) as g:
                for j in range(GC):
                    if j == 0:
                        pe.wait_ge(up_ok, 2 * g - 1)
                    if j == 8:
                        pe.wait_ge(up_ok, 2 * g)
                    if j // 4 % 2 == 0:
                        pe.wait_ge(lo_done, LOOP0 - GC + j + 1 + GC * g)
                        up_products(j % SPLIT, 4 * (j % 4), 0, j % 4 == 0, j % 4 == 3)
                    else:
                        if j == 4:
                            pe.wait_ge(up_high, 1)
                        if j < 8:
                            pe.wait_ge(hd_lo, 4 * g - 7 + j)
                        before = 4 * g + (3 if j < 8 else 5)
                        stream_loop(j, g, of_hidden, 2 * (j % 4), HIGH, j % 4 == 0, j % 4 == 3, lambda t: pe.wait_ge(dve_free, before + t))
            for j in range(4):
                if j == 0:
                    pe.wait_ge(up_ok, 2 * G - 1)
                pe.wait_ge(hd_lo, 4 * G - 3 + j)
                stream_loop(j, G, of_hidden, 2 * j, LOW, j == 0, j == 3)
            for j in range(4, 8):
                stream_loop(j, G, of_hidden, 2 * (j - 4), HIGH, j == 4, j == 7, lambda t: pe.wait_ge(dve_free, 3 + t + 4 * G))


_INS = ["x", "positions", "attn_norm_w", "w_in", "mla_q_norm_w", "mla_w_uq", "mla_kv_norm_w", "mla_w_ukv",
        "cmp_pos_k", "cmp_pos_v", "cmp_w1_k", "cmp_w2_k", "cmp_w1_v", "cmp_w2_v", "mla_out_norm_w",
        "nsa_out_norm_w", "w_o", "mlp_norm_w", "w_up", "w_down", "final_norm_w"]


def kernel(**inputs):
    import concourse.bacc as bacc
    from concourse.bass_utils import run_bass_kernel_spmd

    nc = bacc.Bacc("TRN2", target_bir_lowering=False, num_devices=1)
    freq = (1.0 / (np.float32(10000.0) ** (np.arange(0, ROPE, 2, dtype=np.float32) / np.float32(ROPE)))).astype(np.float32)
    arrays, args = {}, {}
    for name in _INS + ["inv_freq"]:
        v = freq if name == "inv_freq" else np.ascontiguousarray(inputs[name])
        arrays[f"in_{name}"] = v
        args[name] = nc.dram_tensor(f"in_{name}", v.shape, mybir.dt.from_np(v.dtype), kind="ExternalInput").ap()
    out = nc.dram_tensor("out", (1, T, D), F32, kind="ExternalOutput").ap()
    build(nc, args, out)
    result = run_bass_kernel_spmd(nc, [arrays], core_ids=[0])
    return result.results[0]["out"]
```
